# Optimizing a Trainium2 kernel written in Bass

```python
import math
import jax
import jax.numpy as jnp
from jax import lax
import numpy as np

D_MODEL = 1024
BATCH = 1
SEQ = 256
DEPTH = 2

GRID_W = 64
CTX_LEN = 256
N_MIXERS = 2
N_MAMBA = (DEPTH + 1) // 2
N_HYENA = DEPTH // 2
DEEPNORM_ALPHA = (2 * DEPTH) ** 0.25
DEEPNORM_BETA = (8 * DEPTH) ** -0.25
LN_EPS = 1e-5
RMS_EPS = 1e-5

SSM_INNER = 2 * D_MODEL
SSM_HEAD_DIM = 64
SSM_HEADS = SSM_INNER // SSM_HEAD_DIM
SSM_GROUPS = 4
SSM_STATE = 128
SSM_CHUNK = 128
SSM_CONV = 3
SSM_CONV_DIM = SSM_INNER + 2 * SSM_GROUPS * SSM_STATE
SSM_IN_DIM = SSM_INNER + SSM_CONV_DIM + 2 * SSM_HEADS

HYENA_ORDER = 2
HYENA_SHORT = 3
HYENA_EMB = 33
HYENA_FF = 64
HYENA_INNER_MLPS = 2
HYENA_STEEP_DECAY = 0.3
HYENA_GENTLE_DECAY = 1.5
HYENA_TARGET = 1e-2
HYENA_NORM_EPS = 1e-6

PEER_HEADS = 8
PEER_NKEYS = 128
PEER_EXPERTS = PEER_NKEYS * PEER_NKEYS
PEER_DK = 256
PEER_TOPK = 16
PEER_BLOCK = 128

kernel_name = 'hybrid_ssd_hyena_peer_dit'

def layer_norm(x, g, b):
    xf = x.astype(jnp.float32)
    mu = jnp.mean(xf, axis=-1, keepdims=True)
    var = jnp.mean(jnp.square(xf - mu), axis=-1, keepdims=True)
    return ((xf - mu) * lax.rsqrt(var + LN_EPS) * g.astype(jnp.float32) + b.astype(jnp.float32)).astype(x.dtype)

def gated_group_rmsnorm(y, z, w):
    b, L, _ = y.shape
    u = (y * jax.nn.silu(z)).astype(jnp.float32).reshape(b, L, SSM_GROUPS, -1)
    u = u * lax.rsqrt(jnp.mean(jnp.square(u), axis=-1, keepdims=True) + RMS_EPS)
    return (u.reshape(b, L, SSM_INNER) * w.astype(jnp.float32)).astype(y.dtype)

def depthwise_conv_grid(u, w, bias, rows, cols):
    b, L, C = u.shape
    out = lax.conv_general_dilated(u.reshape(b, rows, cols, C), w.astype(u.dtype)[:, :, None, :],
                                   window_strides=(1, 1), padding='SAME',
                                   dimension_numbers=('NHWC', 'HWIO', 'NHWC'), feature_group_count=C)
    return out.reshape(b, L, C) + bias

def ssd_scan(xs, dt, a_neg, bm, cm, init, want_y):
    f32 = jnp.float32
    b, L, H, P = xs.shape
    G, N = bm.shape[2], bm.shape[3]
    R = H // G
    Q = SSM_CHUNK
    nc = L // Q
    xdt = (xs.astype(f32) * dt[..., None]).reshape(b, nc, Q, G, R, P)
    bc = bm.astype(f32).reshape(b, nc, Q, G, N)
    cc = cm.astype(f32).reshape(b, nc, Q, G, N)
    a = (dt * a_neg.astype(f32)).reshape(b, nc, Q, G, R)
    a_cum = jnp.cumsum(a, axis=2)
    decay_to_end = jnp.exp(a_cum[:, :, -1:] - a_cum)
    chunk_states = jnp.einsum('bclgn,bclgrp->bcgrpn', bc, xdt * decay_to_end[..., None])
    chunk_decay = jnp.exp(a_cum[:, :, -1])

    def step(state, inp):
        cs, cd = inp
        return state * cd[..., None, None] + cs, state

    final, prev = lax.scan(step, init.astype(f32).reshape(b, G, R, P, N),
                           (jnp.moveaxis(chunk_states, 1, 0), jnp.moveaxis(chunk_decay, 1, 0)))
    final = final.reshape(b, H, P, N)
    if not want_y:
        return None, final
    prev = jnp.moveaxis(prev, 0, 1)
    seg = a_cum[:, :, :, None] - a_cum[:, :, None, :]
    lower = jnp.tril(jnp.ones((Q, Q), dtype=bool))[None, None, :, :, None, None]
    decay_ls = jnp.exp(jnp.where(lower, seg, -jnp.inf))
    cb = jnp.einsum('bclgn,bcsgn->bclsg', cc, bc)
    y_diag = jnp.einsum('bclsgr,bcsgrp->bclgrp', cb[..., None] * decay_ls, xdt)
    y_off = jnp.einsum('bclgn,bcgrpn->bclgrp', cc, prev) * jnp.exp(a_cum)[..., None]
    y = (y_diag + y_off).reshape(b, L, H, P)
    return y.astype(xs.dtype), final

def mamba2_mixer(h_lat, h_ctx, rows, w_in, conv_w, conv_b, a_log, dt_bias, d_skip, norm_w, w_out, ctx_out):
    f32 = jnp.float32
    a_neg = -jnp.exp(a_log.astype(f32))
    G, N = SSM_GROUPS, SSM_STATE

    def branch(h, rows_, cols_, need_z):
        bb, LL, _ = h.shape
        proj = h @ (w_in if need_z else w_in[:, SSM_INNER:])
        z = None
        if need_z:
            z, proj = proj[..., :SSM_INNER], proj[..., SSM_INNER:]
        xbc = jax.nn.silu(depthwise_conv_grid(proj[..., :SSM_CONV_DIM], conv_w, conv_b, rows_, cols_))
        dt = jax.nn.softplus(proj[..., SSM_CONV_DIM:].astype(f32).reshape(bb, LL, 2, SSM_HEADS)
                             + dt_bias.astype(f32))
        xs = xbc[..., :SSM_INNER].reshape(bb, LL, SSM_HEADS, SSM_HEAD_DIM)
        bm = xbc[..., SSM_INNER:SSM_INNER + G * N].reshape(bb, LL, G, N)
        cm = xbc[..., SSM_INNER + G * N:].reshape(bb, LL, G, N)
        return z, xs, bm, cm, dt

    def scans(xs, bm, cm, dt, init_f, init_b, want_y):
        y_f, s_f = ssd_scan(xs, dt[:, :, 0], a_neg[0], bm, cm, init_f, want_y)
        y_b, s_b = ssd_scan(jnp.flip(xs, 1), jnp.flip(dt[:, :, 1], 1), a_neg[1],
                            jnp.flip(bm, 1), jnp.flip(cm, 1), init_b, want_y)
        y = None
        if want_y:
            y = y_f + jnp.flip(y_b, 1) + xs * d_skip[:, None]
        return y, s_f, s_b

    def finish(y, z):
        bb, LL = y.shape[:2]
        return gated_group_rmsnorm(y.reshape(bb, LL, SSM_INNER), z, norm_w) @ w_out

    bsz = h_ctx.shape[0]
    zeros = jnp.zeros((bsz, SSM_HEADS, SSM_HEAD_DIM, SSM_STATE), f32)
    zc, xc, bmc, cmc, dtc = branch(h_ctx, 1, h_ctx.shape[1], ctx_out)
    yc, s_f, s_b = scans(xc, bmc, cmc, dtc, zeros, zeros, ctx_out)
    zl, xl, bml, cml, dtl = branch(h_lat, rows, GRID_W, True)
    yl, _, _ = scans(xl, bml, cml, dtl, s_f, s_b, True)
    out_ctx = finish(yc, zc) if ctx_out else None
    return finish(yl, zl), out_ctx

def hyena_filters(L, w1, b1, w2, b2, w3, freq):
    f32 = jnp.float32
    t = jnp.linspace(0.0, 1.0, L, dtype=f32)[:, None]
    bands = (HYENA_EMB - 1) // 2
    ang = 2.0 * math.pi * jnp.arange(L, dtype=f32)[:, None] / L
    fb = jnp.linspace(1e-4, bands - 1, bands, dtype=f32)[None, :]
    z = jnp.concatenate([t, jnp.cos(fb * ang), -jnp.sin(fb * ang)], axis=-1)
    fr = freq.astype(f32)
    hid = jnp.sin(fr * (z @ w1.astype(f32) + b1.astype(f32)))
    for j in range(HYENA_INNER_MLPS):
        hid = jnp.sin(fr * (hid @ w2[j].astype(f32) + b2[j].astype(f32)))
    h = (hid @ w3.astype(f32)).reshape(L, HYENA_ORDER, 2, D_MODEL)
    max_decay = math.log(HYENA_TARGET) / HYENA_STEEP_DECAY
    min_decay = math.log(HYENA_TARGET) / HYENA_GENTLE_DECAY
    deltas = jnp.linspace(min_decay, max_decay, D_MODEL, dtype=f32)
    h = h * jnp.exp(-t * jnp.abs(deltas))[:, None, None, :]
    h_fwd, h_bwd = h[:, :, 0], h[:, :, 1]
    two_sided = jnp.concatenate([h_fwd[:1] + h_bwd[:1], h_fwd[1:],
                                 jnp.zeros((1, HYENA_ORDER, D_MODEL), f32),
                                 jnp.flip(h_bwd[1:], 0)], axis=0)
    two_sided = two_sided * lax.rsqrt(jnp.sum(jnp.square(two_sided), axis=0, keepdims=True) + HYENA_NORM_EPS)
    return jnp.fft.rfft(two_sided, n=2 * L, axis=0)

def fft_long_conv(u, hf, bias):
    L = u.shape[1]
    uf = u.astype(jnp.float32)
    y = jnp.fft.irfft(jnp.fft.rfft(uf, n=2 * L, axis=1) * hf[None], n=2 * L, axis=1)[:, :L]
    return (y + uf * bias.astype(jnp.float32)).astype(u.dtype)

def short_conv_centred(u, w, bias):
    up = jnp.pad(u, ((0, 0), (1, 1), (0, 0)))
    return up[:, :-2] * w[0] + up[:, 1:-1] * w[1] + up[:, 2:] * w[2] + bias

def hyena_mixer(h, w_in, conv_w, conv_b, w1, b1, w2, b2, w3, freq, fbias, w_out):
    L = h.shape[1]
    hf = hyena_filters(L, w1, b1, w2, b2, w3, freq)
    u = short_conv_centred(h @ w_in, conv_w, conv_b)
    x1, x2, v = jnp.split(u, 3, axis=-1)
    zz = x1 * fft_long_conv(v, hf[:, 0], fbias[0])
    zz = x2 * fft_long_conv(zz, hf[:, 1], fbias[1])
    return zz @ w_out

def peer_ffn(h, wq, k1, k2, u_tab, v_tab):
    f32 = jnp.float32
    shp = h.shape
    t = h.reshape(-1, D_MODEL)
    T = t.shape[0]
    half = PEER_DK // 2
    q = (t @ wq).astype(f32).reshape(T, PEER_HEADS, PEER_DK)
    s1 = jnp.einsum('thd,hkd->thk', q[..., :half], k1.astype(f32))
    s2 = jnp.einsum('thd,hkd->thk', q[..., half:], k2.astype(f32))
    v1, i1 = lax.top_k(s1, PEER_TOPK)
    v2, i2 = lax.top_k(s2, PEER_TOPK)
    cand_s = (v1[..., :, None] + v2[..., None, :]).reshape(T, PEER_HEADS, PEER_TOPK * PEER_TOPK)
    cand_i = (i1[..., :, None] * PEER_NKEYS + i2[..., None, :]).reshape(T, PEER_HEADS, PEER_TOPK * PEER_TOPK)
    top_s, pos = lax.top_k(cand_s, PEER_TOPK)
    idx = jnp.take_along_axis(cand_i, pos, axis=-1)
    gate = jax.nn.softmax(top_s, axis=-1)
    nb = T // PEER_BLOCK

    def block(args):
        tb, ib, gb = args
        act = jax.nn.gelu(jnp.einsum('td,thkd->thk', tb, u_tab[ib]).astype(f32), approximate=False)
        return jnp.einsum('thk,thkd->td', (gb * act).astype(tb.dtype), v_tab[ib])

    out = lax.map(block, (t.reshape(nb, PEER_BLOCK, D_MODEL),
                          idx.reshape(nb, PEER_BLOCK, PEER_HEADS, PEER_TOPK),
                          gate.reshape(nb, PEER_BLOCK, PEER_HEADS, PEER_TOPK)))
    return out.reshape(shp)

def setup_inputs(seed: int = 0) -> dict:
    key = jax.random.key(seed)
    ks = iter(jax.random.split(key, 48))
    f32 = jnp.float32
    D = D_MODEL

    def nrm(shape, scale):
        return jax.random.normal(next(ks), shape, f32) * scale

    dt0 = jnp.exp(jax.random.uniform(next(ks), (N_MAMBA, 2, SSM_HEADS), f32, math.log(1e-3), math.log(1e-1)))
    a0 = jax.random.uniform(next(ks), (N_MAMBA, 2, SSM_HEADS), f32, 1.0, 16.0)
    return {
        'x': nrm((BATCH, SEQ, D), 1.0),
        'c': nrm((BATCH, D), 1.0),
        'ctx': nrm((BATCH, CTX_LEN, D), 1.0),
        'c_ctx': nrm((D,), 1.0),
        'ada_w': nrm((DEPTH, D, 6 * D), 0.5 * D ** -0.5),
        'ada_b': nrm((DEPTH, 6 * D), 0.02),
        'ln_g': 1.0 + nrm((DEPTH, 2, D), 0.02),
        'ln_b': nrm((DEPTH, 2, D), 0.02),
        'm_w_in': nrm((N_MAMBA, D, SSM_IN_DIM), D ** -0.5),
        'm_conv_w': nrm((N_MAMBA, SSM_CONV, SSM_CONV, SSM_CONV_DIM), 1.0 / SSM_CONV),
        'm_conv_b': nrm((N_MAMBA, SSM_CONV_DIM), 0.02),
        'm_a_log': jnp.log(a0),
        'm_dt_bias': dt0 + jnp.log(-jnp.expm1(-dt0)),
        'm_d': 1.0 + nrm((N_MAMBA, SSM_HEADS), 0.02),
        'm_norm_w': 1.0 + nrm((N_MAMBA, SSM_INNER), 0.02),
        'm_w_out': nrm((N_MAMBA, SSM_INNER, D), DEEPNORM_BETA * SSM_INNER ** -0.5),
        'h_w_in': nrm((N_HYENA, D, 3 * D), D ** -0.5),
        'h_conv_w': nrm((N_HYENA, HYENA_SHORT, 3 * D), HYENA_SHORT ** -0.5),
        'h_conv_b': nrm((N_HYENA, 3 * D), 0.02),
        'h_f_w1': nrm((N_HYENA, HYENA_EMB, HYENA_FF), HYENA_EMB ** -0.5),
        'h_f_b1': nrm((N_HYENA, HYENA_FF), 0.1),
        'h_f_w2': nrm((N_HYENA, HYENA_INNER_MLPS, HYENA_FF, HYENA_FF), HYENA_FF ** -0.5),
        'h_f_b2': nrm((N_HYENA, HYENA_INNER_MLPS, HYENA_FF), 0.1),
        'h_f_w3': nrm((N_HYENA, HYENA_FF, HYENA_ORDER * 2 * D), HYENA_FF ** -0.5),
        'h_freq': 1.0 + nrm((N_HYENA, HYENA_FF), 0.05),
        'h_bias': nrm((N_HYENA, HYENA_ORDER, D), 0.2),
        'h_w_out': nrm((N_HYENA, D, D), DEEPNORM_BETA * D ** -0.5),
        'p_wq': nrm((DEPTH, D, PEER_HEADS * PEER_DK), D ** -0.5),
        'p_k1': nrm((DEPTH, PEER_HEADS, PEER_NKEYS, PEER_DK // 2), (PEER_DK // 2) ** -0.5),
        'p_k2': nrm((DEPTH, PEER_HEADS, PEER_NKEYS, PEER_DK // 2), (PEER_DK // 2) ** -0.5),
        'p_u': nrm((DEPTH, PEER_EXPERTS, D), D ** -0.5),
        'p_v': nrm((DEPTH, PEER_EXPERTS, D), DEEPNORM_BETA),
    }

def reference(x, c, ctx, c_ctx, ada_w, ada_b, ln_g, ln_b,
              m_w_in, m_conv_w, m_conv_b, m_a_log, m_dt_bias, m_d, m_norm_w, m_w_out,
              h_w_in, h_conv_w, h_conv_b, h_f_w1, h_f_b1, h_f_w2, h_f_b2, h_f_w3, h_freq, h_bias, h_w_out,
              p_wq, p_k1, p_k2, p_u, p_v):
    rows = x.shape[1] // GRID_W
    s_lat = jax.nn.silu(c)
    s_ctx = jax.nn.silu(c_ctx)
    for i in range(DEPTH):
        kind, k = i % N_MIXERS, i // N_MIXERS
        ctx_live = any(j % N_MIXERS == 0 for j in range(i + 1, DEPTH))
        ctx_read = (kind == 0) or ctx_live
        sh1, sc1, g1, sh2, sc2, g2 = jnp.split((s_lat @ ada_w[i] + ada_b[i])[:, None, :], 6, axis=-1)
        hx = x * (1 + sc1) + sh1
        if ctx_read:
            csh1, csc1, cg1, csh2, csc2, cg2 = jnp.split(s_ctx @ ada_w[i] + ada_b[i], 6, axis=-1)
            hc = ctx * (1 + csc1) + csh1
        if kind == 0:
            y_lat, y_ctx = mamba2_mixer(hx, hc, rows, m_w_in[k], m_conv_w[k], m_conv_b[k], m_a_log[k],
                                        m_dt_bias[k], m_d[k], m_norm_w[k], m_w_out[k], ctx_live)
        else:
            hyena_w = (h_w_in[k], h_conv_w[k], h_conv_b[k], h_f_w1[k], h_f_b1[k], h_f_w2[k], h_f_b2[k],
                       h_f_w3[k], h_freq[k], h_bias[k], h_w_out[k])
            y_lat = hyena_mixer(hx, *hyena_w)
            y_ctx = hyena_mixer(hc, *hyena_w) if ctx_live else None
        peer_w = (p_wq[i], p_k1[i], p_k2[i], p_u[i], p_v[i])
        x = layer_norm(DEEPNORM_ALPHA * x + g1 * y_lat, ln_g[i, 0], ln_b[i, 0])
        x = layer_norm(DEEPNORM_ALPHA * x + g2 * peer_ffn(x * (1 + sc2) + sh2, *peer_w), ln_g[i, 1], ln_b[i, 1])
        if ctx_live:
            ctx = layer_norm(DEEPNORM_ALPHA * ctx + cg1 * y_ctx, ln_g[i, 0], ln_b[i, 0])
            ctx = layer_norm(DEEPNORM_ALPHA * ctx + cg2 * peer_ffn(ctx * (1 + csc2) + csh2, *peer_w),
                             ln_g[i, 1], ln_b[i, 1])
    return x


_drawn_inputs = setup_inputs


def setup_inputs(seed=0):
    import zlib

    import numpy as np

    out = dict(_drawn_inputs(seed))
    spreads = {}
    factors = {'ctx': 8.0,
     'c_ctx': 8.0,
     'm_conv_b': 8.0,
     'm_d': 64.0,
     'm_norm_w': 28.193,
     'h_conv_b': 3.456}
    for name, (base, spread) in spreads.items():
        noise = np.random.default_rng([zlib.crc32(name.encode()), seed]).standard_normal(out[name].shape)
        drawn = base * np.exp(spread * noise) if base else spread * noise
        out[name] = jnp.asarray(drawn.astype(out[name].dtype))
    for name, factor in factors.items():
        out[name] = (out[name] * factor).astype(out[name].dtype)
    return out
```

```python
import math
from contextlib import ExitStack

import concourse.bass as bass
from concourse import mybir

F32 = mybir.dt.float32
F32R = mybir.dt.float32r
U32 = mybir.dt.uint32
ACT = mybir.ActivationFunctionType
ALU = mybir.AluOpType
AX = mybir.AxisListType

P = 128
D = 1024
KD = D // P
T = 256
TT = T // P
GRID_W = 64
ROWS = T // GRID_W
DEPTH = 2
ALPHA = (2 * DEPTH) ** 0.25
EPS = 1e-5
INNER = 2 * D
HEADS = 32
HD = 64
GROUPS = 4
HPG = HEADS // GROUPS
GW = HPG * HD
XBC_CT = (INNER + 2 * GROUPS * P) // P
ORDER = 2
HY_EPS = 1e-6
HY_FF = 64
HY_EMB = 33
PH = 8
NK = 128
TOPK = 16
NROW = 2 * PH
BLK = 256
RING = 4
UV = 4
TC = 32
NTC = T // TC
OH = 8
GI = 4
ROUND = 8
NROUND = (NK - ROUND) // ROUND
LOWEST = -3.0e38

V_CW, V_CB, V_NW = 0, 216, 240
V_HCW, V_HCB, V_HB, V_C, V_CC = 256, 328, 352, 368, 376
V_ADA = 384
C_ID, C_LE, C_GE, C_LT, C_GT, C_ONE, C_IOTA = range(7)
H_FR, H_FI, H_BZ, H_C0, H_INV, H_WS, H_WD, H_W1 = 0, 512, 1024, 1280, 1536, 2560, 2688, 2816
H_COLS = 2944
(DC_F0, DC_F1, DC_F2, DC_B1, DC_B0, DC_B3, DC_IF2, DC_IF3, DC_IB2, DC_IB3, DC_TF2, DC_TB3) = range(12)


class BankPlan:

    def __init__(self):
        self.count = [0] * 8
        self.where = {}

    def use(self, key, bank, loop=None):
        assert key not in self.where, key
        self.where[key] = (bank, self.count[bank], 0)
        self.count[bank] += 1

    def loop(self, rounds, uses):
        per = [sum(b == bank for _, b in uses) for bank in range(8)]
        seen = [0] * 8
        for key, bank in uses:
            assert key not in self.where, key
            self.where[key] = (bank, self.count[bank] + seen[bank], per[bank])
            seen[bank] += 1
        for bank in range(8):
            self.count[bank] += rounds * per[bank]

    def __call__(self, key, i=0):
        bank, base, per = self.where[key]
        return bank, base + i * per if per else base


class Chain:

    def __init__(self, sem):
        self.sem, self.n, self.i, self.per = sem, 0, None, 0

    def __call__(self, instruction):
        instruction.then_inc(self.sem, 1)
        self.n += 1
        return self.value()

    def value(self):
        return self.n if self.i is None else self.n + self.i * self.per

    def enter(self, i, per):
        self.i, self.per, self.start = i, per, self.n

    def leave(self, rounds):
        assert self.n - self.start == self.per, (self.n - self.start, self.per)
        self.n = self.start + rounds * self.per
        self.i = None


def build_program(nc, A, out):
    ctx = ExitStack()
    with ctx:
        build_in(nc, A, out, ctx)


def build_in(nc, A, out, ctx):
    sems = {}

    def sem(name):
        if name not in sems:
            sems[name] = ctx.enter_context(nc.semaphore(name))
        return sems[name]

    def sb(scope, name, shape, dt=F32):
        return scope.enter_context(nc.sbuf_tensor(name, shape, dt))

    cst = sb(ctx, "constants", [P, 7, P])
    vec = sb(ctx, "channel_vectors", [P, 512])
    xres = sb(ctx, "x_residual", [P, TT, D])
    wring = [sb(ctx, f"weight_block{s}", [P, 2048]) for s in range(RING)]
    lnb = sb(ctx, "ln_gain_bias", [P, 2, D])
    gate = [sb(ctx, f"gate{j}", [P, D]) for j in range(2)]
    s_rep = sb(ctx, "silu_c_repeated", [P, KD, P])
    s_col = sb(ctx, "silu_c_columns", [P, KD, 2])
    ada = sb(ctx, "modulation_columns", [P, 4, KD, 2])
    lnt = sb(ctx, "layer_norm_tmp", [P, 2, 512])
    small = sb(ctx, "layer_norm_small", [P, TT, 24])
    ps = [ctx.enter_context(nc.psum_tensor(f"bank{b}", [P, 512], F32)) for b in range(8)]

    ident = cst[:, C_ID, :]

    with ExitStack() as s:
        hT = sb(s, "mixer_input_T", [P, KD, 2 * T])
        bcT = sb(s, "BC_T", [P, 8, T])
        work = sb(s, "conv_work_or_state2", [P, 4096])
        xtok = sb(s, "x_tokens", [P, 4, INNER])
        btok = sb(s, "B_tokens", [P, 4, GROUPS * P])
        wdt = sb(s, "w_dt", [P, KD, 2 * HEADS])
        dtb = sb(s, "dt_bias_row", [1, 2 * HEADS])
        aneg = sb(s, "a_log_rows", [P, 2 * HEADS])
        dskip = sb(s, "d_skip_rows", [P, HEADS])
        dt_t = sb(s, "dt", [P, 4, 2 * HEADS])
        a_t = sb(s, "a", [P, 4, 2 * HEADS])
        dec = sb(s, "decays", [P, 12, HEADS])
        wst = sb(s, "state_weights", [P, 6, HEADS])
        aM = [sb(s, f"a_masked{j}", [P, HPG, P]) for j in range(2)]
        EM = [sb(s, f"decay_times_cb{j}", [P, HPG, P]) for j in range(2)]
        cbm = sb(s, "cb_masked", [P, 2, P])
        xw = [sb(s, f"x_weighted{j}", [P, INNER]) for j in range(2)]
        S1 = sb(s, "state_ctx", [P, 2, INNER])
        ss = sb(s, "rms", [P, 24])
    ctxb = xw[0][:, :].rearrange("p (t d) -> p t d", t=TT)
    dtw = S1[:, 0, 0:1536].rearrange("p (n c) -> p n c", n=6)
    zs = [aM[j][:, 0:4, :].rearrange("p a b -> p (a b)") for j in range(2)]
    ubuf = [work[:, j * 1536:j * 1536 + 512] for j in range(2)]
    cacc = [work[:, j * 1536 + 512:j * 1536 + 1024] for j in range(2)]
    xc = [work[:, j * 1536 + 1024:j * 1536 + 1536] for j in range(2)]
    stg = hT[:, 0, :].rearrange("p (a b) -> p a b", a=4)
    S2 = work[:, :].rearrange("p (a b) -> p a b", a=2)
    yv = xtok[:, 0:2, :]
    uT = hT[:, :, :].rearrange("p a b -> p (a b)").rearrange("p (a b) -> p a b", a=16)

    with ExitStack() as s:
        uvring = [sb(s, f"expert_rows{j}", [P, 2, D]) for j in range(UV)]
        tThi = sb(s, "t_T_hi", [P, KD, T], F32R)
        tTlo = sb(s, "t_T_lo", [P, KD, T], F32R)
        selT = sb(s, "selected_T", [P, 3, T])
        seltok = sb(s, "selected_tokens", [P, 3, P])
        with ExitStack() as q:
            tT = sb(q, "t_T", [P, KD, T])
            qT = sb(q, "q_T", [P, NROW, T])
            kraw = sb(q, "keys", [P, NROW, P])
            kT = sb(q, "keys_T", [P, NROW, P])
            sc = sb(q, "scores", [P, NROW, NK])
            sc2 = sb(q, "scores_left", [P, NROW, NK])
            topv = sb(q, "top_values", [P, NROW, TOPK])
            topi = sb(q, "top_indices", [P, NROW, TOPK], U32)
            topf = sb(q, "top_indices_f", [P, NROW, TOPK])
            cand = sb(q, "candidates", [P, PH, 256])
            selv = sb(q, "selected_scores", [P, PH, TOPK])
            seli = sb(q, "selected_positions", [P, PH, TOPK], U32)
            posr = sb(q, "position_parts", [P, 2, PH, TOPK], U32)
            posf = sb(q, "position_parts_f", [P, 2, PH * TOPK])
            ksum = sb(q, "gate_sums", [P, 2, PH])
        cand2 = sc2[:, :, :].rearrange("p a b -> p (a b)").rearrange("p (a b) -> p a b", a=PH)
        pick = sc[:, :, :].rearrange("p a b -> p (a b)")
        with ExitStack() as q:
            onea = [sb(q, f"one_hot_first{j}", [P, OH, NK]) for j in range(2)]
            oneb = [sb(q, f"one_hot_second{j}", [P, OH, NK]) for j in range(2)]
            gch = sb(q, "g_chunk", [P, 2, NK, TC])
        with ExitStack() as q:
            UThi = [sb(q, f"u_T_hi{j}", [P, KD, P], F32R) for j in range(2)]
            UTlo = [sb(q, f"u_T_lo{j}", [P, KD, P], F32R) for j in range(2)]
            Vhi = [sb(q, f"v_hi{j}", [P, D], F32R) for j in range(2)]
            Vlo = [sb(q, f"v_lo{j}", [P, D], F32R) for j in range(2)]
            Whi = [sb(q, f"w_hi{j}", [P, T], F32R) for j in range(2)]
            Wlo = [sb(q, f"w_lo{j}", [P, T], F32R) for j in range(2)]
            gel = [sb(q, f"gelu{j}", [P, T]) for j in range(2)]
            gw = [sb(q, f"gelu_gated{j}", [P, T]) for j in range(2)]
            gt = [sb(q, f"g_tile{j}", [P, NTC, GI * TC]) for j in range(2)]

    with ExitStack() as s:
        hc = sb(s, "hyena_constants", [P, H_COLS])
        Hs = sb(s, "filter_spectra", [P, ORDER, 5, D])
        hv = sb(s, "filter_mlp_vectors", [HY_FF, 8])
        hw1 = sb(s, "filter_w1", [HY_EMB, HY_FF])
        hw2 = sb(s, "filter_w2", [HY_FF, 2, HY_FF])
        zf = sb(s, "filter_features", [HY_EMB, T])
        tcol = sb(s, "lag_times", [P, TT])
        with ExitStack() as q:
            hid = sb(q, "filter_hidden", [HY_FF, 4, T])
            w3 = sb(q, "filter_w3", [HY_FF, 4 * D])
            delta = sb(q, "decay_rates", [P, D])
            dcy = sb(q, "lag_decay", [P, TT, D])
            sd = sb(q, "filter_sum_difference", [P, 2, TT, ORDER, D])
            hfb = sb(q, "filter_two_sides", [P, 2, 512])
            rsn = sb(q, "filter_norm", [P, 512])
        with ExitStack() as q:
            hhT = sb(q, "hyena_input_T", [P, KD, T])
            huT = sb(q, "hyena_u_T", [P, 24, T])
            hub = [sb(q, f"hyena_conv_in{j}", [P, 2, T]) for j in range(2)]
            vtok = sb(q, "hyena_v_tokens", [P, TT, D])
            Yf = sb(q, "spectrum_product", [P, 4, D])
            ytm = sb(q, "spectrum_tmp", [P, 4, 512])
            hyt = sb(q, "hyena_long_conv_out", [P, 2, T])

    gdram = nc.dram_tensor("g_scratch", [P, NTC, NK * TC], F32).ap()

    plan = BankPlan()
    stream_base = {}
    full = [sem(f"bank{b}_full") for b in range(8)]
    read = [sem(f"bank{b}_read") for b in range(8)]

    plan.use("vecs", 0)

    def plan_ada(l):
        for n in range(2):
            plan.use(("ada_cols", l, n), 1)
            plan.use(("ada_gate", l, n, 0), 2)
            plan.use(("ada_gate", l, n, 1), 3)

    def plan_peer(l):
        for k in range(4):
            plan.use(("tT", l, k), k)
        for r in range(NROW // 2):
            plan.use(("q", l, r), 4 + r % 4)
        for j in range(4):
            plan.use(("kT", l, j), j)
        for tt in range(TT):
            for j in range(4):
                plan.use(("sc", l, tt, j), 4 + j)
            plan.use(("selT", l, tt), tt)
        plan.loop(NTC // 2, [(("g", l, j), j % 8) for j in range(2 * TC // 4)])
        for j in range(4):
            plan.use(("peer_out", l, j), j)
        stream_base[l] = list(plan.count)
        for b, n in ((4, NK), (5, NK), (6, NK // 2), (7, NK // 2)):
            plan.count[b] += n

    plan_ada(0)
    for k in range(KD):
        plan.use(("hT", k), k % 8)
    plan.use("dt", 4)
    for ct in range(XBC_CT):
        plan.use(("xbc", ct), ct % 4)
        if ct < 4 or ct >= 8:
            plan.use(("xT", ct), 6 + ct % 2)
    plan.use("decay", 4)
    for d in range(2):
        for g in range(GROUPS):
            plan.use(("S1", d, g), g)
        for g in range(GROUPS):
            plan.use(("S2", d, g), 4 + g)
    for c in range(2):
        for g in range(GROUPS):
            plan.use(("yoff", c, g, 0), 0)
            plan.use(("yoff", c, g, 1), 1)
            plan.use(("cb", c, g), 2)
            for d in range(2):
                plan.use(("seg", c, g, d, 0), 4 + 2 * d)
                plan.use(("seg", c, g, d, 1), 5 + 2 * d)
            plan.use(("ydiag", c, g), 3)
    for j in range(8):
        plan.use(("z", j), j % 4)
    for ct in range(8):
        plan.use(("uT", ct), 4 + ct % 2)
    for j in range(4):
        plan.use(("mout", j), j)
    plan_peer(0)
    plan_ada(1)
    for j in range(3):
        plan.use(("hid", j), 4)
    for n in range(2 * TT * ORDER):
        plan.use(("hflt", n, 0), 5 + n % 2)
        plan.use(("hflt", n, 1), 7 if n % 2 else 4)
    for n in range(2 * ORDER):
        plan.use(("hnorm", n), n % 4)
    for n in range(5 * ORDER * 2):
        plan.use(("hspec", n), 4 + n % 4)
    for k in range(4):
        plan.use(("hhT", k), k)
    for b in range(12):
        plan.use(("hu", b), 4 + b % 4)
    for o in range(ORDER):
        for j in range(4):
            plan.use(("vtok", o, j), j)
        for n in range(4):
            plan.use(("vs", o, n, 0), 4 + 2 * (n % 2))
            plan.use(("vs", o, n, 1), 5 + 2 * (n % 2))
        for c in range(4):
            plan.use(("inv", o, c), c)
    for j in range(4):
        plan.use(("hout", j), 4 + j)
    plan_peer(1)

    blocks = []

    def columns(w, c0):
        return w[:, c0:c0 + BLK].rearrange("(k p) c -> p k c", p=P)

    def rows(w, r0):
        return w[r0:r0 + 2 * P, :].rearrange("(k p) c -> p k c", p=P)

    first = {}
    block_done = []
    w_used = sem("weight_blocks_used")
    used = [0]

    def by_count():
        used[0] += 1
        return w_used, used[0]

    def by_bank(key):
        b, n = plan(key)
        return full[b], n + 1

    def stage(name, aps, done):
        first[name] = len(blocks)
        blocks.extend(aps)
        block_done.extend(done(n) for n in range(len(aps)))

    def ada_done(l):
        def done(n):
            j, s = n // 12, n % 12
            return by_count() if s < 8 or s % 2 == 0 else by_bank(("ada_gate", l, j, (s - 8) // 2))
        return done

    for l in range(DEPTH):
        stage(("ada", l), [columns(A["ada_w"][l], BLK * b) for b in range(24)], ada_done(l))
        if l == 0:
            stage("xbc", [columns(A["m_w_in"][0], INNER + BLK * b) for b in (8, 9, 10, 11, *range(8))], lambda n: by_bank(("xbc", 2 * n + 1)))
            stage("z", [columns(A["m_w_in"][0], BLK * b) for b in range(8)], lambda n: by_bank(("z", n)))
            stage("mout", [rows(A["m_w_out"][0], 2 * P * b) for b in range(8)], lambda n: by_count() if n < 7 else by_bank(("mout", 3)))
        else:
            stage("hin", [columns(A["h_w_in"][0], BLK * b) for b in range(12)], lambda n: by_bank(("hu", n)))
            stage("hout", [rows(A["h_w_out"][0], 2 * P * b) for b in range(4)], lambda n: by_count() if n < 3 else by_bank(("hout", 3)))
        stage(("wq", l), [columns(A["p_wq"][l], BLK * b) for b in range(8)], lambda n: by_bank(("q", l, n)))
    w_loaded = [sem(f"weight_block{s}_loaded") for s in range(RING)]

    uv_loaded = [sem(f"expert_rows{j}_loaded") for j in range(UV)]
    g_loaded = [sem(f"g_tiles{j}_loaded") for j in range(2)]
    g_stored = [sem(f"g_chunk{j}_stored") for j in range(2)]
    phase = sem("phase_ended")
    PH_PEER0, PH_BUILD0, PH_STREAM0, PH_HYF, PH_HYM, PH_PEER1, PH_BUILD1, PH_STREAM1 = range(1, 9)

    def phase_end(eng, n):
        eng.drain().then_inc(phase, 1)
        eng.wait_ge(phase, 5 * n)

    def wait_read(eng, key, i=0):
        b, n = plan(key, i)
        eng.wait_ge(read[b], n + 1)

    def wait_full(eng, key, i=0):
        b, n = plan(key, i)
        eng.wait_ge(full[b], n + 1)
        return b

    def place_free(eng, l, n, i):
        if n >= 2:
            b, u = plan(("g", l, 2 * n - 3), i)
            eng.wait_ge(full[b], u + 1)
        else:
            b, u = plan(("g", l, 2 * n + 13), i)
            eng.wait_ge(full[b], u - 1)

    def tiles(eng, step):
        step(0, 0)
        with eng.Fori(0, NROUND) as i:
            for off in range(1, ROUND + 1):
                step(i * ROUND + off, off, i)
        for off in range(ROUND * NROUND + 1, NK):
            step(off, off)

    block = ctx.enter_context(nc.Block())

    @block.sync
    def _(sp):
        sp.dma_start(cst[:], A["constants"].rearrange("p (a b) -> p a b", a=7)).then_inc(sem("constants_in"), 16)
        cw = A["m_conv_w"][0].rearrange("i j (c b) -> (i j c) b", b=P)
        loads = [
            (stg[0:128, 0, :], cw[0:128]), (stg[0:88, 1, :], cw[128:216]),
            (stg[88:112, 1, :], A["m_conv_b"][0].rearrange("(c b) -> c b", b=P)),
            (stg[112:128, 1, :], A["m_norm_w"][0].rearrange("(c b) -> c b", b=P)),
            (stg[0:72, 2, :], A["h_conv_w"][0].rearrange("i (c b) -> (i c) b", b=P)),
            (stg[72:96, 2, :], A["h_conv_b"][0].rearrange("(c b) -> c b", b=P)),
            (stg[96:112, 2, :], A["h_bias"][0].rearrange("i (c b) -> (i c) b", b=P)),
            (stg[112:120, 2, :], A["c"][0].rearrange("(c b) -> c b", b=P)),
            (stg[120:128, 2, :], A["c_ctx"].rearrange("(c b) -> c b", b=P)),
            (stg[0:96, 3, :], A["ada_b"].rearrange("l (c b) -> (l c) b", b=P)),
        ]
        for dst, src in loads:
            sp.dma_start(dst, src).then_inc(sem("vectors_in"), 16)

        def weights(n0, n1):
            for n in range(n0, n1):
                if n >= RING:
                    sp.wait_ge(*block_done[n - RING])
                k = blocks[n].shape[1]
                dst = wring[n % RING][:, :].rearrange("p (k c) -> p k c", k=k)
                sp.dma_start(dst, blocks[n]).then_inc(w_loaded[n % RING], 16)

        def ln_rows(l, j):
            sp.wait_ge(sem("layer_norms_done"), 2 * l + j)
            sp.dma_start(lnb[:, 0, :], A["ln_g"][l, j].partition_broadcast(P)).then_inc(sem("ln_rows_in"), 16)
            sp.dma_start(lnb[:, 1, :], A["ln_b"][l, j].partition_broadcast(P)).then_inc(sem("ln_rows_in"), 16)

        def gate_rows(l):
            sp.wait_ge(sem("layer_norms_done"), 2 * l)
            for j, c0 in enumerate((2 * D, 5 * D)):
                sp.dma_start(gate[j][:], A["ada_b"][l, c0:c0 + D].partition_broadcast(P)).then_inc(sem("gate_rows_in"), 16)

        weights(0, 4)
        gate_rows(0)
        sp.dma_start(ctxb, A["ctx"].rearrange("o (t p) d -> p (o t) d", p=P)).then_inc(sem("tokens_in"), 16)
        sp.dma_start(xres[:], A["x"].rearrange("o (t p) d -> p (o t) d", p=P)).then_inc(sem("tokens_in"), 16)
        sp.dma_start(wdt[:], A["m_w_in"][0][:, INNER + XBC_CT * P:].rearrange("(k p) c -> p k c", p=P)).then_inc(sem("dt_in"), 16)
        sp.dma_start(dtb[:], A["m_dt_bias"].rearrange("o a b -> o (a b)")).then_inc(sem("dt_in"), 16)
        sp.dma_start(aneg[:], A["m_a_log"].rearrange("o a b -> (o a b)").partition_broadcast(P)).then_inc(sem("dt_in"), 16)
        sp.dma_start(dskip[:], A["m_d"].rearrange("o b -> (o b)").partition_broadcast(P)).then_inc(sem("dt_in"), 16)
        ln_rows(0, 0)
        weights(4, first[("wq", 0)] + 4)

        def peer(l):
            u, v = A["p_u"][l], A["p_v"][l]
            sp.dma_start(kraw[:, 0:PH, :], A["p_k1"][l].rearrange("h k d -> k h d")).then_inc(sem("keys_in"), 16)
            sp.dma_start(kraw[:, PH:, :], A["p_k2"][l].rearrange("h k d -> k h d")).then_inc(sem("keys_in"), 16)

            def tile(m, slot):
                sp.dma_start(uvring[slot][:, 0, :], u[bass.ds(m * P, P), :]).then_inc(uv_loaded[slot], 16)
                sp.dma_start(uvring[slot][:, 1, :], v[bass.ds(m * P, P), :]).then_inc(uv_loaded[slot], 16)

            def g_tiles(n, j):
                sp.dma_start(gt[j][:], gdram[:, :, bass.ds(n * GI * TC, GI * TC)]).then_inc(g_loaded[j], 16)

            for m in range(UV):
                tile(m, m)
            weights(first[("wq", l)] + 4, first[("wq", l)] + 8)
            ln_rows(l, 1)
            if l == 0:
                weights(first[("ada", 1)], first[("ada", 1)] + 4)
            phase_end(sp, 2 + 5 * l)
            phase_end(sp, 3 + 5 * l)
            for j in range(2):
                sp.wait_ge(g_stored[j], 16 * (l + 1) * (NTC // 2))
            g_tiles(0, 0)
            g_tiles(1, 1)

            def refill(m, slot):
                sp.wait_ge(sem("v_split"), m + (l * NK - UV + 1))
                sp.wait_ge(uv_loaded[slot], 32)
                tile(m, slot)

            with sp.Fori(0, NROUND) as i:
                for off in range(UV, UV + ROUND):
                    refill(i * ROUND + off, off % UV)
                    if off % GI == GI - 1:
                        n = (off + 1) // GI
                        sp.wait_ge(sem("gated"), i * ROUND + (l * NK + (n - 1) * GI))
                        sp.wait_ge(g_loaded[n % 2], 16)
                        g_tiles(i * 2 + n, n % 2)
            for m in range(UV + ROUND * NROUND, NK):
                refill(m, m % UV)

        phase_end(sp, 1)
        peer(0)
        gate_rows(1)
        weights(first[("ada", 1)] + 4, first["hin"] + 4)
        phase_end(sp, 4)
        for dst, src in [
            (hc[:], A["hyena_constants"]), (hv[:, 0:1], A["h_f_b1"].rearrange("o f -> f o")),
            (hv[:, 1:2], A["h_f_b2"][0, 0:1, :].rearrange("o f -> f o")),
            (hv[:, 2:3], A["h_f_b2"][0, 1:2, :].rearrange("o f -> f o")), (hv[:, 3:4], A["h_freq"].rearrange("o f -> f o")),
            (hw1[:], A["h_f_w1"][0]), (hw2[:], A["h_f_w2"][0].rearrange("j a b -> a j b")),
            (zf[:], A["filter_features"]), (tcol[:], A["lag_times"]),
            (delta[:], A["decay_rates"].partition_broadcast(P)), (w3[:], A["h_f_w3"][0]),
        ]:
            sp.dma_start(dst, src).then_inc(sem("hyena_in"), 16)
        ln_rows(1, 0)
        phase_end(sp, 5)
        weights(first["hin"] + 4, first[("wq", 1)] + 4)
        phase_end(sp, 6)
        peer(1)
        sp.wait_ge(sem("layer_norms_done"), 4)
        sp.dma_start(out.rearrange("o (t p) d -> p (o t) d", p=P), xres[:]).then_inc(sem("out_stored"), 16)
        sp.wait_ge(sem("out_stored"), 16)

    @block.tensor
    def _(pe):
        mm = nc.tensor.matmul
        order = {b: 0 for b in range(8)}

        def begin(key, i=0):
            b, n = plan(key, i)
            pe.wait_ge(read[b], n)
            return b

        def block_in(n):
            pe.wait_ge(w_loaded[n % RING], 16 * (n // RING + 1))
            return wring[n % RING]

        pe.wait_ge(sem("constants_in"), 16)
        pe.wait_ge(sem("vectors_in"), 160)
        for t in range(3):
            nc.tensor.transpose(ps[0][:, t * P:(t + 1) * P], stg[:, t, :], ident)
        nc.tensor.transpose(ps[0][:, 3 * P:3 * P + 96], stg[0:96, 3, :], ident[0:96, 0:96]).then_inc(full[0], 1)

        def modulation(l):
            base = first[("ada", l)] // RING
            for n in range(2):
                if n == 0:
                    pe.wait_ge(sem("silu_c"), 1)
                b = begin(("ada_cols", l, n))
                with pe.Fori(0, 2) as i:
                    for s in range(RING):
                        pe.wait_ge(w_loaded[s], i * 16 + 16 * (base + 3 * n + 1))
                        for c in range(2):
                            o = ps[b][:, bass.ds(i * 16 + 4 * s + 2 * c, 2)]
                            for k in range(KD):
                                last = mm(o, wring[s][:, k * BLK + c * P:k * BLK + (c + 1) * P], s_col[:, k, :],
                                          start=(k == 0), stop=(k == KD - 1))
                        last.then_inc(w_used, 1)
                mm(ps[b][:, 32:34], ident, s_col[:, 0, :], start=True, stop=True).then_inc(full[b], 1)
                if n == 0 and l == 0:
                    pe.wait_ge(sem("silu_c_rows"), 1)
                for h in range(2):
                    b = begin(("ada_gate", l, n, h))
                    for s in (2 * h, 2 * h + 1):
                        w = block_in(first[("ada", l)] + 12 * n + 8 + s)
                        for k in range(KD):
                            last = mm(ps[b][:, (s % 2) * BLK:(s % 2 + 1) * BLK], s_rep[:, k, :], w[:, k * BLK:(k + 1) * BLK],
                                      start=(k == 0), stop=(k == KD - 1))
                        if s % 2 == 0:
                            last.then_inc(w_used, 1)
                    last.then_inc(full[b], 1)

        modulation(0)
        pe.wait_ge(sem("tokens_in"), 32)
        for k in range(KD):
            b = begin(("hT", k))
            for t in range(4):
                src = ctxb[:, t, k * P:(k + 1) * P] if t < 2 else xres[:, t - 2, k * P:(k + 1) * P]
                last = nc.tensor.transpose(ps[b][:, t * P:(t + 1) * P], src, ident)
            last.then_inc(full[b], 1)
        pe.wait_ge(sem("dt_in"), 64)
        b = begin("dt")
        for k in range(KD):
            wait_read(pe, ("hT", k))
        for t in range(4):
            o = ps[b][:, t * 64:(t + 1) * 64]
            for k in range(KD):
                mm(o, hT[:, k, t * P:(t + 1) * P], wdt[:, k, :], start=(k == 0), stop=False)
            last = mm(o, cst[0:1, C_ONE, :], dtb[0:1, :], start=False, stop=True)
        last.then_inc(full[b], 1)
        for q in range(XBC_CT + 2):
            if q < XBC_CT:
                w = block_in(first["xbc"] + q // 2)
                b = begin(("xbc", q))
                for k in range(KD):
                    last = mm(ps[b][:, :], w[:, k * BLK + (q % 2) * P:k * BLK + (q % 2 + 1) * P], hT[:, k, :],
                              start=(k == 0), stop=(k == KD - 1))
                last.then_inc(full[b], 1)
            r = q - 2
            if 0 <= r < 4 or r >= 8:
                pe.wait_ge(sem("conv_silu"), r + 1)
                b = begin(("xT", r))
                for t in range(4):
                    last = nc.tensor.transpose(ps[b][:, t * P:(t + 1) * P], xc[r % 2][:, t * P:(t + 1) * P], ident)
                last.then_inc(full[b], 1)
        pe.wait_ge(sem("a_ready"), 1)
        b = begin("decay")
        F, B = slice(0, HEADS), slice(HEADS, 2 * HEADS)
        for n, terms in enumerate([
            [(C_GT, 0, F), (C_ONE, 1, F)], [(C_GT, 1, F)], [(C_GT, 2, F)],
            [(C_LT, 1, B), (C_ONE, 0, B)], [(C_LT, 0, B)], [(C_LT, 3, B)],
            [(C_LE, 2, F)], [(C_LE, 3, F)], [(C_GE, 2, B)], [(C_GE, 3, B)], [(C_ONE, 2, F)], [(C_ONE, 3, B)],
        ]):
            for j, (m, c, h) in enumerate(terms):
                last = mm(ps[b][:, n * HEADS:(n + 1) * HEADS], cst[:, m, :], a_t[:, c, h],
                          start=(j == 0), stop=(j == len(terms) - 1))
        last.then_inc(full[b], 1)
        for d in range(2):
            chunks = (0, 1, 2) if d == 0 else (1, 0, 3)
            for n, c in enumerate(chunks):
                j = 3 * d + n
                pe.wait_ge(sem("x_weighted"), j + 1)
                for g in range(GROUPS):
                    if n == 0:
                        b = begin(("S1", d, g))
                    elif n == 2:
                        b = begin(("S2", d, g))
                    else:
                        b = plan(("S1", d, g))[0]
                    last = mm(ps[b][:, :], btok[:, c, g * P:(g + 1) * P], xw[j % 2][:, g * GW:(g + 1) * GW],
                              start=(n != 1), stop=(n != 0))
                    if n:
                        last.then_inc(full[b], 1)
                    elif g == GROUPS - 1:
                        last.then_inc(sem("x_weighted_first_used"), 1)
        for c in range(2):
            for g in range(GROUPS):
                ct_ = bcT[:, 4 + g, c * P:(c + 1) * P]
                for d in range(2):
                    b = begin(("yoff", c, g, d))
                    which, states = ("S1", S1) if c == d else ("S2", S2)
                    wait_read(pe, (which, d, g))
                    st = states[:, d, g * GW:(g + 1) * GW]
                    mm(ps[b][:, :], ct_, st, start=True, stop=True).then_inc(full[b], 1)
                b = begin(("cb", c, g))
                mm(ps[b][:, 0:P], bcT[:, g, c * P:(c + 1) * P], ct_, start=True, stop=True).then_inc(full[b], 1)
                for d in range(2):
                    pe.wait_ge(sem("a_masked"), 2 * (4 * c + g) + d + 1)
                    for h in range(HPG):
                        if h % 4 == 0:
                            b = begin(("seg", c, g, d, h // 4))
                        last = mm(ps[b][:, (h % 4) * P:(h % 4 + 1) * P], aM[d][:, h, :], cst[:, (C_LE, C_GE)[d], :],
                                  start=True, stop=True)
                        if h % 4 == 3:
                            last.then_inc(full[b], 1)
                pe.wait_ge(sem("x_dt"), 2 * (c + 1))
                pe.wait_ge(sem("mixing_ready"), 2 * (4 * c + g) + 2)
                b = begin(("ydiag", c, g))
                for h in range(HPG):
                    for d in range(2):
                        hh = g * HPG + h
                        last = mm(ps[b][:, h * HD:(h + 1) * HD], EM[d][:, h, :], xw[d][:, hh * HD:(hh + 1) * HD],
                                  start=(d == 0), stop=(d == 1))
                last.then_inc(full[b], 1)
        for j in range(8):
            w = block_in(first["z"] + j)
            b = begin(("z", j))
            for t in range(TT):
                for k in range(KD):
                    last = mm(ps[b][:, t * BLK:(t + 1) * BLK], hT[:, k, T + t * P:T + (t + 1) * P], w[:, k * BLK:(k + 1) * BLK],
                              start=(k == 0), stop=(k == KD - 1))
            last.then_inc(full[b], 1)
        pe.wait_ge(sem("y_normed"), 1)
        for j in range(8):
            b = begin(("uT", j))
            for c in range(2):
                for t in range(TT):
                    last = nc.tensor.transpose(ps[b][:, (2 * c + t) * P:(2 * c + t + 1) * P],
                                               yv[:, t, (2 * j + c) * P:(2 * j + c + 1) * P], ident)
            last.then_inc(full[b], 1)

        def project(name, keys, lhs, kts, ready):
            for k in range(kts):
                ready(k)
                w = block_in(first[name] + k // 2)
                for t in range(TT):
                    for h in range(2):
                        b = begin(keys[2 * t + h]) if k == 0 else plan(keys[2 * t + h])[0]
                        last = mm(ps[b][:, :], lhs(k, t), w[:, (k % 2) * D + h * 512:(k % 2) * D + (h + 1) * 512],
                                  start=(k == 0), stop=(k == kts - 1))
                        if k == kts - 1:
                            last.then_inc(full[b], 1)
                if k % 2 and k < kts - 1:
                    last.then_inc(w_used, 1)

        project("mout", [("mout", j) for j in range(4)], lambda k, t: uT[:, k, t * P:(t + 1) * P], 16,
                lambda k: wait_read(pe, ("uT", k // 2)))
        phase_end(pe, 1)

        def peer(l):
            pe.wait_ge(sem("layer_norms_done"), 2 * l + 1)
            for j in range(4):
                b = begin(("tT", l, j))
                for c in range(2):
                    for t in range(TT):
                        last = nc.tensor.transpose(ps[b][:, (2 * c + t) * P:(2 * c + t + 1) * P],
                                                   xres[:, t, (2 * j + c) * P:(2 * j + c + 1) * P], ident)
                last.then_inc(full[b], 1)
            for k in range(4):
                wait_read(pe, ("tT", l, k))
            for r in range(NROW // 2):
                w = block_in(first[("wq", l)] + r)
                b = begin(("q", l, r))
                for c in range(2):
                    for k in range(KD):
                        last = mm(ps[b][:, c * T:(c + 1) * T], w[:, k * BLK + c * P:k * BLK + (c + 1) * P], tT[:, k, :],
                                  start=(k == 0), stop=(k == KD - 1))
                last.then_inc(full[b], 1)
            pe.wait_ge(sem("keys_in"), 32 * (l + 1))
            for j in range(4):
                b = begin(("kT", l, j))
                for r in range(4):
                    last = nc.tensor.transpose(ps[b][:, r * P:(r + 1) * P], kraw[:, 4 * j + r, :], ident)
                last.then_inc(full[b], 1)
            for r in range(NROW // 2):
                wait_read(pe, ("q", l, r))
            for t in range(TT):
                for j in range(4):
                    if t == 0:
                        wait_read(pe, ("kT", l, j))
                    b = begin(("sc", l, t, j))
                    for r in range(4):
                        last = mm(ps[b][:, r * P:(r + 1) * P], qT[:, 4 * j + r, t * P:(t + 1) * P], kT[:, 4 * j + r, :],
                                  start=True, stop=True)
                    last.then_inc(full[b], 1)
            for t in range(TT):
                pe.wait_ge(sem("selected"), TT * l + t + 1)
                b = begin(("selT", l, t))
                for j in range(3):
                    last = nc.tensor.transpose(ps[b][:, j * P:(j + 1) * P], seltok[:, j, :], ident)
                last.then_inc(full[b], 1)
            phase_end(pe, 2 + 5 * l)
            groups = 2 * TC // OH
            with pe.Fori(0, NTC // 2) as i:
                for n in range(groups):
                    pe.wait_ge(sem("one_hot_rows"), i * groups + (l * T // OH + n + 1))
                    for t in range(OH):
                        if t % 4 == 0:
                            b = begin(("g", l, 2 * n + t // 4), i)
                        last = mm(ps[b][:, (t % 4) * P:(t % 4 + 1) * P], oneb[n % 2][:, t, :], onea[n % 2][:, t, :],
                                  start=True, stop=True)
                        if t % 4 == 3:
                            last.then_inc(full[b], 1)
            phase_end(pe, 3 + 5 * l)
            base = stream_base[l]
            pe.wait_ge(sem("zeros"), l + 1)
            for j in range(4):
                b = begin(("peer_out", l, j))
                mm(ps[b][:, :], ident, lnt[:, 0, :], start=True, stop=False, skip_group_check=True)

            def transpose_u(m, off, h):
                slot = off % UV
                pe.wait_ge(read[4 + h], m + base[4 + h])
                if h == 0:
                    pe.wait_ge(uv_loaded[slot], (m - slot) * 8 + 32 * (l * (NK // UV) + 1))
                for k in range(4):
                    last = nc.tensor.transpose(ps[4 + h][:, k * P:(k + 1) * P], uvring[slot][:, 0, (4 * h + k) * P:(4 * h + k + 1) * P], ident)
                last.then_inc(full[4 + h], 1)

            def combine(m, off):
                j = off % 2
                pe.wait_ge(sem("w_split"), m + (l * NK + 1))
                pe.wait_ge(sem("v_split"), m + (l * NK + 1))
                final = off == NK - 1
                for t in range(TT):
                    c = slice(t * P, (t + 1) * P)
                    for lhs, rhs in ((Whi, Vhi), (Whi, Vlo), (Wlo, Vhi)):
                        for h in range(2):
                            last = mm(ps[2 * t + h][:, :], lhs[j][:, c], rhs[j][:, h * 512:(h + 1) * 512], start=False,
                                      stop=final and lhs is Wlo, skip_group_check=True)
                            if final and lhs is Wlo:
                                last.then_inc(full[2 * t + h], 1)
                if not final:
                    last.then_inc(sem("combined"), 1)

            def step(m, off, i=None):
                if off != NK - 1:
                    transpose_u(m + 1, off + 1, 0)
                j = off % 2
                half_m = (off // 2) if i is None else i * (ROUND // 2) + off // 2
                pe.wait_ge(read[6 + j], half_m + base[6 + j])
                for h in range(2):
                    pe.wait_ge(read[4 + h], m + (base[4 + h] + 1))
                if off == 0:
                    pe.wait_ge(sem("t_split"), l + 1)
                n = 0
                for k in range(KD):
                    for lhs, rhs in ((UThi, tThi), (UThi, tTlo), (UTlo, tThi)):
                        last = mm(ps[6 + j][:, 0:T], lhs[j][:, k, :], rhs[:, k, :], start=(n == 0), stop=(n == 3 * KD - 1))
                        n += 1
                last.then_inc(full[6 + j], 1)
                if off != NK - 1:
                    transpose_u(m + 1, off + 1, 1)
                if off != 0:
                    combine(m - 1, off - 1)

            for h in range(2):
                transpose_u(0, 0, h)
            tiles(pe, step)
            combine(NK - 1, NK - 1)

        peer(0)
        modulation(1)
        phase_end(pe, 4)
        pe.wait_ge(sem("hyena_in"), 176)
        for j in range(3):
            b = begin(("hid", j))
            if j == 0:
                last = mm(ps[b][0:HY_FF, 0:T], hw1[:], zf[:], start=True, stop=True)
            else:
                pe.wait_ge(sem("sine"), j)
                last = mm(ps[b][0:HY_FF, 0:T], hw2[:, j - 1, :], hid[:, 0, :], start=True, stop=True)
            last.then_inc(full[b], 1)
        pe.wait_ge(sem("sine"), 3)
        n = 0
        for t in range(TT):
            for o in range(ORDER):
                for h in range(2):
                    for side in range(2):
                        b = begin(("hflt", n, side))
                        c = o * 2 * D + side * D + h * 512
                        mm(ps[b][:, :], hid[:, 0, t * P:(t + 1) * P], w3[:, c:c + 512], start=True, stop=True).then_inc(full[b], 1)
                    n += 1
        for o in range(ORDER):
            for h in range(2):
                n = 2 * o + h
                pe.wait_ge(sem("filter_squares"), n + 1)
                b = begin(("hnorm", n))
                for j, w in enumerate((H_WS, H_W1, H_WD, H_W1)):
                    last = mm(ps[b][:, :], hc[:, w:w + P], dcy[:, j // 2, (j % 2) * 512:(j % 2 + 1) * 512],
                              start=(j == 0), stop=(j == 3))
                last.then_inc(full[b], 1)
        n = 0
        for o in range(ORDER):
            for h in range(2):
                pe.wait_ge(sem("filter_normed"), 2 * o + h + 1)
                for tile, (col, step_, side) in enumerate(((H_FR, 256, 0), (H_FR + P, 256, 0), (H_BZ, P, 1), (H_FI + P, 256, 1), (H_C0, P, 0))):
                    b = begin(("hspec", n))
                    for t in range(TT):
                        last = mm(ps[b][:, :], hc[:, col + t * step_:col + t * step_ + P], sd[:, side, t, o, h * 512:(h + 1) * 512],
                                  start=(t == 0), stop=(t == 1))
                    last.then_inc(full[b], 1)
                    n += 1
        phase_end(pe, 5)
        for j in range(4):
            b = begin(("hhT", j))
            for c in range(2):
                for t in range(TT):
                    last = nc.tensor.transpose(ps[b][:, (2 * c + t) * P:(2 * c + t + 1) * P],
                                               xres[:, t, (2 * j + c) * P:(2 * j + c + 1) * P], ident)
            last.then_inc(full[b], 1)
        for j in range(4):
            wait_read(pe, ("hhT", j))
        for n in range(12):
            w = block_in(first["hin"] + n)
            b = begin(("hu", n))
            for c in range(2):
                for k in range(KD):
                    last = mm(ps[b][:, c * T:(c + 1) * T], w[:, k * BLK + c * P:k * BLK + (c + 1) * P], hhT[:, k, :],
                              start=(k == 0), stop=(k == KD - 1))
            last.then_inc(full[b], 1)
        for o in range(ORDER):
            for j in range(4):
                if o == 0:
                    pe.wait_ge(sem("hyena_conv"), 9 + j)
                else:
                    pe.wait_ge(sem("order_done"), 2 * (j + 1))
                b = begin(("vtok", o, j))
                for t in range(TT):
                    for c in range(2):
                        last = nc.tensor.transpose(ps[b][:, (2 * t + c) * P:(2 * t + c + 1) * P],
                                                   huT[:, 16 + 2 * j + c, t * P:(t + 1) * P], ident)
                last.then_inc(full[b], 1)
            for j in range(4):
                wait_read(pe, ("vtok", o, j))
            for n in range(4):
                h, f = n // 2, n % 2
                for part, col in enumerate((H_FR, H_FI)):
                    b = begin(("vs", o, n, part))
                    for t in range(TT):
                        last = mm(ps[b][:, :], hc[:, col + t * 256 + f * P:col + t * 256 + (f + 1) * P], vtok[:, t, h * 512:(h + 1) * 512],
                                  start=(t == 0), stop=(t == 1))
                    last.then_inc(full[b], 1)
            pe.wait_ge(sem("spectrum_done"), 8 * (o + 1))
            for c2 in range(4):
                b = begin(("inv", o, c2))
                for c in range(2):
                    for k in range(4):
                        last = mm(ps[b][:, c * T:(c + 1) * T], Yf[:, k, (2 * c2 + c) * P:(2 * c2 + c + 1) * P],
                                  hc[:, H_INV + k * T:H_INV + (k + 1) * T], start=(k == 0), stop=(k == 3))
                last.then_inc(full[b], 1)
        project("hout", [("hout", j) for j in range(4)], lambda k, t: huT[:, 16 + k, t * P:(t + 1) * P], 8,
                lambda k: pe.wait_ge(sem("order_done"), 8 + k + 1))
        phase_end(pe, 6)
        peer(1)

    @block.gpsimd
    def _(pool):
        tt = nc.gpsimd.tensor_tensor
        pool.wait_ge(sem("a_ready"), 1)
        for c in range(2):
            for g in range(GROUPS):
                for d in range(2):
                    if c + g:
                        wait_full(pool, ("seg", c - (g == 0), (g - 1) % GROUPS, d, 1))
                    a = a_t[:, 2 + c, d * HEADS + g * HPG:d * HEADS + (g + 1) * HPG]
                    tt(aM[d][:, :, :], a.unsqueeze(2).to_broadcast([P, HPG, P]),
                       cst[:, (C_GT, C_LT)[d], :].unsqueeze(1).to_broadcast([P, HPG, P]), ALU.mult).then_inc(sem("a_masked"), 1)
            pool.wait_ge(sem("x_dt"), 2 * (c + 1))
            x3 = xtok[:, 2 + c, :].rearrange("p (h d) -> p h d", h=HEADS)
            tt(x3, x3, dskip[:].unsqueeze(2).to_broadcast([P, HEADS, HD]), ALU.mult).then_inc(sem("x_skip"), 1)
        phase_end(pool, 1)

        def peer(l):
            phase_end(pool, 2 + 5 * l)
            phase_end(pool, 3 + 5 * l)

        peer(0)
        phase_end(pool, 4)
        phase_end(pool, 5)
        phase_end(pool, 6)
        peer(1)

    @block.scalar
    def _(act):
        step = Chain(sem("scalar_steps"))
        f = nc.scalar.activation

        def copy_out(key, out_, in_=None, func=ACT.Copy, **kw):
            b = wait_full(act, key)
            f(out_, ps[b][:, :] if in_ is None else in_(ps[b]), func, **kw).then_inc(read[b], 1)

        wait_read(act, "vecs")
        f(s_col[:, :, :], vec[:, V_C:V_C + 2 * KD].rearrange("p (j k) -> p k j", j=2), ACT.Silu).then_inc(sem("silu_c"), 1)
        act.wait_ge(sem("dt_in"), 64)
        n = step(f(aneg[:], aneg[:], ACT.Exp))
        wait_read(act, "dt")
        n = step(f(dtw[:, 1, :], dtw[:, 0, :], ACT.Abs))
        act.wait_ge(step.sem, n)
        n = step(f(dtw[:, 1, :], dtw[:, 1, :], ACT.Exp, scale=-1.0))
        act.wait_ge(sem("dt_plus_one"), 1)
        n = step(f(dtw[:, 3, :], dtw[:, 2, :], ACT.Ln))
        DT_EXP, DT_LOG = n - 1, n
        assert (DT_EXP, DT_LOG) == (3, 4)
        for q in range(XBC_CT + 2):
            if q < XBC_CT:
                if q >= 2:
                    act.wait_ge(sem("conv_done"), q - 1)
                copy_out(("xbc", q), ubuf[q % 2])
            r = q - 1
            if 0 <= r < XBC_CT:
                act.wait_ge(sem("conv_done"), r + 1)
                if r >= 2 and (r - 2 < 4 or r - 2 >= 8):
                    wait_full(act, ("xT", r - 2))
                if r < 4:
                    f(bcT[:, r, :], cacc[r % 2][:, T:2 * T], ACT.Silu)
                if r < 4 or r >= 8:
                    f(xc[r % 2], cacc[r % 2], ACT.Silu).then_inc(sem("conv_silu"), 1)
                else:
                    f(bcT[:, r, :], cacc[r % 2][:, T:2 * T], ACT.Silu).then_inc(sem("conv_silu"), 1)
            r = q - 2
            if 0 <= r < 4:
                copy_out(("xT", r), btok[:, :, r * P:(r + 1) * P], lambda b: b[:, :].rearrange("p (t c) -> p t c", t=4))
            elif r >= 8:
                copy_out(("xT", r), xtok[:, :, (r - 8) * P:(r - 7) * P], lambda b: b[:, :].rearrange("p (t c) -> p t c", t=4))
        copy_out("decay", dec[:, :, :].rearrange("p a b -> p (a b)"), lambda b: b[:, 0:12 * HEADS], ACT.Exp)
        for d in range(2):
            for g in range(GROUPS):
                copy_out(("S1", d, g), S1[:, d, g * GW:(g + 1) * GW])
        for c in range(2):
            for g in range(GROUPS):
                for d in range(2):
                    if c + g:
                        wait_full(act, ("ydiag", c - (g == 0), (g - 1) % GROUPS))
                    for h in range(2):
                        copy_out(("seg", c, g, d, h), EM[d][:, 4 * h:4 * h + 4, :].rearrange("p a b -> p (a b)"), None, ACT.Exp)
        for j in range(8):
            if j >= 2:
                act.wait_ge(sem("y_gated"), j - 1)
            copy_out(("z", j), zs[j % 2], None, ACT.Silu)
            if j % 2:
                act.wait_ge(sem("y_gated"), j + 1)
                for t in range(TT):
                    n = step(f(lnt[:, t, :], yv[:, t, (j // 2) * GW:(j // 2 + 1) * GW], ACT.Square,
                               accum_out=ss[:, (j // 2) * 2 + t:(j // 2) * 2 + t + 1]))
                    act.wait_ge(step.sem, n)
        assert n == DT_LOG + 8
        act.wait_ge(sem("rms_mean"), 1)
        f(ss[:, 16:24], ss[:, 8:16], ACT.Sqrt).then_inc(sem("rms_root"), 1)
        for j in range(8):
            b = wait_full(act, ("uT", j))
            for c in range(2):
                last = f(uT[:, 2 * j + c, :], ps[b][:, c * T:(c + 1) * T], ACT.Identity, scale=vec[:, V_NW + 2 * j + c:V_NW + 2 * j + c + 1])
            last.then_inc(read[b], 1)

        def layer_norm(l, j):
            act.wait_ge(sem("ln_variance"), 2 * l + j + 1)
            f(small[:, :, 15], small[:, :, 14], ACT.Sqrt).then_inc(sem("ln_root"), 1)

        layer_norm(0, 0)
        phase_end(act, 1)

        def peer(l):
            for j in range(4):
                wait_read(act, ("tT", l, j))
                f(tThi[:, 2 * j:2 * j + 2, :], tT[:, 2 * j:2 * j + 2, :], ACT.Copy).then_inc(sem("t_hi"), 1)
            q4 = qT[:, :, :].rearrange("p (a h) t -> p a h t", a=2)
            for r in range(PH):
                copy_out(("q", l, r), q4[:, :, r, :], lambda b: b[:, :].rearrange("p (a t) -> p a t", a=2))
            for j in range(4):
                copy_out(("kT", l, j), kT[:, 4 * j:4 * j + 4, :].rearrange("p a b -> p (a b)"))
            for t in range(TT):
                if t:
                    act.wait_ge(sem("selected"), TT * l + t)
                for j in range(4):
                    copy_out(("sc", l, t, j), sc[:, 4 * j:4 * j + 4, :].rearrange("p a b -> p (a b)"))
                act.wait_ge(sem("gate_shifted"), TT * l + t + 1)
                f(selv[:, :, :], selv[:, :, :], ACT.Exp).then_inc(sem("gate_exp"), 1)
            phase_end(act, 2 + 5 * l)
            with act.Fori(0, NTC // 2) as i:
                for c in range(2):
                    act.wait_ge(g_stored[c], i * 16 + 16 * l * (NTC // 2))
                    for n in range(TC // 4):
                        key = ("g", l, c * (TC // 4) + n)
                        b, u = plan(key, i)
                        act.wait_ge(full[b], u + 1)
                        f(gch[:, c, :, 4 * n:4 * n + 4].rearrange("p i t -> p t i"), ps[b][:, :].rearrange("p (t i) -> p t i", t=4),
                          ACT.Copy).then_inc(read[b], 1)
                    for n in range(TC // 4):
                        wait_read(act, ("g", l, c * (TC // 4) + n), i)
                    act.dma_start(gdram[:, bass.ds(i * 2 + c, 1), :].rearrange("p o c -> p (o c)"),
                                  gch[:, c, :, :].rearrange("p i t -> p (i t)")).then_inc(g_stored[c], 16)
            for c in range(2):
                act.wait_ge(g_stored[c], 16 * (l + 1) * (NTC // 2))
            phase_end(act, 3 + 5 * l)
            base = stream_base[l]

            def split_u(m, off, h):
                j = off % 2
                act.wait_ge(full[4 + h], m + (base[4 + h] + 1))
                if off >= 2 and h == 0:
                    act.wait_ge(full[6 + j], half(m, off) + base[6 + j])
                f(UThi[j][:, 4 * h:4 * h + 4, :].rearrange("p a b -> p (a b)"), ps[4 + h][:, :], ACT.Copy).then_inc(sem("u_hi"), 1)

            loop = [None]

            def half(m, off):
                return off // 2 if loop[0] is None else loop[0] * (ROUND // 2) + off // 2

            def tile_step(m, off, i=None):
                loop[0] = i
                j = off % 2
                slot = off % UV
                last_tile = off == NK - 1
                if not last_tile:
                    split_u(m + 1, off + 1, 0)
                act.wait_ge(uv_loaded[slot], (m - slot) * 8 + 32 * (l * (NK // UV) + 1))
                if off >= 2:
                    act.wait_ge(sem("combined"), m + (l * (NK - 1) - 1))
                elif off == 1:
                    act.wait_ge(sem("combined"), m + (l * (NK - 1) - 1))
                f(Vhi[j][:], uvring[slot][:, 1, :], ACT.Copy).then_inc(sem("v_hi"), 1)
                if not last_tile:
                    split_u(m + 1, off + 1, 1)
                act.wait_ge(full[6 + j], half(m, off) + (base[6 + j] + 1))
                if off >= 1:
                    act.wait_ge(sem("gated"), m + (l * NK - 1))
                f(gel[j][:], ps[6 + j][:, 0:T], ACT.Gelu).then_inc(read[6 + j], 1)

            for h in range(2):
                split_u(0, 0, h)
            tiles(act, tile_step)
            layer_norm(l, 1)

        peer(0)
        phase_end(act, 4)
        for j in range(3):
            act.wait_ge(sem("sine_argument"), j + 1)
            f(hid[:, 0, :], hid[:, 3, :], ACT.Sin).then_inc(sem("sine"), 1)
        act.wait_ge(sem("hyena_in"), 176)
        for t in range(TT):
            f(dcy[:, t, :], delta[:], ACT.Exp, scale=tcol[:, t:t + 1]).then_inc(sem("lag_decay"), 1)
        for o in range(ORDER):
            for h in range(2):
                n = 2 * o + h
                if n == 0:
                    act.wait_ge(sem("filter_sides"), 2 * TT * ORDER)
                else:
                    wait_full(act, ("hnorm", n - 1))
                for side in range(2):
                    for t in range(TT):
                        last = f(dcy[:, side, t * 512:(t + 1) * 512], sd[:, side, t, o, h * 512:(h + 1) * 512], ACT.Square)
                last.then_inc(sem("filter_squares"), 1)
                wait_read(act, ("hnorm", n))
                f(rsn[:], rsn[:], ACT.Sqrt).then_inc(sem("norm_root"), 1)
        n = 0
        for o in range(ORDER):
            for h in range(2):
                for tile in range(5):
                    copy_out(("hspec", n), Hs[:, o, tile, h * 512:(h + 1) * 512])
                    n += 1
        phase_end(act, 5)
        for n in range(12):
            if n >= 2:
                act.wait_ge(sem("hyena_conv"), n - 1)
            copy_out(("hu", n), hub[n % 2][:, :, :].rearrange("p a b -> p (a b)"))
        for o in range(ORDER):
            for j in range(4):
                copy_out(("vtok", o, j), vtok[:, :, j * 2 * P:(j + 1) * 2 * P], lambda b: b[:, :].rearrange("p (t c) -> p t c", t=TT))
        layer_norm(1, 0)
        phase_end(act, 6)
        peer(1)

    @block.vector
    def _(dve):
        step = Chain(sem("vector_steps"))
        V = nc.vector
        tt, ts, stt = V.tensor_tensor, V.tensor_scalar, V.scalar_tensor_tensor

        def after(n):
            dve.wait_ge(step.sem, n)

        def bc(ap, n, width):
            return ap.unsqueeze(2).to_broadcast([P, n, width])

        dve.wait_ge(full[0], 1)
        V.tensor_copy(vec[:, 0:480], ps[0][:, 0:480]).then_inc(read[0], 1)
        dve.wait_ge(sem("silu_c"), 1)
        V.tensor_copy(s_rep[:, :, :], s_col[:, :, 0:1].to_broadcast([P, KD, P])).then_inc(sem("silu_c_rows"), 1)

        def modulation(l):
            for n in range(2):
                b = wait_full(dve, ("ada_cols", l, n))
                c = V_ADA + 48 * l + 24 * n
                tt(ada[:, 2 * n:2 * n + 2, :, :].rearrange("p a k j -> p (a k) j"), ps[b][:, 0:32].rearrange("p (a j) -> p a j", j=2),
                   bc(vec[:, c:c + 16], 16, 2), ALU.add).then_inc(read[b], 1)
                wait_read(dve, ("ada_cols", l, n))
                sc1 = ada[:, 2 * n + 1, :, :]
                ts(sc1, sc1, 1.0, None, ALU.add).then_inc(sem("modulation_ready"), 1)
                if n == 0:
                    dve.wait_ge(sem("gate_rows_in"), 32 * (l + 1))
                for h in range(2):
                    b = wait_full(dve, ("ada_gate", l, n, h))
                    gh = gate[n][:, h * 512:(h + 1) * 512]
                    tt(gh, ps[b][:, :], gh, ALU.add).then_inc(read[b], 1)

        def modulate(key, dsts, l, pair):
            for j in range(4):
                b = wait_full(dve, key + (j,))
                for c in range(2):
                    k = 2 * j + c
                    last = ts(dsts[:, k, :], ps[b][:, c * T:(c + 1) * T], ada[:, 2 * pair + 1, k, 0:1], ada[:, 2 * pair, k, 0:1], ALU.mult, ALU.add)
                last.then_inc(read[b], 1)

        modulation(0)
        dve.wait_ge(sem("modulation_ready"), 2)
        for k in range(KD):
            b = wait_full(dve, ("hT", k))
            for half_, j in ((0, 1), (1, 0)):
                last = ts(hT[:, k, half_ * T:(half_ + 1) * T], ps[b][:, half_ * T:(half_ + 1) * T],
                          ada[:, 1, k, j:j + 1], ada[:, 0, k, j:j + 1], ALU.mult, ALU.add)
            last.then_inc(read[b], 1)
        b = wait_full(dve, "dt")
        V.tensor_copy(dtw[:, 0, :], ps[b][:, 0:256]).then_inc(read[b], 1)
        dve.wait_ge(sem("scalar_steps"), 3)
        ts(dtw[:, 2, :], dtw[:, 1, :], 1.0, None, ALU.add).then_inc(sem("dt_plus_one"), 1)
        dve.wait_ge(sem("dt_plus_one"), 1)
        n = step(ts(dtw[:, 4, :], dtw[:, 2, :], -1.0, None, ALU.add))
        after(n)
        n = step(ts(dtw[:, 5, :], dtw[:, 4, :], 0.0, None, ALU.is_equal))
        after(n)
        n = step(tt(dtw[:, 4, :], dtw[:, 4, :], dtw[:, 5, :], ALU.add))
        dve.wait_ge(sem("scalar_steps"), 4)
        n = step(tt(dtw[:, 3, :], dtw[:, 3, :], dtw[:, 5, :], ALU.add))
        after(n)
        n = step(tt(dtw[:, 3, :], dtw[:, 3, :], dtw[:, 1, :], ALU.mult))
        n = step(V.reciprocal(dtw[:, 4, :], dtw[:, 4, :]))
        after(n)
        n = step(tt(dtw[:, 3, :], dtw[:, 3, :], dtw[:, 4, :], ALU.mult))
        after(n)
        dtf = dt_t[:, :, :].rearrange("p a b -> p (a b)")
        n = step(stt(dtf, dtw[:, 0, :], 0.0, dtw[:, 3, :], ALU.max, ALU.add))
        after(n)
        stt(a_t[:, :, :], dt_t[:, :, :], -1.0, aneg[:].unsqueeze(1).to_broadcast([P, 4, 2 * HEADS]), ALU.mult, ALU.mult).then_inc(sem("a_ready"), 1)
        for q in range(XBC_CT):
            ct = 16 + q if q < 8 else q - 8
            u, acc = ubuf[q % 2], cacc[q % 2]
            wait_read(dve, ("xbc", q))
            if q >= 2:
                dve.wait_ge(sem("conv_silu"), q - 1)

            def tap(i, j):
                return vec[:, V_CW + (3 * i + j) * 24 + ct:V_CW + (3 * i + j) * 24 + ct + 1]

            bias = vec[:, V_CB + ct:V_CB + ct + 1]
            ug = u[:, T:2 * T].rearrange("p (r c) -> p r c", r=ROWS)
            ag = acc[:, T:2 * T].rearrange("p (r c) -> p r c", r=ROWS)
            nl = nx = step(ts(acc, u, tap(1, 1), bias, ALU.mult, ALU.add))
            ctx_taps = [(1, 0), (1, 2)] if q < 4 or q >= 8 else []
            for i, j in [(1, 0), (1, 2), (0, 1), (2, 1), (0, 0), (0, 2), (2, 0), (2, 2)]:
                if ctx_taps:
                    _, jj = ctx_taps.pop(0)
                    o, s_ = (acc[:, 1:T], u[:, 0:T - 1]) if jj == 0 else (acc[:, 0:T - 1], u[:, 1:T])
                    after(nx)
                    nx = step(stt(o, s_, tap(1, jj), o, ALU.mult, ALU.add))
                di, dj = i - 1, j - 1
                r0, r1, c0, c1 = max(0, -di), ROWS - max(0, di), max(0, -dj), GRID_W - max(0, dj)
                o, s_ = ag[:, r0:r1, c0:c1], ug[:, r0 + di:r1 + di, c0 + dj:c1 + dj]
                after(nl)
                last = stt(o, s_, tap(i, j), o, ALU.mult, ALU.add)
                if (i, j) == (2, 2):
                    last.then_inc(sem("conv_done"), 1)
                else:
                    nl = step(last)
        wait_read(dve, "decay")
        cols = ((DC_F0, 0, 0), (DC_F1, 1, 0), (DC_F2, 2, 0), (DC_B1, 1, 1), (DC_B0, 0, 1), (DC_B3, 3, 1))
        for j, (dc, c, d) in enumerate(cols):
            n = step(tt(wst[:, j, :], dec[:, dc, :], dt_t[:, c, d * HEADS:(d + 1) * HEADS], ALU.mult))
        after(n)
        for r in range(8, XBC_CT):
            if r >= XBC_CT - 2:
                wait_read(dve, ("xT", r))

        def weigh(dst, c, w):
            return tt(dst.rearrange("p (h d) -> p h d", h=HEADS), xtok[:, c, :].rearrange("p (h d) -> p h d", h=HEADS),
                      bc(w, HEADS, HD), ALU.mult)

        def later_state(d):
            for g in range(GROUPS):
                wait_read(dve, ("S1", d, g))
                s2 = S2[:, d, g * GW:(g + 1) * GW]
                t_ = dec[:, (DC_TF2, DC_TB3)[d], g * HPG:(g + 1) * HPG]
                n = step(tt(s2.rearrange("p (h d) -> p h d", h=HPG), S1[:, d, g * GW:(g + 1) * GW].rearrange("p (h d) -> p h d", h=HPG),
                            bc(t_, HPG, HD), ALU.mult))
                b = wait_full(dve, ("S2", d, g))
                after(n)
                tt(s2, s2, ps[b][:, :], ALU.add).then_inc(read[b], 1)

        for j, (dc, c, d) in enumerate(cols):
            if j in (2, 5):
                dve.wait_ge(sem("x_weighted_first_used"), d + 1)
            elif j == 3:
                wait_full(dve, ("S1", 0, GROUPS - 1))
            elif j == 4:
                wait_full(dve, ("S2", 0, GROUPS - 1))
            weigh(xw[j % 2][:, :], c, wst[:, j, :]).then_inc(sem("x_weighted"), 1)
            if j == 2:
                later_state(0)
        later_state(1)
        for c in range(2):
            if c == 0:
                wait_full(dve, ("S1", 1, GROUPS - 1))
                wait_full(dve, ("S2", 1, GROUPS - 1))
            else:
                wait_full(dve, ("ydiag", 0, GROUPS - 1))
            for d in range(2):
                weigh(xw[d][:, :], 2 + c, dt_t[:, 2 + c, d * HEADS:(d + 1) * HEADS]).then_inc(sem("x_dt"), 1)
            for g in range(GROUPS):
                y = yv[:, c, g * GW:(g + 1) * GW]
                b = wait_full(dve, ("cb", c, g))
                n = step(tt(cbm[:, 0, :], ps[b][:, 0:P], cst[:, C_LE, :], ALU.mult))
                tt(cbm[:, 1, :], ps[b][:, 0:P], cst[:, C_GE, :], ALU.mult).then_inc(read[b], 1)
                after(n)
                wait_read(dve, ("cb", c, g))
                for d in range(2):
                    for h in range(2):
                        wait_read(dve, ("seg", c, g, d, h))
                    tt(EM[d][:, :, :], EM[d][:, :, :], cbm[:, d, :].unsqueeze(1).to_broadcast([P, HPG, P]), ALU.mult).then_inc(sem("mixing_ready"), 1)
                for d in range(2):
                    b = wait_full(dve, ("yoff", c, g, d))
                    e = dec[:, (DC_IF2, DC_IB2)[d] + c, g * HPG:(g + 1) * HPG]
                    o = y if d == 0 else lnt[:, 0, :]
                    tt(o.rearrange("p (h d) -> p h d", h=HPG), ps[b][:, :].rearrange("p (h d) -> p h d", h=HPG), bc(e, HPG, HD), ALU.mult).then_inc(read[b], 1)
                for d in range(2):
                    wait_read(dve, ("yoff", c, g, d))
                n = step(tt(y, y, lnt[:, 0, :], ALU.add))
                after(n)
                b = wait_full(dve, ("ydiag", c, g))
                tt(y, y, ps[b][:, :], ALU.add).then_inc(read[b], 1)
            dve.wait_ge(sem("x_skip"), c + 1)
            wait_read(dve, ("ydiag", c, GROUPS - 1))
            n = step(tt(yv[:, c, :], yv[:, c, :], xtok[:, 2 + c, :], ALU.add))
            after(n)
        for j in range(8):
            wait_read(dve, ("z", j))
            y = yv[:, :, j * BLK:(j + 1) * BLK]
            tt(y, y, zs[j % 2].rearrange("p (t c) -> p t c", t=TT), ALU.mult).then_inc(sem("y_gated"), 1)
        dve.wait_ge(sem("scalar_steps"), 12)
        ts(ss[:, 8:16], ss[:, 0:8], 1.0 / GW, EPS, ALU.mult, ALU.add).then_inc(sem("rms_mean"), 1)
        dve.wait_ge(sem("rms_root"), 1)
        n = step(V.reciprocal(ss[:, 0:8], ss[:, 16:24]))
        after(n)
        for t in range(TT):
            for g in range(GROUPS):
                y = yv[:, t, g * GW:(g + 1) * GW]
                last = ts(y, y, ss[:, 2 * g + t:2 * g + t + 1], None, ALU.mult)
        last.then_inc(sem("y_normed"), 1)

        def layer_norm(l, j, keys):
            dve.wait_ge(sem("ln_rows_in"), 32 * (2 * l + j + 1))
            for t in range(TT):
                for h in range(2):
                    b = wait_full(dve, keys[2 * t + h])
                    tt(lnt[:, h, :], ps[b][:, :], gate[j][:, h * 512:(h + 1) * 512], ALU.mult).then_inc(read[b], 1)
                for h in range(2):
                    wait_read(dve, keys[2 * t + h])
                    x = xres[:, t, h * 512:(h + 1) * 512]
                    n = step(stt(x, x, ALPHA, lnt[:, h, :], ALU.mult, ALU.add))
                    after(n)
                    n = step(V.bn_stats(small[:, t, 6 * h:6 * h + 6], x))
                after(n)
                n = step(V.bn_aggr(small[:, t, 12:14], small[:, t, 0:12]))
            after(n)
            ts(small[:, :, 14], small[:, :, 13], EPS, None, ALU.add).then_inc(sem("ln_variance"), 1)
            dve.wait_ge(sem("ln_root"), 2 * l + j + 1)
            n = step(V.reciprocal(small[:, :, 16], small[:, :, 15]))
            after(n)
            for t in range(TT):
                n = step(ts(xres[:, t, :], xres[:, t, :], small[:, t, 12:13], small[:, t, 16:17], ALU.subtract, ALU.mult))
            for t in range(TT):
                after(n - 1 + t)
                m = step(tt(xres[:, t, :], xres[:, t, :], lnb[:, 0, :], ALU.mult))
            for t in range(TT):
                after(m - 1 + t)
                last = tt(xres[:, t, :], xres[:, t, :], lnb[:, 1, :], ALU.add)
            last.then_inc(sem("layer_norms_done"), 1)

        layer_norm(0, 0, [("mout", j) for j in range(4)])
        phase_end(dve, 1)

        def select(l, t):
            for j in range(4):
                wait_read(dve, ("sc", l, t, j))

            def best(rows_, src, left, val, idx):
                for r in range(rows_):
                    n = step(V.max(val[:, r, 0:8], src[:, r, :]))
                after(n)
                for r in range(rows_):
                    step(V.max_index(idx[:, r, 0:8], val[:, r, 0:8], src[:, r, :]))
                    n = step(V.match_replace(left[:, r, :], val[:, r, 0:8], src[:, r, :], LOWEST))
                after(n)
                for r in range(rows_):
                    n = step(V.max(val[:, r, 8:16], left[:, r, :]))
                after(n)
                for r in range(rows_):
                    n = step(V.max_index(idx[:, r, 8:16], val[:, r, 8:16], left[:, r, :]))
                after(n)

            best(NROW, sc, sc2, topv, topi)
            n = step(V.tensor_copy(topf[:, :, :], topi[:, :, :]))
            c4 = cand[:, :, :].rearrange("p h (a b) -> p h a b", a=TOPK)
            step(tt(c4, topv[:, 0:PH, :].unsqueeze(3).to_broadcast([P, PH, TOPK, TOPK]),
                    topv[:, PH:, :].unsqueeze(2).to_broadcast([P, PH, TOPK, TOPK]), ALU.add))
            after(step.n)
            best(PH, cand, cand2, selv, seli)
            m = step(V.tensor_copy(ksum[:, 0, :], selv[:, :, 0]))
            step(ts(posr[:, 0, :, :], seli[:, :, :], 4, None, ALU.logical_shift_right))
            n = step(ts(posr[:, 1, :, :], seli[:, :, :], 15, None, ALU.bitwise_and))
            after(n)
            n = step(V.tensor_copy(posf[:, :, :], posr[:, :, :, :].rearrange("p a h k -> p a (h k)")))
            tt(selv[:, :, :], selv[:, :, :], bc(ksum[:, 0, :], PH, TOPK), ALU.subtract).then_inc(sem("gate_shifted"), 1)
            after(n)
            pk = pick.rearrange("p (r a) -> p r a", a=TOPK)
            pk4 = pick.rearrange("p (h k a) -> p h k a", h=PH, k=TOPK)
            for j in range(2):
                n = step(tt(pk, cst[:, C_IOTA, 0:TOPK].unsqueeze(1).to_broadcast([P, P, TOPK]), bc(posf[:, j, :], P, TOPK), ALU.is_equal))
                after(n)
                n = step(tt(pk4, pk4, topf[:, j * PH:(j + 1) * PH, :].unsqueeze(2).to_broadcast([P, PH, TOPK, TOPK]), ALU.mult))
                after(n)
                if j == 0 and t:
                    wait_full(dve, ("selT", l, t - 1))
                n = step(V.tensor_reduce(seltok[:, j, :], pk, AX.X, ALU.add))
                after(n)
            dve.wait_ge(sem("gate_exp"), TT * l + t + 1)
            n = step(V.tensor_reduce(ksum[:, 0, :], selv[:, :, :], AX.X, ALU.add))
            after(n)
            n = step(V.reciprocal(ksum[:, 1, :], ksum[:, 0, :]))
            after(n)
            tt(seltok[:, 2, :].rearrange("p (h k) -> p h k", h=PH), selv[:, :, :], bc(ksum[:, 1, :], PH, TOPK), ALU.mult).then_inc(sem("selected"), 1)

        def peer(l):
            modulate(("tT", l), tT, l, 1)
            for j in range(4):
                dve.wait_ge(sem("t_hi"), 4 * l + j + 1)
                s_ = slice(2 * j, 2 * j + 2)
                last = tt(tTlo[:, s_, :], tT[:, s_, :], tThi[:, s_, :].bitcast(F32), ALU.subtract)
            last.then_inc(sem("t_split"), 1)
            for t in range(TT):
                select(l, t)
                if t:
                    for u in range(TT):
                        b = wait_full(dve, ("selT", l, u))
                        V.tensor_copy(selT[:, :, u * P:(u + 1) * P], ps[b][:, 0:3 * P].rearrange("p (j c) -> p j c", j=3)).then_inc(read[b], 1)
            for u in range(TT):
                wait_read(dve, ("selT", l, u))
            phase_end(dve, 2 + 5 * l)
            groups = 2 * TC // OH
            with dve.Fori(0, NTC // 2) as i:
                for n in range(groups):
                    place_free(dve, l, n, i)
                    tt(onea[n % 2][:, :, :], cst[:, C_IOTA, :].unsqueeze(1).to_broadcast([P, OH, NK]),
                       bc(selT[:, 0, bass.ds(i * (2 * TC) + n * OH, OH)], OH, NK), ALU.is_equal)
                    for t in range(OH):
                        tok = i * (2 * TC) + (n * OH + t)
                        last = ts(oneb[n % 2][:, t, :], cst[:, C_IOTA, :], selT[:, 1, bass.ds(tok, 1)], selT[:, 2, bass.ds(tok, 1)],
                                  ALU.is_equal, ALU.mult)
                    last.then_inc(sem("one_hot_rows"), 1)
            V.memset(lnt[:, 0, :], 0.0).then_inc(sem("zeros"), 1)
            phase_end(dve, 3 + 5 * l)
            base = stream_base[l]

            def split_u(m, off, h):
                j = off % 2
                dve.wait_ge(sem("u_hi"), m * 2 + (2 * l * NK + h + 1))
                c = slice(4 * h, 4 * h + 4)
                tt(UTlo[j][:, c, :].rearrange("p a b -> p (a b)"), ps[4 + h][:, :], UThi[j][:, c, :].rearrange("p a b -> p (a b)").bitcast(F32),
                   ALU.subtract).then_inc(read[4 + h], 1)

            def tile_step(m, off, i=None):
                j = off % 2
                slot = off % UV
                half = off // 2 if i is None else i * (ROUND // 2) + off // 2
                if off != NK - 1:
                    split_u(m + 1, off + 1, 0)
                dve.wait_ge(sem("v_hi"), m + (l * NK + 1))
                tt(Vlo[j][:], uvring[slot][:, 1, :], Vhi[j][:].bitcast(F32), ALU.subtract).then_inc(sem("v_split"), 1)
                if off != NK - 1:
                    split_u(m + 1, off + 1, 1)
                dve.wait_ge(read[6 + j], half + (base[6 + j] + 1))
                gj = (off // GI) % 2
                rounds_ = off // (2 * GI) if i is None else i + off // (2 * GI)
                dve.wait_ge(g_loaded[gj], rounds_ * 16 + 16 * (l * (NK // GI // 2) + 1))
                tt(gw[j][:].rearrange("p (c t) -> p c t", c=NTC), gel[j][:].rearrange("p (c t) -> p c t", c=NTC),
                   gt[gj][:, :, (off % GI) * TC:(off % GI + 1) * TC], ALU.mult).then_inc(sem("gated"), 1)
                dve.wait_ge(sem("gated"), m + (l * NK + 1))
                V.tensor_copy(Whi[j][:], gw[j][:]).then_inc(sem("w_hi"), 1)
                dve.wait_ge(sem("w_hi"), m + (l * NK + 1))
                tt(Wlo[j][:], gw[j][:], Whi[j][:].bitcast(F32), ALU.subtract).then_inc(sem("w_split"), 1)

            for h in range(2):
                split_u(0, 0, h)
            tiles(dve, tile_step)
            layer_norm(l, 1, [("peer_out", l, j) for j in range(4)])

        peer(0)
        modulation(1)
        phase_end(dve, 4)
        two_pi = 2 * math.pi
        c1 = 6.28125
        c2 = two_pi - c1
        magic = 1.5 * 2.0 ** 23
        dve.wait_ge(sem("hyena_in"), 176)
        for j in range(3):
            b = wait_full(dve, ("hid", j))
            ts(hid[:, 1, :], ps[b][0:HY_FF, 0:T], hv[:, j:j + 1], hv[:, 3:4], ALU.add, ALU.mult).then_inc(read[b], 1)
            wait_read(dve, ("hid", j))
            n = step(ts(hid[:, 2, :], hid[:, 1, :], 1.0 / two_pi, magic, ALU.mult, ALU.add))
            after(n)
            n = step(ts(hid[:, 2, :], hid[:, 2, :], -magic, None, ALU.add))
            after(n)
            n = step(stt(hid[:, 1, :], hid[:, 2, :], -c1, hid[:, 1, :], ALU.mult, ALU.add))
            after(n)
            n = step(stt(hid[:, 1, :], hid[:, 2, :], -c2, hid[:, 1, :], ALU.mult, ALU.add))
            after(n)
            ts(hid[:, 3, :], hid[:, 1, :], 3.1415925, -3.1415925, ALU.min, ALU.max).then_inc(sem("sine_argument"), 1)
        n = 0
        for t in range(TT):
            dve.wait_ge(sem("lag_decay"), t + 1)
            for o in range(ORDER):
                for h in range(2):
                    if n:
                        dve.wait_ge(sem("filter_sides"), n)
                    for side in range(2):
                        b = wait_full(dve, ("hflt", n, side))
                        tt(hfb[:, side, :], ps[b][:, :], dcy[:, t, h * 512:(h + 1) * 512], ALU.mult).then_inc(read[b], 1)
                    for side in range(2):
                        wait_read(dve, ("hflt", n, side))
                    tt(sd[:, 0, t, o, h * 512:(h + 1) * 512], hfb[:, 0, :], hfb[:, 1, :], ALU.add)
                    tt(sd[:, 1, t, o, h * 512:(h + 1) * 512], hfb[:, 0, :], hfb[:, 1, :], ALU.subtract).then_inc(sem("filter_sides"), 1)
                    n += 1
        for o in range(ORDER):
            for h in range(2):
                n = 2 * o + h
                if n:
                    dve.wait_ge(sem("filter_normed"), n)
                b = wait_full(dve, ("hnorm", n))
                ts(rsn[:], ps[b][:, :], HY_EPS, None, ALU.add).then_inc(read[b], 1)
                dve.wait_ge(sem("norm_root"), n + 1)
                k = step(V.reciprocal(rsn[:], rsn[:]))
                after(k)
                for side in range(2):
                    for t in range(TT):
                        s_ = sd[:, side, t, o, h * 512:(h + 1) * 512]
                        last = tt(s_, s_, rsn[:], ALU.mult)
                last.then_inc(sem("filter_normed"), 1)
        phase_end(dve, 5)
        modulate(("hhT",), hhT, 1, 0)
        for m in range(12):
            wait_read(dve, ("hu", m))
            for c in range(2):
                ct = 2 * m + c
                u, o = hub[m % 2][:, c, :], huT[:, ct, :]

                def tap(j):
                    return vec[:, V_HCW + 24 * j + ct:V_HCW + 24 * j + ct + 1]

                n = step(ts(o, u, tap(1), vec[:, V_HCB + ct:V_HCB + ct + 1], ALU.mult, ALU.add))
                after(n)
                n = step(stt(o[:, 1:T], u[:, 0:T - 1], tap(0), o[:, 1:T], ALU.mult, ALU.add))
                after(n)
                last = stt(o[:, 0:T - 1], u[:, 1:T], tap(2), o[:, 0:T - 1], ALU.mult, ALU.add)
            last.then_inc(sem("hyena_conv"), 1)
        for o in range(ORDER):
            for n in range(4):
                h, fr = n // 2, n % 2
                c = slice(h * 512, (h + 1) * 512)
                if o + n:
                    dve.wait_ge(sem("spectrum_done"), 8 * o + 2 * n)
                b0 = wait_full(dve, ("vs", o, n, 0))
                b1 = wait_full(dve, ("vs", o, n, 1))
                fa, fb, fc = Hs[:, o, fr, c], Hs[:, o, 2 + fr, c], Hs[:, o, 4 if fr == 0 else 1, c]
                step(tt(ytm[:, 0, :], ps[b0][:, :], fa, ALU.mult))
                tt(ytm[:, 2, :], ps[b0][:, :], fb, ALU.mult).then_inc(read[b0], 1)
                k = step(tt(ytm[:, 1, :], ps[b1][:, :], fb, ALU.mult))
                tt(ytm[:, 3, :], ps[b1][:, :], fc, ALU.mult).then_inc(read[b1], 1)
                after(k)
                tt(Yf[:, fr, c], ytm[:, 0, :], ytm[:, 1, :], ALU.subtract).then_inc(sem("spectrum_done"), 1)
                wait_read(dve, ("vs", o, n, 0))
                wait_read(dve, ("vs", o, n, 1))
                tt(Yf[:, 2 + fr, c], ytm[:, 2, :], ytm[:, 3, :], ALU.add).then_inc(sem("spectrum_done"), 1)
            for c2 in range(4):
                if o + c2:
                    dve.wait_ge(sem("order_done"), 8 * o + 2 * c2)
                b = wait_full(dve, ("inv", o, c2))
                for c in range(2):
                    ct = 2 * c2 + c
                    v = huT[:, 16 + ct, :]
                    last = stt(hyt[:, c, :], v, vec[:, V_HB + 8 * o + ct:V_HB + 8 * o + ct + 1], ps[b][:, c * T:(c + 1) * T], ALU.mult, ALU.add)
                    if c == 0:
                        k = step(last)
                last.then_inc(read[b], 1)
                after(k)
                wait_read(dve, ("inv", o, c2))
                for c in range(2):
                    ct = 2 * c2 + c
                    tt(huT[:, 16 + ct, :], hyt[:, c, :], huT[:, 8 * o + ct, :], ALU.mult).then_inc(sem("order_done"), 1)
        layer_norm(1, 0, [("hout", j) for j in range(4)])
        phase_end(dve, 6)
        peer(1)


def dft_tables(np):
    n = 2 * T
    tok = np.arange(T)
    frq = np.arange(T)
    ang = 2 * np.pi * np.outer(tok, frq) / n
    alt = (-1.0) ** tok
    re, im = np.cos(ang), -np.sin(ang)
    fi = im.copy()
    fi[:, 0] = alt
    c0 = re[:, :P].copy()
    c0[:, 0] = alt
    inv_r = 2 * re.T / n
    inv_r[0] = 1.0 / n
    inv_i = 2 * im.T / n
    inv_i[0] = alt / n

    def parts(m):
        return m.reshape(-1, P, m.shape[1]).transpose(1, 0, 2).reshape(P, -1)

    ws = np.full((P, P), 0.5)
    ws[0] = 1.0
    wd = np.full((P, P), 0.5)
    wd[0] = 0.0
    half = np.full((P, P), 0.5)
    return np.ascontiguousarray(np.concatenate(
        [parts(re), parts(fi), parts(im[:, :P]), parts(c0), parts(np.concatenate([inv_r, inv_i])), ws, wd, half], axis=1).astype(np.float32))


def shape_constants(np):
    f32 = np.float32
    i = np.arange(P)
    u, t = i[:, None], i[None, :]
    mats = [u == t, u <= t, u >= t, u < t, u > t, np.ones((P, P)), np.broadcast_to(t, (P, P))]
    tl = np.linspace(0.0, 1.0, T, dtype=f32)
    bands = (HY_EMB - 1) // 2
    ang = (f32(2.0 * math.pi) * np.arange(T, dtype=f32) / f32(T)).astype(f32)
    fb = np.linspace(1e-4, bands - 1, bands, dtype=f32)
    arg = (fb[:, None] * ang[None, :]).astype(f32).astype(np.float64)
    feats = np.concatenate([tl[None, :], np.cos(arg), -np.sin(arg)], axis=0).astype(f32)
    rates = np.abs(np.linspace(math.log(1e-2) / 1.5, math.log(1e-2) / 0.3, D, dtype=f32))
    return {
        "constants": np.ascontiguousarray(np.concatenate([np.asarray(m, f32) for m in mats], axis=1)),
        "hyena_constants": dft_tables(np),
        "filter_features": np.ascontiguousarray(feats),
        "lag_times": np.ascontiguousarray(-tl.reshape(TT, P).T),
        "decay_rates": rates.astype(f32),
    }


INPUTS = ["x", "c", "ctx", "c_ctx", "ada_w", "ada_b", "ln_g", "ln_b", "m_w_in", "m_conv_w", "m_conv_b", "m_a_log",
          "m_dt_bias", "m_d", "m_norm_w", "m_w_out", "h_w_in", "h_conv_w", "h_conv_b", "h_f_w1", "h_f_b1", "h_f_w2",
          "h_f_b2", "h_f_w3", "h_freq", "h_bias", "h_w_out", "p_wq", "p_k1", "p_k2", "p_u", "p_v"]


def kernel(**inputs):
    import numpy as np
    import concourse.bacc as bacc
    from concourse.bass_utils import run_bass_kernel_spmd as run

    nc = bacc.Bacc("TRN2", target_bir_lowering=False, num_devices=1)
    arrays, aps = {}, {}
    given = {n: np.ascontiguousarray(inputs[n]) for n in INPUTS} | shape_constants(np)
    for name, a in given.items():
        arrays[f"in_{name}"] = a
        aps[name] = nc.dram_tensor(f"in_{name}", a.shape, mybir.dt.from_np(a.dtype), kind="ExternalInput").ap()
    out = nc.dram_tensor("out_x", (1, T, D), F32, kind="ExternalOutput").ap()
    build_program(nc, aps, out)
    r = run(nc, [arrays], core_ids=[0])
    return r.results[0]["out_x"]
```

```python
import math
from contextlib import ExitStack

import concourse.bass as bass
from concourse import mybir

F32 = mybir.dt.float32
F32R = mybir.dt.float32r
U32 = mybir.dt.uint32
ACT = mybir.ActivationFunctionType
ALU = mybir.AluOpType
AX = mybir.AxisListType

P = 128
D = 1024
KD = D // P
T = 256
TT = T // P
GRID_W = 64
ROWS = T // GRID_W
DEPTH = 2
ALPHA = (2 * DEPTH) ** 0.25
EPS = 1e-5
INNER = 2 * D
HEADS = 32
HD = 64
GROUPS = 4
HPG = HEADS // GROUPS
GW = HPG * HD
XBC_CT = (INNER + 2 * GROUPS * P) // P
GATES = (2, 5)
UNITS0 = ((0, 1, 2, 3), tuple(range(4, 12)))
UNITS1 = ((0, 1, 2), tuple(range(3, 12)))
ORDER = 2
HY_EPS = 1e-6
HY_FF = 64
HY_EMB = 33
PH = 8
NK = 128
TOPK = 16
NROW = 2 * PH
BLK = 256
RING = 4
UV = 4
TC = 32
NTC = T // TC
OH = 8
OHR = 4
GI = 4
ROUND = 8
NROUND = (NK - ROUND) // ROUND
PEELED = 2
LOWEST = -3.0e38

V_CW, V_CB, V_NW = 0, 216, 240
V_HCW, V_HCB, V_HB, V_C, V_CC = 256, 328, 352, 368, 376
C_ID, C_LE, C_GE, C_LT, C_GT, C_ONE, C_IOTA = range(7)
H_FR, H_FI, H_BZ, H_C0, H_INV, H_WS, H_WD, H_W1 = 0, 512, 1024, 1280, 1536, 2560, 2688, 2816
H_COLS = 2944
(DC_F0, DC_F1, DC_F2, DC_B1, DC_B0, DC_B3, DC_IF2, DC_IF3, DC_IB2, DC_IB3, DC_TF2, DC_TB3) = range(12)


class BankPlan:

    def __init__(self):
        self.count = [0] * 8
        self.where = {}

    def use(self, key, bank, loop=None):
        assert key not in self.where, key
        self.where[key] = (bank, self.count[bank], 0)
        self.count[bank] += 1

    def loop(self, rounds, uses):
        per = [sum(b == bank for _, b in uses) for bank in range(8)]
        seen = [0] * 8
        for key, bank in uses:
            assert key not in self.where, key
            self.where[key] = (bank, self.count[bank] + seen[bank], per[bank])
            seen[bank] += 1
        for bank in range(8):
            self.count[bank] += rounds * per[bank]

    def __call__(self, key, i=0):
        bank, base, per = self.where[key]
        return bank, base + i * per if per else base


class Chain:

    def __init__(self, sem):
        self.sem, self.n, self.i, self.per = sem, 0, None, 0

    def __call__(self, instruction):
        instruction.then_inc(self.sem, 1)
        self.n += 1
        return self.value()

    def value(self):
        return self.n if self.i is None else self.n + self.i * self.per

    def enter(self, i, per):
        self.i, self.per, self.start = i, per, self.n

    def leave(self, rounds):
        assert self.n - self.start == self.per, (self.n - self.start, self.per)
        self.n = self.start + rounds * self.per
        self.i = None


def build_program(nc, A, out):
    ctx = ExitStack()
    with ctx:
        build_in(nc, A, out, ctx)


def build_in(nc, A, out, ctx):
    sems = {}

    def sem(name):
        if name not in sems:
            sems[name] = ctx.enter_context(nc.semaphore(name))
        return sems[name]

    def sb(scope, name, shape, dt=F32):
        return scope.enter_context(nc.sbuf_tensor(name, shape, dt))

    cst = sb(ctx, "constants", [P, 7, P])
    vec = sb(ctx, "channel_vectors", [P, 3 * P])
    xres = sb(ctx, "x_residual", [P, TT, D])
    wring = [sb(ctx, f"weight_block{s}", [P, 2048]) for s in range(RING)]
    lnb = sb(ctx, "ln_gain_bias", [P, 2, D])
    gate = [sb(ctx, f"gate{j}", [P, D]) for j in range(2)]
    s_rep = sb(ctx, "silu_c_repeated", [P, KD, P])
    s_col = sb(ctx, "silu_c_columns", [P, KD, 2])
    brow = sb(ctx, "modulation_bias_rows", [24 * DEPTH, BLK])
    mrow = [sb(ctx, f"modulation_rows{j}", [2, 512]) for j in range(2)]
    ada = [sb(ctx, f"modulation_columns{l}", [P, 4, KD, 2]) for l in range(DEPTH)]
    lnt = sb(ctx, "layer_norm_tmp", [P, 2, 512])
    small = sb(ctx, "layer_norm_small", [P, TT, 24])
    ps = [ctx.enter_context(nc.psum_tensor(f"bank{b}", [P, 512], F32)) for b in range(8)]

    ident = cst[:, C_ID, :]

    with ExitStack() as s:
        hT = sb(s, "mixer_input_T", [P, KD, 2 * T])
        bcT = sb(s, "BC_T", [P, 8, T])
        work = sb(s, "conv_work_or_state2", [P, 4096])
        xtok = sb(s, "x_tokens", [P, 4, INNER])
        btok = sb(s, "B_tokens", [P, 4, GROUPS * P])
        dtb = sb(s, "dt_bias_row", [1, 2 * HEADS])
        aneg = sb(s, "a_log_rows", [P, 2 * HEADS])
        dskip = sb(s, "d_skip_rows", [P, HEADS])
        dt_t = sb(s, "dt", [P, 4, 2 * HEADS])
        a_t = sb(s, "a", [P, 4, 2 * HEADS])
        dec = sb(s, "decays", [P, 12, HEADS])
        wst = sb(s, "state_weights", [P, 6, HEADS])
        aM = [sb(s, f"a_masked{j}", [P, HPG, P]) for j in range(2)]
        EM = [sb(s, f"decay_times_cb{j}", [P, HPG, P]) for j in range(2)]
        xw = [sb(s, f"x_weighted{j}", [P, INNER]) for j in range(2)]
        S1 = sb(s, "state_ctx", [P, 2, INNER])
        ss = sb(s, "rms", [P, 24])
    wdt = EM[0][:, 0:4, :].rearrange("p a b -> p (a b)").rearrange("p (k c) -> p k c", k=KD)
    cbm = btok[:, 0, 0:2 * P].rearrange("p (a b) -> p a b", a=2)
    ctxb = xw[0][:, :].rearrange("p (t d) -> p t d", t=TT)
    dtw = S1[:, 0, 0:1536].rearrange("p (n c) -> p n c", n=6)
    zs = [aM[j][:, 0:4, :].rearrange("p a b -> p (a b)") for j in range(2)]
    ubuf = [work[:, j * 1536:j * 1536 + 512] for j in range(2)]
    cacc = [work[:, j * 1536 + 512:j * 1536 + 1024] for j in range(2)]
    xc = [work[:, j * 1536 + 1024:j * 1536 + 1536] for j in range(2)]
    stg = hT[:, 0, 0:3 * P].rearrange("p (a b) -> p a b", a=3)
    S2 = work[:, :].rearrange("p (a b) -> p a b", a=2)
    yv = xtok[:, 0:2, :]
    uT = hT[:, :, :].rearrange("p a b -> p (a b)").rearrange("p (a b) -> p a b", a=16)

    gate.append(sb(ctx, "gate2", [P, D]))

    with ExitStack() as s:
        uvring = [sb(s, f"expert_rows{j}", [P, 2, D]) for j in range(UV)]
        tThi = sb(s, "t_T_hi", [P, KD, T], F32R)
        tTlo = sb(s, "t_T_lo", [P, KD, T], F32R)
        selT = sb(s, "selected_T", [P, 3, T])
        seltok = sb(s, "selected_tokens", [P, TT, 3, P])
        with ExitStack() as q:
            tT = sb(q, "t_T", [P, KD, T])
            qT = [sb(q, f"q_T{j}", [P, 2, T]) for j in range(2)]
            kraw = sb(q, "keys", [P, NROW, P])
            kT = sb(q, "keys_T", [P, NROW, P])
            sc = [sb(q, f"scores{j}", [P, 4, NK]) for j in range(2)]
            left = sb(q, "scores_left", [P, 4, NK])
            topv = [sb(q, f"top_values{j}", [P, 4, TOPK]) for j in range(2)]
            topi = [sb(q, f"top_indices{j}", [P, 4, TOPK], U32) for j in range(2)]
            topf = [sb(q, f"top_indices_f{j}", [P, 4, TOPK]) for j in range(3)]
            cand = [sb(q, f"candidates{j}", [P, TT, TOPK * TOPK]) for j in range(2)]
            cand_left = sb(q, "candidates_left", [P, TT, TOPK * TOPK])
            selv = sb(q, "selected_scores", [P, TT, PH, TOPK])
            seli = sb(q, "selected_positions", [P, TT, TOPK], U32)
            posr = sb(q, "position_parts", [P, TT, 2, TOPK], U32)
            posf = sb(q, "position_parts_f", [P, TT, 2, TOPK])
            pick = [sb(q, f"position_one_hot{j}", [P, 2 * TT, TOPK, TOPK]) for j in range(2)]
            ksum = sb(q, "gate_sums", [P, 2, TT, PH])
        with ExitStack() as q:
            onea = [sb(q, f"one_hot_first{j}", [P, OH, NK]) for j in range(OHR)]
            oneb = [sb(q, f"one_hot_second{j}", [P, OH, NK]) for j in range(OHR)]
            gch = sb(q, "g_chunk", [P, 2, NK, TC])
        with ExitStack() as q:
            UThi = [sb(q, f"u_T_hi{j}", [P, KD, P], F32R) for j in range(2)]
            UTlo = [sb(q, f"u_T_lo{j}", [P, KD, P], F32R) for j in range(2)]
            Vhi = [sb(q, f"v_hi{j}", [P, D], F32R) for j in range(2)]
            Vlo = [sb(q, f"v_lo{j}", [P, D], F32R) for j in range(2)]
            Whi = [sb(q, f"w_hi{j}", [P, T], F32R) for j in range(2)]
            Wlo = [sb(q, f"w_lo{j}", [P, T], F32R) for j in range(2)]
            gel = [sb(q, f"gelu{j}", [P, T]) for j in range(2)]
            gw = [sb(q, f"gelu_gated{j}", [P, T]) for j in range(2)]
            gt = [sb(q, f"g_tile{j}", [P, NTC, GI * TC]) for j in range(2)]

    with ExitStack() as s:
        hc = sb(s, "hyena_constants", [P, H_COLS])
        Hs = sb(s, "filter_spectra", [P, ORDER, 5, D])
        hv = sb(s, "filter_mlp_vectors", [HY_FF, 8])
        hw1 = sb(s, "filter_w1", [HY_EMB, HY_FF])
        hw2 = sb(s, "filter_w2", [HY_FF, 2, HY_FF])
        zf = sb(s, "filter_features", [HY_EMB, T])
        tcol = sb(s, "lag_times", [P, TT])
        with ExitStack() as q:
            hid = sb(q, "filter_hidden", [HY_FF, 4, T])
            w3 = sb(q, "filter_w3", [HY_FF, 4 * D])
            delta = sb(q, "decay_rates", [P, D])
            dcy = sb(q, "lag_decay", [P, TT, D])
            sd = sb(q, "filter_sum_difference", [P, 2, TT, ORDER, D])
            hfb = sb(q, "filter_two_sides", [P, 2, 512])
            rsn = sb(q, "filter_norm", [P, 512])
        with ExitStack() as q:
            hhT = sb(q, "hyena_input_T", [P, KD, T])
            huT = sb(q, "hyena_u_T", [P, 24, T])
            hub = [sb(q, f"hyena_conv_in{j}", [P, 2, T]) for j in range(2)]
            vtok = sb(q, "hyena_v_tokens", [P, TT, D])
            Yf = sb(q, "spectrum_product", [P, 4, D])
            ytm = sb(q, "spectrum_tmp", [P, 4, 512])
            hyt = sb(q, "hyena_long_conv_out", [P, 2, T])

    gdram = nc.dram_tensor("g_scratch", [P, NTC, NK * TC], F32).ap()

    plan = BankPlan()
    stream_base = {}
    full = [sem(f"bank{b}_full") for b in range(8)]
    read = [sem(f"bank{b}_read") for b in range(8)]

    plan.use("vecs", 0)

    def plan_ada(l, units, banks, tbanks):
        before = None
        for u in (*units, None):
            if u is not None:
                plan.use(("ada", l, u), banks[u % 2])
            if before is not None and before // 2 not in GATES:
                plan.use(("adaT", l, before), tbanks[before % 2])
            before = u

    def plan_peer(l):
        for k in range(4):
            plan.use(("tT", l, k), k)
        for j in range(4):
            plan.use(("kT", l, j), j)
        for r in range(PH):
            plan.use(("q", l, r), 4 + r % 2)
            plan.use(("sc", l, r), r % 2)
        if l == 0:
            plan_ada(1, UNITS1[1], (2, 3), (6, 7))
        for t in range(TT):
            plan.use(("selT", l, t), t)
        plan.loop(NTC // 2, [(("g", l, j), j % 8) for j in range(2 * TC // 4)])
        for j in range(4):
            plan.use(("peer_out", l, j), j)
        stream_base[l] = list(plan.count)
        for b, n in ((4, NK), (5, NK), (6, NK // 2), (7, NK // 2)):
            plan.count[b] += n

    plan_ada(0, UNITS0[0], (1, 2), (3, 3))
    for k in range(KD):
        plan.use(("hT", k), k % 8)
    plan.use("dt", 4)
    for ct in range(XBC_CT):
        plan.use(("xbc", ct), ct % 4)
        if ct < 4 or ct >= 8:
            plan.use(("xT", ct), 6 + ct % 2)
    plan.use("decay", 4)
    for d in range(2):
        for g in range(GROUPS):
            plan.use(("S1", d, g), g)
        for g in range(GROUPS):
            plan.use(("S2", d, g), 4 + g)
    for c in range(2):
        for g in range(GROUPS):
            plan.use(("yoff", c, g, 0), 0)
            plan.use(("yoff", c, g, 1), 1)
            plan.use(("cb", c, g), 2)
            for d in range(2):
                plan.use(("seg", c, g, d, 0), 4 + 2 * d)
                plan.use(("seg", c, g, d, 1), 5 + 2 * d)
            plan_ada(0, (UNITS0[1][4 * c + g],), (4, 4), (5, 5))
            plan.use(("ydiag", c, g), 3)
    for j in range(8):
        plan.use(("z", j), j % 4)
    for ct in range(8):
        plan.use(("uT", ct), 4 + ct % 2)
    for j in range(4):
        plan.use(("mout", j), j)
    plan_ada(1, UNITS1[0], (4, 5), (6, 7))
    plan_peer(0)
    for j in range(3):
        plan.use(("hid", j), 4)
    for n in range(2 * TT * ORDER):
        plan.use(("hflt", n, 0), 5 + n % 2)
        plan.use(("hflt", n, 1), 7 if n % 2 else 4)
    for n in range(2 * ORDER):
        plan.use(("hnorm", n), n % 4)
    for n in range(5 * ORDER * 2):
        plan.use(("hspec", n), 4 + n % 4)
    for k in range(4):
        plan.use(("hhT", k), k)
    for b in range(12):
        plan.use(("hu", b), 4 + b % 4)
    for o in range(ORDER):
        for j in range(4):
            plan.use(("vtok", o, j), j)
        for n in range(4):
            plan.use(("vs", o, n, 0), 4 + 2 * (n % 2))
            plan.use(("vs", o, n, 1), 5 + 2 * (n % 2))
        for c in range(4):
            plan.use(("inv", o, c), c)
    for j in range(4):
        plan.use(("hout", j), 4 + j)
    plan_peer(1)

    blocks = []

    def columns(w, c0):
        return w[:, c0:c0 + BLK].rearrange("(k p) c -> p k c", p=P)

    def rows(w, r0):
        return w[r0:r0 + 2 * P, :].rearrange("(k p) c -> p k c", p=P)

    first = {}
    block_done = []
    w_used = sem("weight_blocks_used")
    used = [0]

    def by_count():
        used[0] += 1
        return w_used, used[0]

    def by_bank(key):
        b, n = plan(key)
        return full[b], n + 1

    def stage(name, aps, done):
        first[name] = len(blocks)
        blocks.extend(aps)
        block_done.extend(done(n) for n in range(len(aps)))

    def stage_ada(l, units):
        for u in units:
            stage(("ada", l, u), [columns(A["ada_w"][l], BLK * (2 * u + s)) for s in range(2)],
                  lambda n: by_bank(("ada", l, u)) if n else by_count())

    stage_ada(0, UNITS0[0])
    stage("xbc", [columns(A["m_w_in"][0], INNER + BLK * b) for b in (8, 9, 10, 11, *range(8))], lambda n: by_bank(("xbc", 2 * n + 1)))
    stage_ada(0, UNITS0[1])
    stage("z", [columns(A["m_w_in"][0], BLK * b) for b in range(8)], lambda n: by_bank(("z", n)))
    stage("mout", [rows(A["m_w_out"][0], 2 * P * b) for b in range(8)], lambda n: by_count() if n < 7 else by_bank(("mout", 3)))
    stage_ada(1, UNITS1[0])
    stage(("wq", 0), [columns(A["p_wq"][0], BLK * b) for b in range(8)], lambda n: by_bank(("q", 0, n)))
    stage_ada(1, UNITS1[1])
    stage("hin", [columns(A["h_w_in"][0], BLK * b) for b in range(12)], lambda n: by_bank(("hu", n)))
    stage("hout", [rows(A["h_w_out"][0], 2 * P * b) for b in range(4)], lambda n: by_count() if n < 3 else by_bank(("hout", 3)))
    stage(("wq", 1), [columns(A["p_wq"][1], BLK * b) for b in range(8)], lambda n: by_bank(("q", 1, n)))
    w_loaded = [sem(f"weight_block{s}_loaded") for s in range(RING)]

    uv_loaded = [sem(f"expert_rows{j}_loaded") for j in range(UV)]
    g_loaded = [sem(f"g_tiles{j}_loaded") for j in range(2)]
    g_stored = [sem(f"g_chunk{j}_stored") for j in range(2)]
    phase = sem("phase_ended")
    PH_PEER0, PH_BUILD0, PH_STREAM0, PH_HYF, PH_HYM, PH_PEER1, PH_BUILD1, PH_STREAM1 = range(1, 9)

    def phase_end(eng, n):
        eng.drain().then_inc(phase, 1)
        eng.wait_ge(phase, 5 * n)

    def wait_read(eng, key, i=0):
        b, n = plan(key, i)
        eng.wait_ge(read[b], n + 1)

    def wait_full(eng, key, i=0):
        b, n = plan(key, i)
        eng.wait_ge(full[b], n + 1)
        return b

    def place_free(eng, l, n, i):
        if n >= OHR:
            b, u = plan(("g", l, 2 * (n - OHR) + 1), i)
            eng.wait_ge(full[b], u + 1)
        else:
            b, u = plan(("g", l, 2 * (n + OHR) + 1), i)
            eng.wait_ge(full[b], u - 1)

    def tiles(eng, step):
        for off in range(PEELED):
            step(off, off)
        with eng.Fori(0, NROUND) as i:
            for off in range(PEELED, PEELED + ROUND):
                step(i * ROUND + off, off, i)
        for off in range(ROUND * NROUND + PEELED, NK):
            step(off, off)

    block = ctx.enter_context(nc.Block())

    @block.sync
    def _(sp):
        sp.dma_start(cst[:], A["constants"].rearrange("p (a b) -> p a b", a=7)).then_inc(sem("constants_in"), 16)
        cw = A["m_conv_w"][0].rearrange("i j (c b) -> (i j c) b", b=P)
        loads = [
            (stg[0:128, 0, :], cw[0:128]), (stg[0:88, 1, :], cw[128:216]),
            (stg[88:112, 1, :], A["m_conv_b"][0].rearrange("(c b) -> c b", b=P)),
            (stg[112:128, 1, :], A["m_norm_w"][0].rearrange("(c b) -> c b", b=P)),
            (stg[0:72, 2, :], A["h_conv_w"][0].rearrange("i (c b) -> (i c) b", b=P)),
            (stg[72:96, 2, :], A["h_conv_b"][0].rearrange("(c b) -> c b", b=P)),
            (stg[96:112, 2, :], A["h_bias"][0].rearrange("i (c b) -> (i c) b", b=P)),
            (stg[112:120, 2, :], A["c"][0].rearrange("(c b) -> c b", b=P)),
            (stg[120:128, 2, :], A["c_ctx"].rearrange("(c b) -> c b", b=P)),
            (brow[:], A["ada_b"].rearrange("l (b c) -> (l b) c", c=BLK)),
        ]
        for dst, src in loads:
            sp.dma_start(dst, src).then_inc(sem("vectors_in"), 16)

        def weights(n0, n1):
            for n in range(n0, n1):
                if n >= RING:
                    sp.wait_ge(*block_done[n - RING])
                k = blocks[n].shape[1]
                dst = wring[n % RING][:, :].rearrange("p (k c) -> p k c", k=k)
                sp.dma_start(dst, blocks[n]).then_inc(w_loaded[n % RING], 16)

        def ln_rows(l, j):
            sp.wait_ge(sem("layer_norms_done"), 2 * l + j)
            sp.dma_start(lnb[:, 0, :], A["ln_g"][l, j].partition_broadcast(P)).then_inc(sem("ln_rows_in"), 16)
            sp.dma_start(lnb[:, 1, :], A["ln_b"][l, j].partition_broadcast(P)).then_inc(sem("ln_rows_in"), 16)

        weights(0, 4)
        sp.dma_start(ctxb, A["ctx"].rearrange("o (t p) d -> p (o t) d", p=P)).then_inc(sem("tokens_in"), 16)
        sp.dma_start(xres[:], A["x"].rearrange("o (t p) d -> p (o t) d", p=P)).then_inc(sem("tokens_in"), 16)
        sp.dma_start(wdt, A["m_w_in"][0][:, INNER + XBC_CT * P:].rearrange("(k p) c -> p k c", p=P)).then_inc(sem("dt_in"), 16)
        sp.dma_start(dtb[:], A["m_dt_bias"].rearrange("o a b -> o (a b)")).then_inc(sem("dt_in"), 16)
        sp.dma_start(aneg[:], A["m_a_log"].rearrange("o a b -> (o a b)").partition_broadcast(P)).then_inc(sem("dt_in"), 16)
        sp.dma_start(dskip[:], A["m_d"].rearrange("o b -> (o b)").partition_broadcast(P)).then_inc(sem("dt_in"), 16)
        ln_rows(0, 0)
        weights(4, first[("wq", 0)] + 4)

        def peer(l):
            u, v = A["p_u"][l], A["p_v"][l]
            sp.dma_start(kraw[:, 0:PH, :], A["p_k1"][l].rearrange("h k d -> k h d")).then_inc(sem("keys_in"), 16)
            sp.dma_start(kraw[:, PH:, :], A["p_k2"][l].rearrange("h k d -> k h d")).then_inc(sem("keys_in"), 16)

            def tile(m, slot):
                sp.dma_start(uvring[slot][:, 0, :], u[bass.ds(m * P, P), :]).then_inc(uv_loaded[slot], 16)
                sp.dma_start(uvring[slot][:, 1, :], v[bass.ds(m * P, P), :]).then_inc(uv_loaded[slot], 16)

            def g_tiles(n, j):
                sp.dma_start(gt[j][:], gdram[:, :, bass.ds(n * GI * TC, GI * TC)]).then_inc(g_loaded[j], 16)

            weights(first[("wq", l)] + 4, first[("wq", l)] + 8)
            for m in range(UV):
                tile(m, m)
            ln_rows(l, 1)
            if l == 0:
                weights(first[("ada", 1, UNITS1[1][0])], first["hin"] + 4)
            phase_end(sp, 2 + 5 * l)
            phase_end(sp, 3 + 5 * l)
            for j in range(2):
                sp.wait_ge(g_stored[j], 16 + 16 * (l + 1) * (NTC // 2))
            g_tiles(0, 0)
            g_tiles(1, 1)

            def refill(m, slot):
                sp.wait_ge(sem("v_split"), m + (l * NK - UV + 1))
                sp.wait_ge(uv_loaded[slot], 32)
                tile(m, slot)

            with sp.Fori(0, NROUND) as i:
                for off in range(UV, UV + ROUND):
                    refill(i * ROUND + off, off % UV)
                    if off % GI == GI - 1:
                        n = (off + 1) // GI
                        sp.wait_ge(sem("gated"), i * ROUND + (l * NK + (n - 1) * GI))
                        sp.wait_ge(g_loaded[n % 2], 16)
                        g_tiles(i * 2 + n, n % 2)
            for m in range(UV + ROUND * NROUND, NK):
                refill(m, m % UV)

        phase_end(sp, 1)
        peer(0)
        phase_end(sp, 4)
        for dst, src in [
            (hc[:], A["hyena_constants"]), (hv[:, 0:1], A["h_f_b1"].rearrange("o f -> f o")),
            (hv[:, 1:2], A["h_f_b2"][0, 0:1, :].rearrange("o f -> f o")),
            (hv[:, 2:3], A["h_f_b2"][0, 1:2, :].rearrange("o f -> f o")), (hv[:, 3:4], A["h_freq"].rearrange("o f -> f o")),
            (hw1[:], A["h_f_w1"][0]), (hw2[:], A["h_f_w2"][0].rearrange("j a b -> a j b")),
            (zf[:], A["filter_features"]), (tcol[:], A["lag_times"]),
            (delta[:], A["decay_rates"].partition_broadcast(P)), (w3[:], A["h_f_w3"][0]),
        ]:
            sp.dma_start(dst, src).then_inc(sem("hyena_in"), 16)
        ln_rows(1, 0)
        phase_end(sp, 5)
        weights(first["hin"] + 4, first[("wq", 1)] + 4)
        phase_end(sp, 6)
        peer(1)
        sp.wait_ge(sem("layer_norms_done"), 4)
        sp.dma_start(out.rearrange("o (t p) d -> p (o t) d", p=P), xres[:]).then_inc(sem("out_stored"), 16)
        sp.wait_ge(sem("out_stored"), 16)

    @block.tensor
    def _(pe):
        mm = nc.tensor.matmul
        order = {b: 0 for b in range(8)}

        def begin(key, i=0):
            b, n = plan(key, i)
            pe.wait_ge(read[b], n)
            return b

        def block_in(n):
            pe.wait_ge(w_loaded[n % RING], 16 * (n // RING + 1))
            return wring[n % RING]

        pe.wait_ge(sem("constants_in"), 16)
        pe.wait_ge(sem("vectors_in"), 160)
        for t in range(3):
            last = nc.tensor.transpose(ps[0][:, t * P:(t + 1) * P], stg[:, t, :], ident)
        last.then_inc(full[0], 1)

        def modulation_products(l, u):
            gates = u // 2 in GATES
            m = P if gates else 2
            if gates:
                pe.wait_ge(sem("silu_c_rows"), 1)
            b = begin(("ada", l, u))
            for s in range(2):
                w = block_in(first[("ada", l, u)] + s)
                row = 24 * l + 2 * u + s
                o = ps[b][0:m, s * BLK:(s + 1) * BLK]
                mm(o, ident[0:24 * DEPTH, row:row + 1].to_broadcast([24 * DEPTH, m]), brow[:], start=True, stop=False)
                for k in range(KD):
                    last = mm(o, s_rep[:, k, :] if gates else s_col[:, k, :], w[:, k * BLK:(k + 1) * BLK],
                              start=False, stop=(k == KD - 1))
                if s == 0:
                    last.then_inc(w_used, 1)
            last.then_inc(full[b], 1)

        def modulation_columns(l, u):
            if u // 2 in GATES:
                return
            wait_read(pe, ("ada", l, u))
            b = begin(("adaT", l, u))
            for c in range(4):
                last = nc.tensor.transpose(ps[b][:, 2 * c:2 * c + 2], mrow[u % 2][:, c * P:(c + 1) * P], ident[0:2, 0:2])
            last.then_inc(full[b], 1)

        def modulation(l, units):
            for n, u in enumerate(units):
                modulation_products(l, u)
                if n:
                    modulation_columns(l, units[n - 1])
            modulation_columns(l, units[-1])

        pe.wait_ge(sem("silu_c"), 1)
        modulation(0, UNITS0[0])
        pe.wait_ge(sem("tokens_in"), 32)
        for k in range(KD):
            b = begin(("hT", k))
            for t in range(4):
                src = ctxb[:, t, k * P:(k + 1) * P] if t < 2 else xres[:, t - 2, k * P:(k + 1) * P]
                last = nc.tensor.transpose(ps[b][:, t * P:(t + 1) * P], src, ident)
            last.then_inc(full[b], 1)
        pe.wait_ge(sem("dt_in"), 64)
        b = begin("dt")
        for k in range(KD):
            wait_read(pe, ("hT", k))
        for t in range(4):
            o = ps[b][:, t * 64:(t + 1) * 64]
            for k in range(KD):
                mm(o, hT[:, k, t * P:(t + 1) * P], wdt[:, k, :], start=(k == 0), stop=False)
            last = mm(o, cst[0:1, C_ONE, :], dtb[0:1, :], start=False, stop=True)
        last.then_inc(full[b], 1)
        for q in range(XBC_CT + 2):
            if q < XBC_CT:
                w = block_in(first["xbc"] + q // 2)
                b = begin(("xbc", q))
                for k in range(KD):
                    last = mm(ps[b][:, :], w[:, k * BLK + (q % 2) * P:k * BLK + (q % 2 + 1) * P], hT[:, k, :],
                              start=(k == 0), stop=(k == KD - 1))
                last.then_inc(full[b], 1)
            r = q - 2
            if 0 <= r < 4 or r >= 8:
                pe.wait_ge(sem("conv_silu"), r + 1)
                b = begin(("xT", r))
                for t in range(4):
                    last = nc.tensor.transpose(ps[b][:, t * P:(t + 1) * P], xc[r % 2][:, t * P:(t + 1) * P], ident)
                last.then_inc(full[b], 1)
        pe.wait_ge(sem("a_ready"), 1)
        b = begin("decay")
        F, B = slice(0, HEADS), slice(HEADS, 2 * HEADS)
        for n, terms in enumerate([
            [(C_GT, 0, F), (C_ONE, 1, F)], [(C_GT, 1, F)], [(C_GT, 2, F)],
            [(C_LT, 1, B), (C_ONE, 0, B)], [(C_LT, 0, B)], [(C_LT, 3, B)],
            [(C_LE, 2, F)], [(C_LE, 3, F)], [(C_GE, 2, B)], [(C_GE, 3, B)], [(C_ONE, 2, F)], [(C_ONE, 3, B)],
        ]):
            for j, (m, c, h) in enumerate(terms):
                last = mm(ps[b][:, n * HEADS:(n + 1) * HEADS], cst[:, m, :], a_t[:, c, h],
                          start=(j == 0), stop=(j == len(terms) - 1))
        last.then_inc(full[b], 1)
        for d in range(2):
            chunks = (0, 1, 2) if d == 0 else (1, 0, 3)
            for n, c in enumerate(chunks):
                j = 3 * d + n
                pe.wait_ge(sem("x_weighted"), j + 1)
                for g in range(GROUPS):
                    if n == 0:
                        b = begin(("S1", d, g))
                    elif n == 2:
                        b = begin(("S2", d, g))
                    else:
                        b = plan(("S1", d, g))[0]
                    last = mm(ps[b][:, :], btok[:, c, g * P:(g + 1) * P], xw[j % 2][:, g * GW:(g + 1) * GW],
                              start=(n != 1), stop=(n != 0))
                    if n:
                        last.then_inc(full[b], 1)
                    elif g == GROUPS - 1:
                        last.then_inc(sem("x_weighted_first_used"), 1)
        for c in range(2):
            for g in range(GROUPS):
                ct_ = bcT[:, 4 + g, c * P:(c + 1) * P]
                for d in range(2):
                    b = begin(("yoff", c, g, d))
                    which, states = ("S1", S1) if c == d else ("S2", S2)
                    wait_read(pe, (which, d, g))
                    st = states[:, d, g * GW:(g + 1) * GW]
                    mm(ps[b][:, :], ct_, st, start=True, stop=True).then_inc(full[b], 1)
                b = begin(("cb", c, g))
                mm(ps[b][:, 0:P], bcT[:, g, c * P:(c + 1) * P], ct_, start=True, stop=True).then_inc(full[b], 1)
                for d in range(2):
                    pe.wait_ge(sem("a_masked"), 2 * (4 * c + g) + d + 1)
                    for h in range(HPG):
                        if h % 4 == 0:
                            b = begin(("seg", c, g, d, h // 4))
                        last = mm(ps[b][:, (h % 4) * P:(h % 4 + 1) * P], aM[d][:, h, :], cst[:, (C_LE, C_GE)[d], :],
                                  start=True, stop=True)
                        if h % 4 == 3:
                            last.then_inc(full[b], 1)
                modulation_products(0, UNITS0[1][4 * c + g])
                pe.wait_ge(sem("x_dt"), 2 * (c + 1))
                pe.wait_ge(sem("mixing_ready"), 2 * (4 * c + g) + 2)
                b = begin(("ydiag", c, g))
                for h in range(HPG):
                    for d in range(2):
                        hh = g * HPG + h
                        last = mm(ps[b][:, h * HD:(h + 1) * HD], EM[d][:, h, :], xw[d][:, hh * HD:(hh + 1) * HD],
                                  start=(d == 0), stop=(d == 1))
                last.then_inc(full[b], 1)
                modulation_columns(0, UNITS0[1][4 * c + g])
        for j in range(8):
            w = block_in(first["z"] + j)
            b = begin(("z", j))
            for t in range(TT):
                for k in range(KD):
                    last = mm(ps[b][:, t * BLK:(t + 1) * BLK], hT[:, k, T + t * P:T + (t + 1) * P], w[:, k * BLK:(k + 1) * BLK],
                              start=(k == 0), stop=(k == KD - 1))
            last.then_inc(full[b], 1)
        pe.wait_ge(sem("y_normed"), 1)
        for j in range(8):
            b = begin(("uT", j))
            for c in range(2):
                for t in range(TT):
                    last = nc.tensor.transpose(ps[b][:, (2 * c + t) * P:(2 * c + t + 1) * P],
                                               yv[:, t, (2 * j + c) * P:(2 * j + c + 1) * P], ident)
            last.then_inc(full[b], 1)

        def project(name, keys, lhs, kts, ready):
            for k in range(kts):
                ready(k)
                w = block_in(first[name] + k // 2)
                for t in range(TT):
                    for h in range(2):
                        b = begin(keys[2 * t + h]) if k == 0 else plan(keys[2 * t + h])[0]
                        last = mm(ps[b][:, :], lhs(k, t), w[:, (k % 2) * D + h * 512:(k % 2) * D + (h + 1) * 512],
                                  start=(k == 0), stop=(k == kts - 1))
                        if k == kts - 1:
                            last.then_inc(full[b], 1)
                if k % 2 and k < kts - 1:
                    last.then_inc(w_used, 1)

        project("mout", [("mout", j) for j in range(4)], lambda k, t: uT[:, k, t * P:(t + 1) * P], 16,
                lambda k: wait_read(pe, ("uT", k // 2)))
        modulation(1, UNITS1[0])
        phase_end(pe, 1)

        def peer(l):
            pe.wait_ge(sem("layer_norms_done"), 2 * l + 1)
            for j in range(4):
                b = begin(("tT", l, j))
                for c in range(2):
                    for t in range(TT):
                        last = nc.tensor.transpose(ps[b][:, (2 * c + t) * P:(2 * c + t + 1) * P],
                                                   xres[:, t, (2 * j + c) * P:(2 * j + c + 1) * P], ident)
                last.then_inc(full[b], 1)
            for k in range(4):
                wait_read(pe, ("tT", l, k))
            pe.wait_ge(sem("keys_in"), 32 * (l + 1))
            for j in range(4):
                b = begin(("kT", l, j))
                for r in range(4):
                    last = nc.tensor.transpose(ps[b][:, r * P:(r + 1) * P], kraw[:, 4 * j + r, :], ident)
                last.then_inc(full[b], 1)

            def queries(r):
                w = block_in(first[("wq", l)] + r)
                b = begin(("q", l, r))
                for c in range(2):
                    for k in range(KD):
                        last = mm(ps[b][:, c * T:(c + 1) * T], w[:, k * BLK + c * P:k * BLK + (c + 1) * P], tT[:, k, :],
                                  start=(k == 0), stop=(k == KD - 1))
                last.then_inc(full[b], 1)

            def scores(r):
                wait_read(pe, ("q", l, r))
                b = begin(("sc", l, r))
                for t in range(TT):
                    for a in range(2):
                        last = mm(ps[b][:, (2 * t + a) * P:(2 * t + a + 1) * P], qT[r % 2][:, a, t * P:(t + 1) * P], kT[:, PH * a + r, :],
                                  start=True, stop=True)
                last.then_inc(full[b], 1)

            queries(0)
            for j in range(4):
                wait_read(pe, ("kT", l, j))
            for r in range(PH):
                if r + 1 < PH:
                    queries(r + 1)
                scores(r)
            if l == 0:
                modulation(1, UNITS1[1])
            pe.wait_ge(sem("selected"), l + 1)
            for t in range(TT):
                b = begin(("selT", l, t))
                for j in range(3):
                    last = nc.tensor.transpose(ps[b][:, j * P:(j + 1) * P], seltok[:, t, j, :], ident)
                last.then_inc(full[b], 1)
            phase_end(pe, 2 + 5 * l)
            groups = 2 * TC // OH
            with pe.Fori(0, NTC // 2) as i:
                for n in range(groups):
                    pe.wait_ge(sem("one_hot_first"), i * groups + (l * T // OH + n + 1))
                    pe.wait_ge(sem("one_hot_gated"), i * groups + (l * T // OH + n + 1))
                    for t in range(OH):
                        if t % 4 == 0:
                            b = begin(("g", l, 2 * n + t // 4), i)
                        last = mm(ps[b][:, (t % 4) * P:(t % 4 + 1) * P], oneb[n % OHR][:, t, :], onea[n % OHR][:, t, :],
                                  start=True, stop=True)
                        if t % 4 == 3:
                            last.then_inc(full[b], 1)
            phase_end(pe, 3 + 5 * l)
            base = stream_base[l]
            pe.wait_ge(sem("zeros"), l + 1)
            for j in range(4):
                b = begin(("peer_out", l, j))
                mm(ps[b][:, :], ident, lnt[:, 0, :], start=True, stop=False, skip_group_check=True)

            def transpose_u(m, off, h):
                slot = off % UV
                pe.wait_ge(read[4 + h], m + base[4 + h])
                if h == 0:
                    pe.wait_ge(uv_loaded[slot], (m - slot) * 8 + 32 * (l * (NK // UV) + 1))
                for k in range(4):
                    last = nc.tensor.transpose(ps[4 + h][:, k * P:(k + 1) * P], uvring[slot][:, 0, (4 * h + k) * P:(4 * h + k + 1) * P], ident)
                last.then_inc(full[4 + h], 1)

            def combine(m, off):
                j = off % 2
                pe.wait_ge(sem("w_split"), m + (l * NK + 1))
                pe.wait_ge(sem("v_split"), m + (l * NK + 1))
                final = off == NK - 1
                for t in range(TT):
                    c = slice(t * P, (t + 1) * P)
                    for lhs, rhs in ((Whi, Vhi), (Whi, Vlo), (Wlo, Vhi)):
                        for h in range(2):
                            last = mm(ps[2 * t + h][:, :], lhs[j][:, c], rhs[j][:, h * 512:(h + 1) * 512], start=False,
                                      stop=final and lhs is Wlo, skip_group_check=True)
                            if final and lhs is Wlo:
                                last.then_inc(full[2 * t + h], 1)
                if not final:
                    last.then_inc(sem("combined"), 1)

            def step(m, off, i=None):
                if off != NK - 1:
                    transpose_u(m + 1, off + 1, 0)
                j = off % 2
                half_m = (off // 2) if i is None else i * (ROUND // 2) + off // 2
                pe.wait_ge(read[6 + j], half_m + base[6 + j])
                for h in range(2):
                    pe.wait_ge(read[4 + h], m + (base[4 + h] + 1))
                if off == 0:
                    pe.wait_ge(sem("t_split"), l + 1)
                n = 0
                for k in range(KD):
                    for lhs, rhs in ((UThi, tThi), (UThi, tTlo), (UTlo, tThi)):
                        last = mm(ps[6 + j][:, 0:T], lhs[j][:, k, :], rhs[:, k, :], start=(n == 0), stop=(n == 3 * KD - 1))
                        n += 1
                last.then_inc(full[6 + j], 1)
                if off != NK - 1:
                    transpose_u(m + 1, off + 1, 1)
                if off != 0:
                    combine(m - 1, off - 1)

            for h in range(2):
                transpose_u(0, 0, h)
            tiles(pe, step)
            combine(NK - 1, NK - 1)

        peer(0)
        phase_end(pe, 4)
        pe.wait_ge(sem("hyena_in"), 176)
        for j in range(3):
            b = begin(("hid", j))
            if j == 0:
                last = mm(ps[b][0:HY_FF, 0:T], hw1[:], zf[:], start=True, stop=True)
            else:
                pe.wait_ge(sem("sine"), j)
                last = mm(ps[b][0:HY_FF, 0:T], hw2[:, j - 1, :], hid[:, 0, :], start=True, stop=True)
            last.then_inc(full[b], 1)
        pe.wait_ge(sem("sine"), 3)
        n = 0
        for t in range(TT):
            for o in range(ORDER):
                for h in range(2):
                    for side in range(2):
                        b = begin(("hflt", n, side))
                        c = o * 2 * D + side * D + h * 512
                        mm(ps[b][:, :], hid[:, 0, t * P:(t + 1) * P], w3[:, c:c + 512], start=True, stop=True).then_inc(full[b], 1)
                    n += 1
        for o in range(ORDER):
            for h in range(2):
                n = 2 * o + h
                pe.wait_ge(sem("filter_squares"), n + 1)
                b = begin(("hnorm", n))
                for j, w in enumerate((H_WS, H_W1, H_WD, H_W1)):
                    last = mm(ps[b][:, :], hc[:, w:w + P], dcy[:, j // 2, (j % 2) * 512:(j % 2 + 1) * 512],
                              start=(j == 0), stop=(j == 3))
                last.then_inc(full[b], 1)
        n = 0
        for o in range(ORDER):
            for h in range(2):
                pe.wait_ge(sem("filter_normed"), 2 * o + h + 1)
                for tile, (col, step_, side) in enumerate(((H_FR, 256, 0), (H_FR + P, 256, 0), (H_BZ, P, 1), (H_FI + P, 256, 1), (H_C0, P, 0))):
                    b = begin(("hspec", n))
                    for t in range(TT):
                        last = mm(ps[b][:, :], hc[:, col + t * step_:col + t * step_ + P], sd[:, side, t, o, h * 512:(h + 1) * 512],
                                  start=(t == 0), stop=(t == 1))
                    last.then_inc(full[b], 1)
                    n += 1
        phase_end(pe, 5)
        for j in range(4):
            b = begin(("hhT", j))
            for c in range(2):
                for t in range(TT):
                    last = nc.tensor.transpose(ps[b][:, (2 * c + t) * P:(2 * c + t + 1) * P],
                                               xres[:, t, (2 * j + c) * P:(2 * j + c + 1) * P], ident)
            last.then_inc(full[b], 1)
        for j in range(4):
            wait_read(pe, ("hhT", j))
        for n in range(12):
            w = block_in(first["hin"] + n)
            b = begin(("hu", n))
            for c in range(2):
                for k in range(KD):
                    last = mm(ps[b][:, c * T:(c + 1) * T], w[:, k * BLK + c * P:k * BLK + (c + 1) * P], hhT[:, k, :],
                              start=(k == 0), stop=(k == KD - 1))
            last.then_inc(full[b], 1)
        for o in range(ORDER):
            for j in range(4):
                if o == 0:
                    pe.wait_ge(sem("hyena_conv"), 9 + j)
                else:
                    pe.wait_ge(sem("order_done"), 2 * (j + 1))
                b = begin(("vtok", o, j))
                for t in range(TT):
                    for c in range(2):
                        last = nc.tensor.transpose(ps[b][:, (2 * t + c) * P:(2 * t + c + 1) * P],
                                                   huT[:, 16 + 2 * j + c, t * P:(t + 1) * P], ident)
                last.then_inc(full[b], 1)
            for j in range(4):
                wait_read(pe, ("vtok", o, j))
            for n in range(4):
                h, f = n // 2, n % 2
                for part, col in enumerate((H_FR, H_FI)):
                    b = begin(("vs", o, n, part))
                    for t in range(TT):
                        last = mm(ps[b][:, :], hc[:, col + t * 256 + f * P:col + t * 256 + (f + 1) * P], vtok[:, t, h * 512:(h + 1) * 512],
                                  start=(t == 0), stop=(t == 1))
                    last.then_inc(full[b], 1)
            pe.wait_ge(sem("spectrum_done"), 8 * (o + 1))
            for c2 in range(4):
                b = begin(("inv", o, c2))
                for c in range(2):
                    for k in range(4):
                        last = mm(ps[b][:, c * T:(c + 1) * T], Yf[:, k, (2 * c2 + c) * P:(2 * c2 + c + 1) * P],
                                  hc[:, H_INV + k * T:H_INV + (k + 1) * T], start=(k == 0), stop=(k == 3))
                last.then_inc(full[b], 1)
        project("hout", [("hout", j) for j in range(4)], lambda k, t: huT[:, 16 + k, t * P:(t + 1) * P], 8,
                lambda k: pe.wait_ge(sem("order_done"), 8 + k + 1))
        phase_end(pe, 6)
        peer(1)

    @block.gpsimd
    def _(pool):
        tt = nc.gpsimd.tensor_tensor
        pool.wait_ge(sem("a_ready"), 1)
        for c in range(2):
            for g in range(GROUPS):
                for d in range(2):
                    if c + g:
                        wait_full(pool, ("seg", c - (g == 0), (g - 1) % GROUPS, d, 1))
                    a = a_t[:, 2 + c, d * HEADS + g * HPG:d * HEADS + (g + 1) * HPG]
                    tt(aM[d][:, :, :], a.unsqueeze(2).to_broadcast([P, HPG, P]),
                       cst[:, (C_GT, C_LT)[d], :].unsqueeze(1).to_broadcast([P, HPG, P]), ALU.mult).then_inc(sem("a_masked"), 1)
            pool.wait_ge(sem("x_dt"), 2 * (c + 1))
            x3 = xtok[:, 2 + c, :].rearrange("p (h d) -> p h d", h=HEADS)
            tt(x3, x3, dskip[:].unsqueeze(2).to_broadcast([P, HEADS, HD]), ALU.mult).then_inc(sem("x_skip"), 1)
        phase_end(pool, 1)

        def peer(l):
            def sums(r):
                pool.wait_ge(sem("keys_selected"), PH * l + r + 1)
                if r >= 2:
                    pool.wait_ge(sem("pairs_selected"), PH * l + r - 1)
                v = topv[r % 2][:, :, :].rearrange("p (t a) k -> p t a k", a=2)
                shape = [P, TOPK, TOPK]
                for t in range(TT):
                    last = tt(cand[r % 2][:, t, :].rearrange("p (a b) -> p a b", a=TOPK), v[:, t, 0, :].unsqueeze(2).to_broadcast(shape),
                              v[:, t, 1, :].unsqueeze(1).to_broadcast(shape), ALU.add)
                last.then_inc(sem("pair_sums"), 1)

            def weigh(r):
                pool.wait_ge(sem("pairs_selected"), PH * l + r + 1)
                for n in range(2 * TT):
                    p = pick[r % 2][:, n, :, :]
                    last = tt(p, p, topf[r % 3][:, n, :].unsqueeze(1).to_broadcast([P, TOPK, TOPK]), ALU.mult)
                last.then_inc(sem("positions_weighed"), 1)

            for r in range(PH + 1):
                if r < PH:
                    sums(r)
                if r >= 1:
                    weigh(r - 1)
            phase_end(pool, 2 + 5 * l)
            groups = 2 * TC // OH
            with pool.Fori(0, NTC // 2) as i:
                for n in range(groups):
                    pool.wait_ge(sem("one_hot_second"), i * groups + (l * T // OH + n + 1))
                    tt(oneb[n % OHR][:, :, :], oneb[n % OHR][:, :, :],
                       selT[:, 2, bass.ds(i * (2 * TC) + n * OH, OH)].unsqueeze(2).to_broadcast([P, OH, NK]),
                       ALU.mult).then_inc(sem("one_hot_gated"), 1)
            phase_end(pool, 3 + 5 * l)

        peer(0)
        phase_end(pool, 4)
        phase_end(pool, 5)
        phase_end(pool, 6)
        peer(1)

    @block.scalar
    def _(act):
        step = Chain(sem("scalar_steps"))
        f = nc.scalar.activation

        def copy_out(key, out_, in_=None, func=ACT.Copy, **kw):
            b = wait_full(act, key)
            f(out_, ps[b][:, :] if in_ is None else in_(ps[b]), func, **kw).then_inc(read[b], 1)

        wait_read(act, "vecs")
        f(s_col[:, :, :], vec[:, V_C:V_C + 2 * KD].rearrange("p (j k) -> p k j", j=2), ACT.Silu).then_inc(sem("silu_c"), 1)

        def copy_modulation(l, u):
            part = u // 2
            if part in GATES:
                g = 0 if part == GATES[0] else 1 + l
                copy_out(("ada", l, u), gate[g][:, (u % 2) * 512:(u % 2 + 1) * 512])
            else:
                copy_out(("ada", l, u), mrow[u % 2][:, :], lambda b: b[0:2, :], bias=1.0 if part in (1, 4) else 0.0)

        def copy_modulation_columns(l, u):
            part, k = u // 2, 4 * (u % 2)
            if part not in GATES:
                copy_out(("adaT", l, u), ada[l][:, (0, 1, None, 2, 3)[part], k:k + 4, :], lambda b: b[:, 0:8].rearrange("p (k j) -> p k j", j=2))

        def modulation(l, units):
            for n, u in enumerate(units):
                copy_modulation(l, u)
                if n:
                    copy_modulation_columns(l, units[n - 1])
            copy_modulation_columns(l, units[-1])

        modulation(0, UNITS0[0])
        act.wait_ge(sem("dt_in"), 64)
        n = step(f(aneg[:], aneg[:], ACT.Exp))
        wait_read(act, "dt")
        n = step(f(dtw[:, 1, :], dtw[:, 0, :], ACT.Abs))
        act.wait_ge(step.sem, n)
        n = step(f(dtw[:, 1, :], dtw[:, 1, :], ACT.Exp, scale=-1.0))
        act.wait_ge(sem("dt_plus_one"), 1)
        n = step(f(dtw[:, 3, :], dtw[:, 2, :], ACT.Ln))
        DT_EXP, DT_LOG = n - 1, n
        assert (DT_EXP, DT_LOG) == (3, 4)
        for q in range(XBC_CT + 2):
            if q < XBC_CT:
                if q >= 2:
                    act.wait_ge(sem("conv_done"), q - 1)
                copy_out(("xbc", q), ubuf[q % 2])
            r = q - 1
            if 0 <= r < XBC_CT:
                act.wait_ge(sem("conv_done"), r + 1)
                if r >= 2 and (r - 2 < 4 or r - 2 >= 8):
                    wait_full(act, ("xT", r - 2))
                if r < 4:
                    f(bcT[:, r, :], cacc[r % 2][:, T:2 * T], ACT.Silu)
                if r < 4 or r >= 8:
                    f(xc[r % 2], cacc[r % 2], ACT.Silu).then_inc(sem("conv_silu"), 1)
                else:
                    f(bcT[:, r, :], cacc[r % 2][:, T:2 * T], ACT.Silu).then_inc(sem("conv_silu"), 1)
            r = q - 2
            if 0 <= r < 4:
                copy_out(("xT", r), btok[:, :, r * P:(r + 1) * P], lambda b: b[:, :].rearrange("p (t c) -> p t c", t=4))
            elif r >= 8:
                copy_out(("xT", r), xtok[:, :, (r - 8) * P:(r - 7) * P], lambda b: b[:, :].rearrange("p (t c) -> p t c", t=4))
        copy_out("decay", dec[:, :, :].rearrange("p a b -> p (a b)"), lambda b: b[:, 0:12 * HEADS], ACT.Exp)
        for d in range(2):
            for g in range(GROUPS):
                copy_out(("S1", d, g), S1[:, d, g * GW:(g + 1) * GW])
        for c in range(2):
            for g in range(GROUPS):
                for d in range(2):
                    if c + g:
                        wait_full(act, ("ydiag", c - (g == 0), (g - 1) % GROUPS))
                    for h in range(2):
                        copy_out(("seg", c, g, d, h), EM[d][:, 4 * h:4 * h + 4, :].rearrange("p a b -> p (a b)"), None, ACT.Exp)
                modulation(0, (UNITS0[1][4 * c + g],))
        for j in range(8):
            if j >= 2:
                act.wait_ge(sem("y_gated"), j - 1)
            copy_out(("z", j), zs[j % 2], None, ACT.Silu)
            if j % 2:
                act.wait_ge(sem("y_gated"), j + 1)
                for t in range(TT):
                    n = step(f(lnt[:, t, :], yv[:, t, (j // 2) * GW:(j // 2 + 1) * GW], ACT.Square,
                               accum_out=ss[:, (j // 2) * 2 + t:(j // 2) * 2 + t + 1]))
                    act.wait_ge(step.sem, n)
        assert n == DT_LOG + 8
        act.wait_ge(sem("rms_mean"), 1)
        f(ss[:, 16:24], ss[:, 8:16], ACT.Sqrt).then_inc(sem("rms_root"), 1)
        for j in range(8):
            b = wait_full(act, ("uT", j))
            for c in range(2):
                last = f(uT[:, 2 * j + c, :], ps[b][:, c * T:(c + 1) * T], ACT.Identity, scale=vec[:, V_NW + 2 * j + c:V_NW + 2 * j + c + 1])
            last.then_inc(read[b], 1)

        def layer_norm(l, j):
            act.wait_ge(sem("ln_variance"), 2 * l + j + 1)
            f(small[:, :, 15], small[:, :, 14], ACT.Sqrt).then_inc(sem("ln_root"), 1)

        modulation(1, UNITS1[0])
        layer_norm(0, 0)
        phase_end(act, 1)

        def peer(l):
            for j in range(4):
                wait_read(act, ("tT", l, j))
                f(tThi[:, 2 * j:2 * j + 2, :], tT[:, 2 * j:2 * j + 2, :], ACT.Copy).then_inc(sem("t_hi"), 1)
            for j in range(4):
                copy_out(("kT", l, j), kT[:, 4 * j:4 * j + 4, :].rearrange("p a b -> p (a b)"))

            def copy_queries(r):
                if r >= 2:
                    wait_full(act, ("sc", l, r - 2))
                copy_out(("q", l, r), qT[r % 2][:, :, :].rearrange("p a t -> p (a t)"))

            copy_queries(0)
            for r in range(PH):
                if r + 1 < PH:
                    copy_queries(r + 1)
                if r >= 2:
                    act.wait_ge(sem("keys_selected"), PH * l + r - 1)
                copy_out(("sc", l, r), sc[r % 2][:, :, :].rearrange("p a b -> p (a b)"))
            if l == 0:
                modulation(1, UNITS1[1])
            act.wait_ge(sem("gate_shifted"), l + 1)
            f(selv[:], selv[:], ACT.Exp).then_inc(sem("gate_exp"), 1)
            if l == 0:
                for c in range(2):
                    act.drain().then_inc(g_stored[c], 16)
            phase_end(act, 2 + 5 * l)
            with act.Fori(0, NTC // 2) as i:
                for c in range(2):
                    act.wait_ge(g_stored[c], i * 16 + (16 + 16 * l * (NTC // 2)))
                    for n in range(TC // 4):
                        key = ("g", l, c * (TC // 4) + n)
                        b, u = plan(key, i)
                        act.wait_ge(full[b], u + 1)
                        f(gch[:, c, :, 4 * n:4 * n + 4].rearrange("p i t -> p t i"), ps[b][:, :].rearrange("p (t i) -> p t i", t=4),
                          ACT.Copy).then_inc(read[b], 1)
                    for n in range(TC // 4):
                        wait_read(act, ("g", l, c * (TC // 4) + n), i)
                    act.dma_start(gdram[:, bass.ds(i * 2 + c, 1), :].rearrange("p o c -> p (o c)"),
                                  gch[:, c, :, :].rearrange("p i t -> p (i t)")).then_inc(g_stored[c], 16)
            for c in range(2):
                act.wait_ge(g_stored[c], 16 + 16 * (l + 1) * (NTC // 2))
            phase_end(act, 3 + 5 * l)
            base = stream_base[l]

            def split_u(m, off, h):
                j = off % 2
                act.wait_ge(full[4 + h], m + (base[4 + h] + 1))
                if off >= 2 and h == 0:
                    act.wait_ge(full[6 + j], half(m, off) + base[6 + j])
                f(UThi[j][:, 4 * h:4 * h + 4, :].rearrange("p a b -> p (a b)"), ps[4 + h][:, :], ACT.Copy).then_inc(sem("u_hi"), 1)

            loop = [None]

            def half(m, off):
                return off // 2 if loop[0] is None else loop[0] * (ROUND // 2) + off // 2

            def tile_step(m, off, i=None):
                loop[0] = i
                j = off % 2
                slot = off % UV
                last_tile = off == NK - 1
                if not last_tile:
                    split_u(m + 1, off + 1, 0)
                act.wait_ge(uv_loaded[slot], (m - slot) * 8 + 32 * (l * (NK // UV) + 1))
                if off >= 2:
                    act.wait_ge(sem("combined"), m + (l * (NK - 1) - 1))
                f(Vhi[j][:], uvring[slot][:, 1, :], ACT.Copy).then_inc(sem("v_hi"), 1)
                if not last_tile:
                    split_u(m + 1, off + 1, 1)
                act.wait_ge(full[6 + j], half(m, off) + (base[6 + j] + 1))
                if off >= 2:
                    act.wait_ge(sem("gated"), m + (l * NK - 1))
                f(gel[j][:], ps[6 + j][:, 0:T], ACT.Gelu).then_inc(read[6 + j], 1)

            for h in range(2):
                split_u(0, 0, h)
            tiles(act, tile_step)
            layer_norm(l, 1)

        peer(0)
        phase_end(act, 4)
        for j in range(3):
            act.wait_ge(sem("sine_argument"), j + 1)
            f(hid[:, 0, :], hid[:, 3, :], ACT.Sin).then_inc(sem("sine"), 1)
        act.wait_ge(sem("hyena_in"), 176)
        for t in range(TT):
            f(dcy[:, t, :], delta[:], ACT.Exp, scale=tcol[:, t:t + 1]).then_inc(sem("lag_decay"), 1)
        for o in range(ORDER):
            for h in range(2):
                n = 2 * o + h
                if n == 0:
                    act.wait_ge(sem("filter_sides"), 2 * TT * ORDER)
                else:
                    wait_full(act, ("hnorm", n - 1))
                for side in range(2):
                    for t in range(TT):
                        last = f(dcy[:, side, t * 512:(t + 1) * 512], sd[:, side, t, o, h * 512:(h + 1) * 512], ACT.Square)
                last.then_inc(sem("filter_squares"), 1)
                wait_read(act, ("hnorm", n))
                f(rsn[:], rsn[:], ACT.Sqrt).then_inc(sem("norm_root"), 1)
        n = 0
        for o in range(ORDER):
            for h in range(2):
                for tile in range(5):
                    copy_out(("hspec", n), Hs[:, o, tile, h * 512:(h + 1) * 512])
                    n += 1
        phase_end(act, 5)
        for n in range(12):
            if n >= 2:
                act.wait_ge(sem("hyena_conv"), n - 1)
            copy_out(("hu", n), hub[n % 2][:, :, :].rearrange("p a b -> p (a b)"))
        for o in range(ORDER):
            for j in range(4):
                copy_out(("vtok", o, j), vtok[:, :, j * 2 * P:(j + 1) * 2 * P], lambda b: b[:, :].rearrange("p (t c) -> p t c", t=TT))
        layer_norm(1, 0)
        phase_end(act, 6)
        peer(1)

    @block.vector
    def _(dve):
        step = Chain(sem("vector_steps"))
        V = nc.vector
        tt, ts, stt = V.tensor_tensor, V.tensor_scalar, V.scalar_tensor_tensor

        def after(n):
            dve.wait_ge(step.sem, n)

        def bc(ap, n, width):
            return ap.unsqueeze(2).to_broadcast([P, n, width])

        dve.wait_ge(full[0], 1)
        V.tensor_copy(vec[:, 0:3 * P], ps[0][:, 0:3 * P]).then_inc(read[0], 1)
        dve.wait_ge(sem("silu_c"), 1)
        V.tensor_copy(s_rep[:, :, :], s_col[:, :, 0:1].to_broadcast([P, KD, P])).then_inc(sem("silu_c_rows"), 1)

        def modulate(key, dsts, l, pair):
            for u in range(4):
                wait_read(dve, ("adaT", l, 6 * pair + u))
            for j in range(4):
                b = wait_full(dve, key + (j,))
                for c in range(2):
                    k = 2 * j + c
                    last = ts(dsts[:, k, :], ps[b][:, c * T:(c + 1) * T], ada[l][:, 2 * pair + 1, k, 0:1], ada[l][:, 2 * pair, k, 0:1], ALU.mult, ALU.add)
                last.then_inc(read[b], 1)

        for u in range(4):
            wait_read(dve, ("adaT", 0, u))
        for k in range(KD):
            b = wait_full(dve, ("hT", k))
            for half_, j in ((0, 1), (1, 0)):
                last = ts(hT[:, k, half_ * T:(half_ + 1) * T], ps[b][:, half_ * T:(half_ + 1) * T],
                          ada[0][:, 1, k, j:j + 1], ada[0][:, 0, k, j:j + 1], ALU.mult, ALU.add)
            last.then_inc(read[b], 1)
        b = wait_full(dve, "dt")
        V.tensor_copy(dtw[:, 0, :], ps[b][:, 0:256]).then_inc(read[b], 1)
        dve.wait_ge(sem("scalar_steps"), 3)
        ts(dtw[:, 2, :], dtw[:, 1, :], 1.0, None, ALU.add).then_inc(sem("dt_plus_one"), 1)
        dve.wait_ge(sem("dt_plus_one"), 1)
        n = step(ts(dtw[:, 4, :], dtw[:, 2, :], -1.0, None, ALU.add))
        after(n)
        n = step(ts(dtw[:, 5, :], dtw[:, 4, :], 0.0, None, ALU.is_equal))
        after(n)
        n = step(tt(dtw[:, 4, :], dtw[:, 4, :], dtw[:, 5, :], ALU.add))
        dve.wait_ge(sem("scalar_steps"), 4)
        n = step(tt(dtw[:, 3, :], dtw[:, 3, :], dtw[:, 5, :], ALU.add))
        after(n)
        n = step(tt(dtw[:, 3, :], dtw[:, 3, :], dtw[:, 1, :], ALU.mult))
        n = step(V.reciprocal(dtw[:, 4, :], dtw[:, 4, :]))
        after(n)
        n = step(tt(dtw[:, 3, :], dtw[:, 3, :], dtw[:, 4, :], ALU.mult))
        after(n)
        dtf = dt_t[:, :, :].rearrange("p a b -> p (a b)")
        n = step(stt(dtf, dtw[:, 0, :], 0.0, dtw[:, 3, :], ALU.max, ALU.add))
        after(n)
        stt(a_t[:, :, :], dt_t[:, :, :], -1.0, aneg[:].unsqueeze(1).to_broadcast([P, 4, 2 * HEADS]), ALU.mult, ALU.mult).then_inc(sem("a_ready"), 1)
        for q in range(XBC_CT):
            ct = 16 + q if q < 8 else q - 8
            u, acc = ubuf[q % 2], cacc[q % 2]
            wait_read(dve, ("xbc", q))
            if q >= 2:
                dve.wait_ge(sem("conv_silu"), q - 1)

            def tap(i, j):
                return vec[:, V_CW + (3 * i + j) * 24 + ct:V_CW + (3 * i + j) * 24 + ct + 1]

            bias = vec[:, V_CB + ct:V_CB + ct + 1]
            ug = u[:, T:2 * T].rearrange("p (r c) -> p r c", r=ROWS)
            ag = acc[:, T:2 * T].rearrange("p (r c) -> p r c", r=ROWS)
            nl = nx = step(ts(acc, u, tap(1, 1), bias, ALU.mult, ALU.add))
            ctx_taps = [(1, 0), (1, 2)] if q < 4 or q >= 8 else []
            for i, j in [(1, 0), (1, 2), (0, 1), (2, 1), (0, 0), (0, 2), (2, 0), (2, 2)]:
                if ctx_taps:
                    _, jj = ctx_taps.pop(0)
                    o, s_ = (acc[:, 1:T], u[:, 0:T - 1]) if jj == 0 else (acc[:, 0:T - 1], u[:, 1:T])
                    after(nx)
                    nx = step(stt(o, s_, tap(1, jj), o, ALU.mult, ALU.add))
                di, dj = i - 1, j - 1
                r0, r1, c0, c1 = max(0, -di), ROWS - max(0, di), max(0, -dj), GRID_W - max(0, dj)
                o, s_ = ag[:, r0:r1, c0:c1], ug[:, r0 + di:r1 + di, c0 + dj:c1 + dj]
                after(nl)
                last = stt(o, s_, tap(i, j), o, ALU.mult, ALU.add)
                if (i, j) == (2, 2):
                    last.then_inc(sem("conv_done"), 1)
                else:
                    nl = step(last)
        wait_read(dve, "decay")
        cols = ((DC_F0, 0, 0), (DC_F1, 1, 0), (DC_F2, 2, 0), (DC_B1, 1, 1), (DC_B0, 0, 1), (DC_B3, 3, 1))
        for j, (dc, c, d) in enumerate(cols):
            n = step(tt(wst[:, j, :], dec[:, dc, :], dt_t[:, c, d * HEADS:(d + 1) * HEADS], ALU.mult))
        after(n)
        for r in range(8, XBC_CT):
            if r >= XBC_CT - 2:
                wait_read(dve, ("xT", r))

        def weigh(dst, c, w):
            return tt(dst.rearrange("p (h d) -> p h d", h=HEADS), xtok[:, c, :].rearrange("p (h d) -> p h d", h=HEADS),
                      bc(w, HEADS, HD), ALU.mult)

        def later_state(d):
            for g in range(GROUPS):
                wait_read(dve, ("S1", d, g))
                s2 = S2[:, d, g * GW:(g + 1) * GW]
                t_ = dec[:, (DC_TF2, DC_TB3)[d], g * HPG:(g + 1) * HPG]
                n = step(tt(s2.rearrange("p (h d) -> p h d", h=HPG), S1[:, d, g * GW:(g + 1) * GW].rearrange("p (h d) -> p h d", h=HPG),
                            bc(t_, HPG, HD), ALU.mult))
                b = wait_full(dve, ("S2", d, g))
                after(n)
                tt(s2, s2, ps[b][:, :], ALU.add).then_inc(read[b], 1)

        for j, (dc, c, d) in enumerate(cols):
            if j in (2, 5):
                dve.wait_ge(sem("x_weighted_first_used"), d + 1)
            elif j == 3:
                wait_full(dve, ("S1", 0, GROUPS - 1))
            elif j == 4:
                wait_full(dve, ("S2", 0, GROUPS - 1))
            weigh(xw[j % 2][:, :], c, wst[:, j, :]).then_inc(sem("x_weighted"), 1)
            if j == 2:
                later_state(0)
        later_state(1)
        for c in range(2):
            if c == 0:
                wait_full(dve, ("S1", 1, GROUPS - 1))
                wait_full(dve, ("S2", 1, GROUPS - 1))
            else:
                wait_full(dve, ("ydiag", 0, GROUPS - 1))
            for d in range(2):
                weigh(xw[d][:, :], 2 + c, dt_t[:, 2 + c, d * HEADS:(d + 1) * HEADS]).then_inc(sem("x_dt"), 1)
            for g in range(GROUPS):
                y = yv[:, c, g * GW:(g + 1) * GW]
                b = wait_full(dve, ("cb", c, g))
                n = step(tt(cbm[:, 0, :], ps[b][:, 0:P], cst[:, C_LE, :], ALU.mult))
                tt(cbm[:, 1, :], ps[b][:, 0:P], cst[:, C_GE, :], ALU.mult).then_inc(read[b], 1)
                after(n)
                wait_read(dve, ("cb", c, g))
                for d in range(2):
                    for h in range(2):
                        wait_read(dve, ("seg", c, g, d, h))
                    tt(EM[d][:, :, :], EM[d][:, :, :], cbm[:, d, :].unsqueeze(1).to_broadcast([P, HPG, P]), ALU.mult).then_inc(sem("mixing_ready"), 1)
                for d in range(2):
                    b = wait_full(dve, ("yoff", c, g, d))
                    e = dec[:, (DC_IF2, DC_IB2)[d] + c, g * HPG:(g + 1) * HPG]
                    o = y if d == 0 else lnt[:, 0, :]
                    tt(o.rearrange("p (h d) -> p h d", h=HPG), ps[b][:, :].rearrange("p (h d) -> p h d", h=HPG), bc(e, HPG, HD), ALU.mult).then_inc(read[b], 1)
                for d in range(2):
                    wait_read(dve, ("yoff", c, g, d))
                n = step(tt(y, y, lnt[:, 0, :], ALU.add))
                after(n)
                b = wait_full(dve, ("ydiag", c, g))
                tt(y, y, ps[b][:, :], ALU.add).then_inc(read[b], 1)
            dve.wait_ge(sem("x_skip"), c + 1)
            wait_read(dve, ("ydiag", c, GROUPS - 1))
            n = step(tt(yv[:, c, :], yv[:, c, :], xtok[:, 2 + c, :], ALU.add))
            after(n)
        for j in range(8):
            wait_read(dve, ("z", j))
            y = yv[:, :, j * BLK:(j + 1) * BLK]
            tt(y, y, zs[j % 2].rearrange("p (t c) -> p t c", t=TT), ALU.mult).then_inc(sem("y_gated"), 1)
        dve.wait_ge(sem("scalar_steps"), 12)
        ts(ss[:, 8:16], ss[:, 0:8], 1.0 / GW, EPS, ALU.mult, ALU.add).then_inc(sem("rms_mean"), 1)
        dve.wait_ge(sem("rms_root"), 1)
        n = step(V.reciprocal(ss[:, 0:8], ss[:, 16:24]))
        after(n)
        for t in range(TT):
            for g in range(GROUPS):
                y = yv[:, t, g * GW:(g + 1) * GW]
                last = ts(y, y, ss[:, 2 * g + t:2 * g + t + 1], None, ALU.mult)
        last.then_inc(sem("y_normed"), 1)

        def layer_norm(l, j, keys):
            dve.wait_ge(sem("ln_rows_in"), 32 * (2 * l + j + 1))
            for u in range(2):
                wait_read(dve, ("ada", l, 2 * GATES[j] + u))
            gates = gate[j + l * j]
            for t in range(TT):
                for h in range(2):
                    b = wait_full(dve, keys[2 * t + h])
                    tt(lnt[:, h, :], ps[b][:, :], gates[:, h * 512:(h + 1) * 512], ALU.mult).then_inc(read[b], 1)
                for h in range(2):
                    wait_read(dve, keys[2 * t + h])
                    x = xres[:, t, h * 512:(h + 1) * 512]
                    n = step(stt(x, x, ALPHA, lnt[:, h, :], ALU.mult, ALU.add))
                    after(n)
                    n = step(V.bn_stats(small[:, t, 6 * h:6 * h + 6], x))
                after(n)
                n = step(V.bn_aggr(small[:, t, 12:14], small[:, t, 0:12]))
            after(n)
            ts(small[:, :, 14], small[:, :, 13], EPS, None, ALU.add).then_inc(sem("ln_variance"), 1)
            dve.wait_ge(sem("ln_root"), 2 * l + j + 1)
            n = step(V.reciprocal(small[:, :, 16], small[:, :, 15]))
            after(n)
            for t in range(TT):
                n = step(ts(xres[:, t, :], xres[:, t, :], small[:, t, 12:13], small[:, t, 16:17], ALU.subtract, ALU.mult))
            for t in range(TT):
                after(n - 1 + t)
                m = step(tt(xres[:, t, :], xres[:, t, :], lnb[:, 0, :], ALU.mult))
            for t in range(TT):
                after(m - 1 + t)
                last = tt(xres[:, t, :], xres[:, t, :], lnb[:, 1, :], ALU.add)
            last.then_inc(sem("layer_norms_done"), 1)

        layer_norm(0, 0, [("mout", j) for j in range(4)])
        phase_end(dve, 1)

        def best(count, src, rest, val, idx):
            for r in range(count):
                n = step(V.max(val(r)[:, 0:8], src(r)))
            after(n)
            for r in range(count):
                step(V.max_index(idx(r)[:, 0:8], val(r)[:, 0:8], src(r)))
                n = step(V.match_replace(rest(r), val(r)[:, 0:8], src(r), LOWEST))
            after(n)
            for r in range(count):
                n = step(V.max(val(r)[:, 8:16], rest(r)))
            after(n)
            for r in range(count):
                n = step(V.max_index(idx(r)[:, 8:16], val(r)[:, 8:16], rest(r)))
            after(n)

        def select_keys(l, r):
            wait_read(dve, ("sc", l, r))
            if r >= 2:
                dve.wait_ge(sem("pair_sums"), PH * l + r - 1)
            if r >= 3:
                dve.wait_ge(sem("positions_weighed"), PH * l + r - 2)
            j = r % 2
            best(4, lambda n: sc[j][:, n, :], lambda n: left[:, n, :], lambda n: topv[j][:, n, :], lambda n: topi[j][:, n, :])
            V.tensor_copy(topf[r % 3][:, :, :], topi[j][:, :, :]).then_inc(sem("keys_selected"), 1)

        def select_pairs(l, r):
            dve.wait_ge(sem("pair_sums"), PH * l + r + 1)
            j = r % 2
            best(TT, lambda t: cand[j][:, t, :], lambda t: cand_left[:, t, :], lambda t: selv[:, t, r, :], lambda t: seli[:, t, :])
            step(ts(posr[:, :, 0, :], seli[:, :, :], 4, None, ALU.logical_shift_right))
            n = step(ts(posr[:, :, 1, :], seli[:, :, :], 15, None, ALU.bitwise_and))
            after(n)
            n = step(V.tensor_copy(posf[:, :, :, :], posr[:, :, :, :]))
            after(n)
            tt(pick[j][:, :, :, :].rearrange("p n k a -> p (n k) a"), cst[:, C_IOTA, 0:TOPK].unsqueeze(1).to_broadcast([P, 4 * TOPK, TOPK]),
               bc(posf[:, :, :, :].rearrange("p t a k -> p (t a k)"), 4 * TOPK, TOPK), ALU.is_equal).then_inc(sem("pairs_selected"), 1)

        def selected_keys(l, r):
            dve.wait_ge(sem("positions_weighed"), PH * l + r + 1)
            for t in range(TT):
                n = step(V.tensor_reduce(seltok[:, t, 0:2, r * TOPK:(r + 1) * TOPK], pick[r % 2][:, 2 * t:2 * t + 2, :, :], AX.X, ALU.add))
            after(n)

        def peer(l):
            modulate(("tT", l), tT, l, 1)
            for j in range(4):
                dve.wait_ge(sem("t_hi"), 4 * l + j + 1)
                s_ = slice(2 * j, 2 * j + 2)
                last = tt(tTlo[:, s_, :], tT[:, s_, :], tThi[:, s_, :].bitcast(F32), ALU.subtract)
            last.then_inc(sem("t_split"), 1)
            for r in range(PH + 2):
                if r < PH:
                    select_keys(l, r)
                if r >= 2:
                    selected_keys(l, r - 2)
                if 1 <= r <= PH:
                    select_pairs(l, r - 1)
            n = step(V.tensor_copy(ksum[:, 0, :, :], selv[:, :, :, 0]))
            after(n)
            flat = selv[:, :, :, :].rearrange("p t h k -> p (t h) k")
            sums = ksum[:, :, :, :].rearrange("p j t h -> p j (t h)")
            tt(flat, flat, bc(sums[:, 0, :], TT * PH, TOPK), ALU.subtract).then_inc(sem("gate_shifted"), 1)
            dve.wait_ge(sem("gate_exp"), l + 1)
            n = step(V.tensor_reduce(sums[:, 0, :], flat, AX.X, ALU.add))
            after(n)
            n = step(V.reciprocal(sums[:, 1, :], sums[:, 0, :]))
            after(n)
            for t in range(TT):
                last = tt(seltok[:, t, 2, :].rearrange("p (h k) -> p h k", h=PH), selv[:, t, :, :], bc(ksum[:, 1, t, :], PH, TOPK), ALU.mult)
            last.then_inc(sem("selected"), 1)
            for u in range(TT):
                b = wait_full(dve, ("selT", l, u))
                V.tensor_copy(selT[:, :, u * P:(u + 1) * P], ps[b][:, 0:3 * P].rearrange("p (j c) -> p j c", j=3)).then_inc(read[b], 1)
            for u in range(TT):
                wait_read(dve, ("selT", l, u))
            phase_end(dve, 2 + 5 * l)
            groups = 2 * TC // OH
            with dve.Fori(0, NTC // 2) as i:
                for n in range(groups):
                    place_free(dve, l, n, i)
                    for half, one in ((1, oneb), (0, onea)):
                        tt(one[n % OHR][:, :, :], cst[:, C_IOTA, :].unsqueeze(1).to_broadcast([P, OH, NK]),
                           bc(selT[:, half, bass.ds(i * (2 * TC) + n * OH, OH)], OH, NK),
                           ALU.is_equal).then_inc(sem(("one_hot_first", "one_hot_second")[half]), 1)
            V.memset(lnt[:, 0, :], 0.0).then_inc(sem("zeros"), 1)
            phase_end(dve, 3 + 5 * l)
            base = stream_base[l]

            def split_u(m, off, h):
                j = off % 2
                dve.wait_ge(sem("u_hi"), m * 2 + (2 * l * NK + h + 1))
                c = slice(4 * h, 4 * h + 4)
                tt(UTlo[j][:, c, :].rearrange("p a b -> p (a b)"), ps[4 + h][:, :], UThi[j][:, c, :].rearrange("p a b -> p (a b)").bitcast(F32),
                   ALU.subtract).then_inc(read[4 + h], 1)

            def tile_step(m, off, i=None):
                j = off % 2
                slot = off % UV
                half = off // 2 if i is None else i * (ROUND // 2) + off // 2
                if off != NK - 1:
                    split_u(m + 1, off + 1, 0)
                dve.wait_ge(sem("v_hi"), m + (l * NK + 1))
                tt(Vlo[j][:], uvring[slot][:, 1, :], Vhi[j][:].bitcast(F32), ALU.subtract).then_inc(sem("v_split"), 1)
                if off != NK - 1:
                    split_u(m + 1, off + 1, 1)
                dve.wait_ge(read[6 + j], half + (base[6 + j] + 1))
                gj = (off // GI) % 2
                rounds_ = off // (2 * GI) if i is None else i + off // (2 * GI)
                dve.wait_ge(g_loaded[gj], rounds_ * 16 + 16 * (l * (NK // GI // 2) + 1))
                tt(gw[j][:].rearrange("p (c t) -> p c t", c=NTC), gel[j][:].rearrange("p (c t) -> p c t", c=NTC),
                   gt[gj][:, :, (off % GI) * TC:(off % GI + 1) * TC], ALU.mult).then_inc(sem("gated"), 1)
                dve.wait_ge(sem("gated"), m + (l * NK + 1))
                V.tensor_copy(Whi[j][:], gw[j][:]).then_inc(sem("w_hi"), 1)
                dve.wait_ge(sem("w_hi"), m + (l * NK + 1))
                tt(Wlo[j][:], gw[j][:], Whi[j][:].bitcast(F32), ALU.subtract).then_inc(sem("w_split"), 1)

            for h in range(2):
                split_u(0, 0, h)
            tiles(dve, tile_step)
            layer_norm(l, 1, [("peer_out", l, j) for j in range(4)])

        peer(0)
        phase_end(dve, 4)
        two_pi = 2 * math.pi
        c1 = 6.28125
        c2 = two_pi - c1
        magic = 1.5 * 2.0 ** 23
        dve.wait_ge(sem("hyena_in"), 176)
        for j in range(3):
            b = wait_full(dve, ("hid", j))
            ts(hid[:, 1, :], ps[b][0:HY_FF, 0:T], hv[:, j:j + 1], hv[:, 3:4], ALU.add, ALU.mult).then_inc(read[b], 1)
            wait_read(dve, ("hid", j))
            n = step(ts(hid[:, 2, :], hid[:, 1, :], 1.0 / two_pi, magic, ALU.mult, ALU.add))
            after(n)
            n = step(ts(hid[:, 2, :], hid[:, 2, :], -magic, None, ALU.add))
            after(n)
            n = step(stt(hid[:, 1, :], hid[:, 2, :], -c1, hid[:, 1, :], ALU.mult, ALU.add))
            after(n)
            n = step(stt(hid[:, 1, :], hid[:, 2, :], -c2, hid[:, 1, :], ALU.mult, ALU.add))
            after(n)
            ts(hid[:, 3, :], hid[:, 1, :], 3.1415925, -3.1415925, ALU.min, ALU.max).then_inc(sem("sine_argument"), 1)
        n = 0
        for t in range(TT):
            dve.wait_ge(sem("lag_decay"), t + 1)
            for o in range(ORDER):
                for h in range(2):
                    if n:
                        dve.wait_ge(sem("filter_sides"), n)
                    for side in range(2):
                        b = wait_full(dve, ("hflt", n, side))
                        tt(hfb[:, side, :], ps[b][:, :], dcy[:, t, h * 512:(h + 1) * 512], ALU.mult).then_inc(read[b], 1)
                    for side in range(2):
                        wait_read(dve, ("hflt", n, side))
                    tt(sd[:, 0, t, o, h * 512:(h + 1) * 512], hfb[:, 0, :], hfb[:, 1, :], ALU.add)
                    tt(sd[:, 1, t, o, h * 512:(h + 1) * 512], hfb[:, 0, :], hfb[:, 1, :], ALU.subtract).then_inc(sem("filter_sides"), 1)
                    n += 1
        for o in range(ORDER):
            for h in range(2):
                n = 2 * o + h
                if n:
                    dve.wait_ge(sem("filter_normed"), n)
                b = wait_full(dve, ("hnorm", n))
                ts(rsn[:], ps[b][:, :], HY_EPS, None, ALU.add).then_inc(read[b], 1)
                dve.wait_ge(sem("norm_root"), n + 1)
                k = step(V.reciprocal(rsn[:], rsn[:]))
                after(k)
                for side in range(2):
                    for t in range(TT):
                        s_ = sd[:, side, t, o, h * 512:(h + 1) * 512]
                        last = tt(s_, s_, rsn[:], ALU.mult)
                last.then_inc(sem("filter_normed"), 1)
        phase_end(dve, 5)
        modulate(("hhT",), hhT, 1, 0)
        for m in range(12):
            wait_read(dve, ("hu", m))
            for c in range(2):
                ct = 2 * m + c
                u, o = hub[m % 2][:, c, :], huT[:, ct, :]

                def tap(j):
                    return vec[:, V_HCW + 24 * j + ct:V_HCW + 24 * j + ct + 1]

                n = step(ts(o, u, tap(1), vec[:, V_HCB + ct:V_HCB + ct + 1], ALU.mult, ALU.add))
                after(n)
                n = step(stt(o[:, 1:T], u[:, 0:T - 1], tap(0), o[:, 1:T], ALU.mult, ALU.add))
                after(n)
                last = stt(o[:, 0:T - 1], u[:, 1:T], tap(2), o[:, 0:T - 1], ALU.mult, ALU.add)
            last.then_inc(sem("hyena_conv"), 1)
        for o in range(ORDER):
            for n in range(4):
                h, fr = n // 2, n % 2
                c = slice(h * 512, (h + 1) * 512)
                if o + n:
                    dve.wait_ge(sem("spectrum_done"), 8 * o + 2 * n)
                b0 = wait_full(dve, ("vs", o, n, 0))
                b1 = wait_full(dve, ("vs", o, n, 1))
                fa, fb, fc = Hs[:, o, fr, c], Hs[:, o, 2 + fr, c], Hs[:, o, 4 if fr == 0 else 1, c]
                step(tt(ytm[:, 0, :], ps[b0][:, :], fa, ALU.mult))
                tt(ytm[:, 2, :], ps[b0][:, :], fb, ALU.mult).then_inc(read[b0], 1)
                k = step(tt(ytm[:, 1, :], ps[b1][:, :], fb, ALU.mult))
                tt(ytm[:, 3, :], ps[b1][:, :], fc, ALU.mult).then_inc(read[b1], 1)
                after(k)
                tt(Yf[:, fr, c], ytm[:, 0, :], ytm[:, 1, :], ALU.subtract).then_inc(sem("spectrum_done"), 1)
                wait_read(dve, ("vs", o, n, 0))
                wait_read(dve, ("vs", o, n, 1))
                tt(Yf[:, 2 + fr, c], ytm[:, 2, :], ytm[:, 3, :], ALU.add).then_inc(sem("spectrum_done"), 1)
            for c2 in range(4):
                if o + c2:
                    dve.wait_ge(sem("order_done"), 8 * o + 2 * c2)
                b = wait_full(dve, ("inv", o, c2))
                for c in range(2):
                    ct = 2 * c2 + c
                    v = huT[:, 16 + ct, :]
                    last = stt(hyt[:, c, :], v, vec[:, V_HB + 8 * o + ct:V_HB + 8 * o + ct + 1], ps[b][:, c * T:(c + 1) * T], ALU.mult, ALU.add)
                    if c == 0:
                        k = step(last)
                last.then_inc(read[b], 1)
                after(k)
                wait_read(dve, ("inv", o, c2))
                for c in range(2):
                    ct = 2 * c2 + c
                    tt(huT[:, 16 + ct, :], hyt[:, c, :], huT[:, 8 * o + ct, :], ALU.mult).then_inc(sem("order_done"), 1)
        layer_norm(1, 0, [("hout", j) for j in range(4)])
        phase_end(dve, 6)
        peer(1)


def dft_tables(np):
    n = 2 * T
    tok = np.arange(T)
    frq = np.arange(T)
    ang = 2 * np.pi * np.outer(tok, frq) / n
    alt = (-1.0) ** tok
    re, im = np.cos(ang), -np.sin(ang)
    fi = im.copy()
    fi[:, 0] = alt
    c0 = re[:, :P].copy()
    c0[:, 0] = alt
    inv_r = 2 * re.T / n
    inv_r[0] = 1.0 / n
    inv_i = 2 * im.T / n
    inv_i[0] = alt / n

    def parts(m):
        return m.reshape(-1, P, m.shape[1]).transpose(1, 0, 2).reshape(P, -1)

    ws = np.full((P, P), 0.5)
    ws[0] = 1.0
    wd = np.full((P, P), 0.5)
    wd[0] = 0.0
    half = np.full((P, P), 0.5)
    return np.ascontiguousarray(np.concatenate(
        [parts(re), parts(fi), parts(im[:, :P]), parts(c0), parts(np.concatenate([inv_r, inv_i])), ws, wd, half], axis=1).astype(np.float32))


def shape_constants(np):
    f32 = np.float32
    i = np.arange(P)
    u, t = i[:, None], i[None, :]
    mats = [u == t, u <= t, u >= t, u < t, u > t, np.ones((P, P)), np.broadcast_to(t, (P, P))]
    tl = np.linspace(0.0, 1.0, T, dtype=f32)
    bands = (HY_EMB - 1) // 2
    ang = (f32(2.0 * math.pi) * np.arange(T, dtype=f32) / f32(T)).astype(f32)
    fb = np.linspace(1e-4, bands - 1, bands, dtype=f32)
    arg = (fb[:, None] * ang[None, :]).astype(f32).astype(np.float64)
    feats = np.concatenate([tl[None, :], np.cos(arg), -np.sin(arg)], axis=0).astype(f32)
    rates = np.abs(np.linspace(math.log(1e-2) / 1.5, math.log(1e-2) / 0.3, D, dtype=f32))
    return {
        "constants": np.ascontiguousarray(np.concatenate([np.asarray(m, f32) for m in mats], axis=1)),
        "hyena_constants": dft_tables(np),
        "filter_features": np.ascontiguousarray(feats),
        "lag_times": np.ascontiguousarray(-tl.reshape(TT, P).T),
        "decay_rates": rates.astype(f32),
    }


INPUTS = ["x", "c", "ctx", "c_ctx", "ada_w", "ada_b", "ln_g", "ln_b", "m_w_in", "m_conv_w", "m_conv_b", "m_a_log",
          "m_dt_bias", "m_d", "m_norm_w", "m_w_out", "h_w_in", "h_conv_w", "h_conv_b", "h_f_w1", "h_f_b1", "h_f_w2",
          "h_f_b2", "h_f_w3", "h_freq", "h_bias", "h_w_out", "p_wq", "p_k1", "p_k2", "p_u", "p_v"]


def kernel(**inputs):
    import numpy as np
    import concourse.bacc as bacc
    from concourse.bass_utils import run_bass_kernel_spmd as run

    nc = bacc.Bacc("TRN2", target_bir_lowering=False, num_devices=1)
    arrays, aps = {}, {}
    given = {n: np.ascontiguousarray(inputs[n]) for n in INPUTS} | shape_constants(np)
    for name, a in given.items():
        arrays[f"in_{name}"] = a
        aps[name] = nc.dram_tensor(f"in_{name}", a.shape, mybir.dt.from_np(a.dtype), kind="ExternalInput").ap()
    out = nc.dram_tensor("out_x", (1, T, D), F32, kind="ExternalOutput").ap()
    build_program(nc, aps, out)
    r = run(nc, [arrays], core_ids=[0])
    return r.results[0]["out_x"]
```

```python
import math
from contextlib import ExitStack

import concourse.bass as bass
from concourse import mybir

F32 = mybir.dt.float32
F32R = mybir.dt.float32r
U32 = mybir.dt.uint32
ACT = mybir.ActivationFunctionType
ALU = mybir.AluOpType
AX = mybir.AxisListType

P = 128
D = 1024
KD = D // P
T = 256
TT = T // P
GRID_W = 64
ROWS = T // GRID_W
DEPTH = 2
ALPHA = (2 * DEPTH) ** 0.25
EPS = 1e-5
INNER = 2 * D
HEADS = 32
HD = 64
GROUPS = 4
HPG = HEADS // GROUPS
GW = HPG * HD
XBC_CT = (INNER + 2 * GROUPS * P) // P
GATES = (2, 5)
UNITS0 = ((0, 1, 2, 3), tuple(range(4, 12)))
UNITS1 = ((0, 1, 2, 3), tuple(range(4, 10)), (10, 11))
ORDER = 2
HY_EPS = 1e-6
HY_FF = 64
HY_EMB = 33
PH = 8
NK = 128
TOPK = 16
HEAD_STEPS = [(do, r) for r in range(3) for do in ("queries", "scores")] + [("queries", 3)] + \
             [(do, r + (do == "queries")) for r in range(3, PH) for do in ("queries", "scores") if (do, r) != ("queries", PH - 1)]
NROW = 2 * PH
BLK = 256
RING = 4
UV = 4
TC = 32
NTC = T // TC
SPLIT = {"xbc": 0, "mout": XBC_CT, "hin": XBC_CT + INNER // P}
OH = 8
OHR = 4
GI = 4
ROUND = 8
NROUND = (NK - ROUND) // ROUND
PEELED = 2
LOWEST = -3.0e38

V_CW, V_CB, V_NW = 0, 216, 240
V_HCW, V_HCB, V_HB, V_C = 256, 328, 352, 368
C_ID, C_LE, C_GE, C_LT, C_GT, C_ONE, C_IOTA = range(7)
H_FR, H_FI, H_BZ, H_C0, H_INV, H_WS, H_WD, H_W1 = 0, 512, 1024, 1280, 1536, 2560, 2688, 2816
H_COLS = 2944
(DC_F0, DC_F1, DC_F2, DC_B1, DC_B0, DC_B3, DC_IF2, DC_IF3, DC_IB2, DC_IB3, DC_TF2, DC_TB3) = range(12)


class BankPlan:

    def __init__(self):
        self.count = [0] * 8
        self.where = {}

    def use(self, key, bank):
        assert key not in self.where, key
        self.where[key] = (bank, self.count[bank], 0)
        self.count[bank] += 1

    def loop(self, rounds, uses):
        per = [sum(b == bank for _, b in uses) for bank in range(8)]
        seen = [0] * 8
        for key, bank in uses:
            assert key not in self.where, key
            self.where[key] = (bank, self.count[bank] + seen[bank], per[bank])
            seen[bank] += 1
        for bank in range(8):
            self.count[bank] += rounds * per[bank]

    def __call__(self, key, i=0):
        bank, base, per = self.where[key]
        return bank, base + i * per if per else base


class Chain:

    def __init__(self, sem):
        self.sem, self.n = sem, 0

    def __call__(self, instruction):
        instruction.then_inc(self.sem, 1)
        self.n += 1
        return self.n


def build_program(nc, A, out):
    ctx = ExitStack()
    with ctx:
        build_in(nc, A, out, ctx)


def build_in(nc, A, out, ctx):
    sems = {}

    def sem(name):
        if name not in sems:
            sems[name] = ctx.enter_context(nc.semaphore(name))
        return sems[name]

    def sb(scope, name, shape, dt=F32):
        return scope.enter_context(nc.sbuf_tensor(name, shape, dt))

    cst = sb(ctx, "constants", [P, 7, P])
    vec = sb(ctx, "channel_vectors", [P, 3 * P])
    xres = sb(ctx, "x_residual", [P, TT, D])
    wring = [sb(ctx, f"weight_block{s}", [P, 2048]) for s in range(RING)]
    lnb = sb(ctx, "ln_gain_bias", [P, 2, D])
    gate = [sb(ctx, f"gate{j}", [P, D]) for j in range(2)]
    s_rep = sb(ctx, "silu_c_repeated", [P, KD, P])
    s_col = sb(ctx, "silu_c_columns", [P, KD, 2])
    brow = sb(ctx, "modulation_bias_rows", [24 * DEPTH, BLK])
    mrow = [sb(ctx, f"modulation_rows{j}", [2, 512]) for j in range(2)]
    ada = [sb(ctx, f"modulation_columns{l}", [P, 4, KD, 2]) for l in range(DEPTH)]
    lnt = sb(ctx, "layer_norm_tmp", [P, 2, 512])
    small = sb(ctx, "layer_norm_small", [P, TT, 24])
    ps = [ctx.enter_context(nc.psum_tensor(f"bank{b}", [P, 512], F32)) for b in range(8)]

    ident = cst[:, C_ID, :]

    with ExitStack() as s:
        hT = sb(s, "mixer_input_T", [P, KD, 2 * T])
        bcT = sb(s, "BC_T", [P, 8, T])
        work = sb(s, "conv_work_or_state2", [P, 4096])
        xtok = sb(s, "x_tokens", [P, 4, INNER])
        btok = sb(s, "B_tokens", [P, 4, GROUPS * P])
        dtb = sb(s, "dt_bias", [2 * HEADS, 1])
        aneg = sb(s, "a_log_rows", [P, 2 * HEADS])
        dskip = sb(s, "d_skip_rows", [P, HEADS])
        dt_t = sb(s, "dt", [P, 4, 2 * HEADS])
        a_t = sb(s, "a", [P, 4, 2 * HEADS])
        dec = sb(s, "decays", [P, 12, HEADS])
        wst = sb(s, "state_weights", [P, 6, HEADS])
        ss = sb(s, "rms", [P, 24])
        with ExitStack() as q:
            hThi = sb(q, "mixer_input_T_hi", [P, KD, 2 * T], F32R)
            hTlo = sb(q, "mixer_input_T_lo", [P, KD, 2 * T], F32R)
            whi = [sb(q, f"weights_hi{j}", [P, KD, P], F32R) for j in range(2)]
            wlo = [sb(q, f"weights_lo{j}", [P, KD, P], F32R) for j in range(2)]
        with ExitStack() as q:
            aM = [sb(q, f"a_masked{j}", [P, HPG, P]) for j in range(2)]
            EM = [sb(q, f"decay_times_cb{j}", [P, HPG, P]) for j in range(2)]
            xw = [sb(q, f"x_weighted{j}", [P, INNER]) for j in range(2)]
            S1 = sb(q, "state_ctx", [P, 2, INNER])
    ctxb = xtok[:, 0, :].rearrange("p (t d) -> p t d", t=TT)
    wdt = xtok[:, 1, 0:KD * 2 * HEADS].rearrange("p (k c) -> p k c", k=KD)
    dtrow = xtok[0:2 * HEADS, 1, KD * 2 * HEADS:KD * 2 * HEADS + 2 * T]
    dtw = xtok[:, 2, 0:1536].rearrange("p (n c) -> p n c", n=6)
    cbm = btok[:, 0, 0:2 * P].rearrange("p (a b) -> p a b", a=2)
    zs = [aM[j][:, 0:4, :].rearrange("p a b -> p (a b)") for j in range(2)]
    ubuf = [work[:, j * 1536:j * 1536 + 512] for j in range(2)]
    cacc = [work[:, j * 1536 + 512:j * 1536 + 1024] for j in range(2)]
    xc = [work[:, j * 1536 + 1024:j * 1536 + 1536] for j in range(2)]
    stg = hT[:, 0, 0:3 * P].rearrange("p (a b) -> p a b", a=3)
    fv = xtok[0:HY_FF, 3, 0:8]
    fw1 = xtok[0:HY_EMB, 3, 64:128]
    fw2 = xtok[0:HY_FF, 3, 128:256].rearrange("p (j b) -> p j b", j=2)
    feat = xtok[0:HY_EMB, 3, 256:512]
    hid = xtok[0:HY_FF, 3, 512:1536].rearrange("p (j t) -> p j t", j=4)
    S2 = work[:, :].rearrange("p (a b) -> p a b", a=2)
    yv = xtok[:, 0:2, :]
    uThi, uTlo = (x[:, :, :].rearrange("p a b -> p (a b)").rearrange("p (a b) -> p a b", a=16) for x in (hThi, hTlo))

    gate.append(sb(ctx, "gate2", [P, D]))

    with ExitStack() as s:
        uvring = [sb(s, f"expert_rows{j}", [P, 2, D]) for j in range(UV)]
        tThi = sb(s, "t_T_hi", [P, KD, T], F32R)
        tTlo = sb(s, "t_T_lo", [P, KD, T], F32R)
        selT = sb(s, "selected_T", [P, 3, T])
        seltok = sb(s, "selected_tokens", [P, TT, 3, P])
        with ExitStack() as q:
            tT = sb(q, "t_T", [P, KD, T])
            qT = [sb(q, f"q_T{j}", [P, 2, T]) for j in range(2)]
            kraw = sb(q, "keys", [P, NROW, P])
            kT = sb(q, "keys_T", [P, NROW, P])
            sc = [sb(q, f"scores{j}", [P, 4, NK]) for j in range(2)]
            left = sb(q, "scores_left", [P, 4, NK])
            topv = [sb(q, f"top_values{j}", [P, 4, TOPK]) for j in range(2)]
            topi = [sb(q, f"top_indices{j}", [P, 4, TOPK], U32) for j in range(2)]
            topf = [sb(q, f"top_indices_f{j}", [P, 4, TOPK]) for j in range(3)]
            cand = [sb(q, f"candidates{j}", [P, TT, TOPK * TOPK]) for j in range(2)]
            cand_left = sb(q, "candidates_left", [P, TT, TOPK * TOPK])
            selv = sb(q, "selected_scores", [P, TT, PH, TOPK])
            seli = sb(q, "selected_positions", [P, TT, TOPK], U32)
            posr = sb(q, "position_parts", [P, TT, 2, TOPK], U32)
            posf = sb(q, "position_parts_f", [P, TT, 2, TOPK])
            pick = [sb(q, f"position_one_hot{j}", [P, 2 * TT, TOPK, TOPK]) for j in range(2)]
            ksum = sb(q, "gate_sums", [P, 2, TT, PH])
        with ExitStack() as q:
            onea = [sb(q, f"one_hot_first{j}", [P, OH, NK]) for j in range(OHR)]
            oneb = [sb(q, f"one_hot_second{j}", [P, OH, NK]) for j in range(OHR)]
            gch = sb(q, "g_chunk", [P, 2, NK, TC])
        with ExitStack() as q:
            UThi = [sb(q, f"u_T_hi{j}", [P, KD, P], F32R) for j in range(2)]
            UTlo = [sb(q, f"u_T_lo{j}", [P, KD, P], F32R) for j in range(2)]
            Vhi = [sb(q, f"v_hi{j}", [P, D], F32R) for j in range(2)]
            Vlo = [sb(q, f"v_lo{j}", [P, D], F32R) for j in range(2)]
            Whi = [sb(q, f"w_hi{j}", [P, T], F32R) for j in range(2)]
            Wlo = [sb(q, f"w_lo{j}", [P, T], F32R) for j in range(2)]
            gel = [sb(q, f"gelu{j}", [P, T]) for j in range(2)]
            gw = [sb(q, f"gelu_gated{j}", [P, T]) for j in range(2)]
            gt = [sb(q, f"g_tile{j}", [P, NTC, GI * TC]) for j in range(2)]

    with ExitStack() as s:
        hc = sb(s, "hyena_constants", [P, H_COLS])
        Hs = sb(s, "filter_spectra", [P, ORDER, 5, D])
        rsn = sb(s, "filter_norms", [P, 2 * ORDER, 512])
        tcol = sb(s, "lag_times", [P, TT])
        with ExitStack() as q:
            hidden = sb(q, "filter_hidden", [HY_FF, T])
            squares = sb(q, "filter_squares", [P, 4, 512])
            w3 = sb(q, "filter_w3", [HY_FF, 4 * D])
            delta = sb(q, "decay_rates", [P, D])
            dcy = sb(q, "lag_decay", [P, TT, D])
            sqr = [dcy[:, :, :].rearrange("p a (b c) -> p (a b) c", b=2), squares[:, :, :]]
            sd = sb(q, "filter_sum_difference", [P, 2, TT, ORDER, D])
        with ExitStack() as q:
            hhT = sb(q, "hyena_input_T", [P, KD, T])
            huT = sb(q, "hyena_u_T", [P, 24, T])
            hub = [sb(q, f"hyena_conv_in{j}", [P, 2, T]) for j in range(2)]
            with ExitStack() as r:
                hhThi = sb(r, "hyena_input_T_hi", [P, KD, T], F32R)
                hhTlo = sb(r, "hyena_input_T_lo", [P, KD, T], F32R)
                hwhi = [sb(r, f"hyena_weights_hi{j}", [P, KD, P], F32R) for j in range(2)]
                hwlo = [sb(r, f"hyena_weights_lo{j}", [P, KD, P], F32R) for j in range(2)]
            with ExitStack() as r:
                vtok = sb(r, "hyena_v_tokens", [P, TT, D])
                Yf = sb(r, "spectrum_product", [P, 4, D])
                ytm = sb(r, "spectrum_tmp", [P, 4, 512])
            hyt = lnt[:, 0, :].rearrange("p (c t) -> p c t", c=2)

    gdram = nc.dram_tensor("g_scratch", [P, NTC, NK * TC], F32).ap()

    hdram = nc.dram_tensor("hidden_scratch", [HY_FF, T], F32).ap()

    plan = BankPlan()
    stream_base = {}
    full = [sem(f"bank{b}_full") for b in range(8)]
    read = [sem(f"bank{b}_read") for b in range(8)]

    plan.use("vecs", 0)

    def plan_ada(l, units, banks, tbanks):
        before = None
        for u in (*units, None):
            if u is not None:
                plan.use(("ada", l, u), banks[u % 2])
            if before is not None and before // 2 not in GATES:
                plan.use(("adaT", l, before), tbanks[before % 2])
            before = u

    def plan_peer(l):
        for k in range(4):
            plan.use(("tT", l, k), k)
        for j in range(4):
            plan.use(("kT", l, j), j)
        for r in range(PH):
            plan.use(("q", l, r), 4 + r % 2)
            plan.use(("sc", l, r), r % 2)
        if l == 0:
            plan_ada(1, UNITS1[1], (2, 3), (6, 7))
        for t in range(TT):
            plan.use(("selT", l, t), t)
        plan.loop(NTC // 2, [(("g", l, j), j % 8) for j in range(2 * TC // 4)])
        for j in range(4):
            plan.use(("peer_out", l, j), j)
        stream_base[l] = list(plan.count)
        for b, n in ((4, NK), (5, NK), (6, NK // 2), (7, NK // 2)):
            plan.count[b] += n

    plan_ada(0, UNITS0[0], (1, 2), (3, 3))
    for j in range(3):
        plan.use(("hid", j), 7)
    for k in range(KD):
        plan.use(("hT", k), k % 8)
    plan.use("dt_rows", 5)
    plan.use("dt", 4)
    for ct in range(XBC_CT):
        plan.use(("xbc", ct), ct % 4)
        if ct < 4 or ct >= 8:
            plan.use(("xT", ct), 6 + ct % 2)
    plan.use("decay", 4)
    for d in range(2):
        for g in range(GROUPS):
            plan.use(("S1", d, g), g)
        for g in range(GROUPS):
            plan.use(("S2", d, g), 4 + g)
    for c in range(2):
        for g in range(GROUPS):
            plan.use(("yoff", c, g, 0), 0)
            plan.use(("yoff", c, g, 1), 1)
            plan.use(("cb", c, g), 2)
            for d in range(2):
                plan.use(("seg", c, g, d, 0), 4 + 2 * d)
                plan.use(("seg", c, g, d, 1), 5 + 2 * d)
            plan_ada(0, (UNITS0[1][4 * c + g],), (4, 4), (5, 5))
            plan.use(("ydiag", c, g), 3)
    for j in range(8):
        plan.use(("z", j), j % 4)
    for ct in range(8):
        plan.use(("uT", ct), 4 + ct % 4)
    for j in range(4):
        plan.use(("mout", j), j)
    plan_ada(1, UNITS1[0], (4, 5), (6, 7))
    plan_peer(0)
    plan_ada(1, UNITS1[2], (4, 5), (4, 5))
    for n in range(2 * TT * ORDER):
        plan.use(("hflt", n, 0), 5 + n % 2)
        plan.use(("hflt", n, 1), 7 if n % 2 else 4)
    for n in range(2 * ORDER):
        plan.use(("hnorm", n), n % 4)
    for n in range(5 * ORDER * 2):
        plan.use(("hspec", n), 4 + n % 4)
    for k in range(4):
        plan.use(("hhT", k), k)
    for b in range(12):
        plan.use(("hu", b), 4 + b % 4)
    for o in range(ORDER):
        for j in range(4):
            plan.use(("vtok", o, j), j)
        for n in range(4):
            plan.use(("vs", o, n, 0), 4 + 2 * (n % 2))
            plan.use(("vs", o, n, 1), 5 + 2 * (n % 2))
        for c in range(4):
            plan.use(("inv", o, c), c)
    for j in range(4):
        plan.use(("hout", j), 4 + j)
    plan_peer(1)

    blocks = []

    def columns(w, c0):
        return w[:, c0:c0 + BLK].rearrange("(k p) c -> p k c", p=P)

    def rows(w, r0):
        return w[r0:r0 + 2 * P, :].rearrange("(k p) c -> p k c", p=P)

    first = {}
    block_done = []
    w_used = sem("weight_blocks_used")
    used = [0]

    def by_count():
        used[0] += 1
        return w_used, used[0]

    def by_bank(key):
        b, n = plan(key)
        return full[b], n + 1

    def stage(name, aps, done):
        first[name] = len(blocks)
        blocks.extend(aps)
        block_done.extend(done(n) for n in range(len(aps)))

    def split_done(name, n):
        return sem("weights_lo"), SPLIT[name] + 2 * (n + 1)

    def stage_ada(l, units):
        for u in units:
            stage(("ada", l, u), [columns(A["ada_w"][l], BLK * (2 * u + s)) for s in range(2)],
                  lambda n: by_bank(("ada", l, u)) if n else by_count())

    stage_ada(0, UNITS0[0])
    stage("xbc", [columns(A["m_w_in"][0], INNER + BLK * b) for b in (8, 9, 10, 11, *range(8))], lambda n: split_done("xbc", n))
    stage_ada(0, UNITS0[1])
    stage("z", [columns(A["m_w_in"][0], BLK * b) for b in range(8)], lambda n: by_bank(("z", n)))
    stage("mout", [rows(A["m_w_out"][0], 2 * P * b) for b in range(8)], lambda n: split_done("mout", n))
    stage_ada(1, UNITS1[0])
    stage(("wq", 0), [columns(A["p_wq"][0], BLK * b) for b in range(8)], lambda n: by_bank(("q", 0, n)))
    stage_ada(1, UNITS1[1] + UNITS1[2])
    stage("hin", [columns(A["h_w_in"][0], BLK * b) for b in range(12)], lambda n: split_done("hin", n))
    stage("hout", [rows(A["h_w_out"][0], 2 * P * b) for b in range(4)], lambda n: by_count() if n < 3 else by_bank(("hout", 3)))
    stage(("wq", 1), [columns(A["p_wq"][1], BLK * b) for b in range(8)], lambda n: by_bank(("q", 1, n)))
    w_loaded = [sem(f"weight_block{s}_loaded") for s in range(RING)]

    uv_loaded = [sem(f"expert_rows{j}_loaded") for j in range(UV)]
    g_loaded = [sem(f"g_tiles{j}_loaded") for j in range(2)]
    g_stored = [sem(f"g_chunk{j}_stored") for j in range(2)]
    phase = sem("phase_ended")

    def phase_end(eng, n):
        eng.drain().then_inc(phase, 1)
        eng.wait_ge(phase, 5 * n)

    def wait_read(eng, key, i=0):
        b, n = plan(key, i)
        eng.wait_ge(read[b], n + 1)

    def wait_full(eng, key, i=0):
        b, n = plan(key, i)
        eng.wait_ge(full[b], n + 1)
        return b

    def place_free(eng, l, n, i):
        if n >= OHR:
            b, u = plan(("g", l, 2 * (n - OHR) + 1), i)
            eng.wait_ge(full[b], u + 1)
        else:
            b, u = plan(("g", l, 2 * (n + OHR) + 1), i)
            eng.wait_ge(full[b], u - 1)

    def tiles(eng, step):
        for off in range(PEELED):
            step(off, off)
        with eng.Fori(0, NROUND) as i:
            for off in range(PEELED, PEELED + ROUND):
                step(i * ROUND + off, off, i)
        for off in range(ROUND * NROUND + PEELED, NK):
            step(off, off)

    def half_block(name, q):
        w = wring[(first[name] + q // 2) % RING]
        if name == "mout":
            return w[:, (q % 2) * D:(q % 2 + 1) * D].rearrange("p (k c) -> p k c", k=KD)
        return w[:, :].rearrange("p (k c) -> p k c", k=KD)[:, :, (q % 2) * P:(q % 2 + 1) * P]

    def weights_lo(eng, tt, name, hi, lo, q):
        eng.wait_ge(sem("weights_hi"), SPLIT[name] + q + 1)
        tt(lo[q % 2][:, :, :], half_block(name, q), hi[q % 2][:, :, :].bitcast(F32), ALU.subtract).then_inc(sem("weights_lo"), 1)

    block = ctx.enter_context(nc.Block())

    @block.sync
    def _(sp):
        sp.dma_start(cst[:], A["constants"].rearrange("p (a b) -> p a b", a=7)).then_inc(sem("constants_in"), 16)
        cw = A["m_conv_w"][0].rearrange("i j (c b) -> (i j c) b", b=P)
        loads = [
            (stg[0:128, 0, :], cw[0:128]), (stg[0:88, 1, :], cw[128:216]),
            (stg[88:112, 1, :], A["m_conv_b"][0].rearrange("(c b) -> c b", b=P)),
            (stg[112:128, 1, :], A["m_norm_w"][0].rearrange("(c b) -> c b", b=P)),
            (stg[0:72, 2, :], A["h_conv_w"][0].rearrange("i (c b) -> (i c) b", b=P)),
            (stg[72:96, 2, :], A["h_conv_b"][0].rearrange("(c b) -> c b", b=P)),
            (stg[96:112, 2, :], A["h_bias"][0].rearrange("i (c b) -> (i c) b", b=P)),
            (stg[112:120, 2, :], A["c"][0].rearrange("(c b) -> c b", b=P)),
            (stg[120:128, 2, :], A["c_ctx"].rearrange("(c b) -> c b", b=P)),
            (brow[:], A["ada_b"].rearrange("l (b c) -> (l b) c", c=BLK)),
        ]
        for dst, src in loads:
            sp.dma_start(dst, src).then_inc(sem("vectors_in"), 16)

        for dst, src in [
            (fv[:, 0:1], A["h_f_b1"].rearrange("o f -> f o")), (fv[:, 1:2], A["h_f_b2"][0, 0:1, :].rearrange("o f -> f o")),
            (fv[:, 2:3], A["h_f_b2"][0, 1:2, :].rearrange("o f -> f o")), (fv[:, 3:4], A["h_freq"].rearrange("o f -> f o")),
            (fw1, A["h_f_w1"][0]), (fw2, A["h_f_w2"][0].rearrange("j a b -> a j b")), (feat, A["filter_features"]),
        ]:
            sp.dma_start(dst, src).then_inc(sem("filter_network_in"), 16)

        def weights(n0, n1):
            for n in range(n0, n1):
                if n >= RING:
                    sp.wait_ge(*block_done[n - RING])
                k = blocks[n].shape[1]
                dst = wring[n % RING][:, :].rearrange("p (k c) -> p k c", k=k)
                sp.dma_start(dst, blocks[n]).then_inc(w_loaded[n % RING], 16)

        def ln_rows(l, j):
            sp.wait_ge(sem("layer_norms_done"), 2 * l + j)
            sp.dma_start(lnb[:, 0, :], A["ln_g"][l, j].partition_broadcast(P)).then_inc(sem("ln_rows_in"), 16)
            sp.dma_start(lnb[:, 1, :], A["ln_b"][l, j].partition_broadcast(P)).then_inc(sem("ln_rows_in"), 16)

        weights(0, 4)
        sp.dma_start(ctxb, A["ctx"].rearrange("o (t p) d -> p (o t) d", p=P)).then_inc(sem("tokens_in"), 16)
        sp.dma_start(xres[:], A["x"].rearrange("o (t p) d -> p (o t) d", p=P)).then_inc(sem("tokens_in"), 16)
        sp.dma_start(wdt, A["m_w_in"][0][:, INNER + XBC_CT * P:].rearrange("(k p) c -> p k c", p=P)).then_inc(sem("dt_in"), 16)
        sp.dma_start(dtb[:], A["m_dt_bias"].rearrange("o a b -> (a b) o")).then_inc(sem("dt_in"), 16)
        sp.dma_start(aneg[:], A["m_a_log"].rearrange("o a b -> (o a b)").partition_broadcast(P)).then_inc(sem("dt_in"), 16)
        sp.dma_start(dskip[:], A["m_d"].rearrange("o b -> (o b)").partition_broadcast(P)).then_inc(sem("dt_in"), 16)
        ln_rows(0, 0)
        weights(4, first["xbc"] + 2)
        sp.wait_ge(sem("sine"), 3)
        sp.dma_start(hdram, hid[:, 0, :]).then_inc(sem("hidden_stored"), 16)
        weights(first["xbc"] + 2, first[("wq", 0)] + 4)

        def peer(l):
            u, v = A["p_u"][l], A["p_v"][l]
            sp.dma_start(kraw[:, 0:PH, :], A["p_k1"][l].rearrange("h k d -> k h d")).then_inc(sem("keys_in"), 16)
            sp.dma_start(kraw[:, PH:, :], A["p_k2"][l].rearrange("h k d -> k h d")).then_inc(sem("keys_in"), 16)

            def tile(m, slot):
                sp.dma_start(uvring[slot][:, 0, :], u[bass.ds(m * P, P), :]).then_inc(uv_loaded[slot], 16)
                sp.dma_start(uvring[slot][:, 1, :], v[bass.ds(m * P, P), :]).then_inc(uv_loaded[slot], 16)

            def g_tiles(n, j):
                sp.dma_start(gt[j][:], gdram[:, :, bass.ds(n * GI * TC, GI * TC)]).then_inc(g_loaded[j], 16)

            weights(first[("wq", l)] + 4, first[("wq", l)] + 8)
            for m in range(UV):
                tile(m, m)
            ln_rows(l, 1)
            if l == 0:
                weights(first[("ada", 1, UNITS1[1][0])], first["hin"])
            phase_end(sp, 2 + 5 * l)
            phase_end(sp, 3 + 5 * l)
            for j in range(2):
                sp.wait_ge(g_stored[j], 16 + 16 * (l + 1) * (NTC // 2))
            g_tiles(0, 0)
            g_tiles(1, 1)

            def refill(m, slot):
                sp.wait_ge(sem("v_split"), m + (l * NK - UV + 1))
                sp.wait_ge(uv_loaded[slot], 32)
                tile(m, slot)

            with sp.Fori(0, NROUND) as i:
                for off in range(UV, UV + ROUND):
                    refill(i * ROUND + off, off % UV)
                    if off % GI == GI - 1:
                        n = (off + 1) // GI
                        sp.wait_ge(sem("gated"), i * ROUND + (l * NK + (n - 1) * GI))
                        sp.wait_ge(g_loaded[n % 2], 16)
                        g_tiles(i * 2 + n, n % 2)
            for m in range(UV + ROUND * NROUND, NK):
                refill(m, m % UV)

        phase_end(sp, 1)
        peer(0)
        phase_end(sp, 4)
        sp.wait_ge(sem("hidden_stored"), 16)
        for dst, src in [
            (tcol[:], A["lag_times"]), (delta[:], A["decay_rates"].partition_broadcast(P)), (hidden[:], hdram),
            (w3[:], A["h_f_w3"][0]), (hc[:], A["hyena_constants"]),
        ]:
            sp.dma_start(dst, src).then_inc(sem("hyena_in"), 16)
        weights(first["hin"], first["hin"] + 4)
        ln_rows(1, 0)
        phase_end(sp, 5)
        weights(first["hin"] + 4, first[("wq", 1)] + 4)
        phase_end(sp, 6)
        peer(1)
        sp.wait_ge(sem("layer_norms_done"), 4)
        sp.dma_start(out.rearrange("o (t p) d -> p (o t) d", p=P), xres[:]).then_inc(sem("out_stored"), 16)
        sp.wait_ge(sem("out_stored"), 16)

    @block.tensor
    def _(pe):
        mm = nc.tensor.matmul

        def begin(key, i=0):
            b, n = plan(key, i)
            pe.wait_ge(read[b], n)
            return b

        def block_in(n):
            pe.wait_ge(w_loaded[n % RING], 16 * (n // RING + 1))
            return wring[n % RING]

        pe.wait_ge(sem("constants_in"), 16)
        pe.wait_ge(sem("vectors_in"), 160)
        for t in range(3):
            last = nc.tensor.transpose(ps[0][:, t * P:(t + 1) * P], stg[:, t, :], ident)
        last.then_inc(full[0], 1)

        def modulation_products(l, u):
            gates = u // 2 in GATES
            m = P if gates else 2
            if gates:
                pe.wait_ge(sem("silu_c_rows"), 1)
            b = begin(("ada", l, u))
            for s in range(2):
                w = block_in(first[("ada", l, u)] + s)
                row = 24 * l + 2 * u + s
                o = ps[b][0:m, s * BLK:(s + 1) * BLK]
                mm(o, ident[0:24 * DEPTH, row:row + 1].to_broadcast([24 * DEPTH, m]), brow[:], start=True, stop=False)
                for k in range(KD):
                    last = mm(o, s_rep[:, k, :] if gates else s_col[:, k, :], w[:, k * BLK:(k + 1) * BLK],
                              start=False, stop=(k == KD - 1))
                if s == 0:
                    last.then_inc(w_used, 1)
            last.then_inc(full[b], 1)

        def modulation_columns(l, u):
            if u // 2 in GATES:
                return
            wait_read(pe, ("ada", l, u))
            b = begin(("adaT", l, u))
            for c in range(4):
                last = nc.tensor.transpose(ps[b][:, 2 * c:2 * c + 2], mrow[u % 2][:, c * P:(c + 1) * P], ident[0:2, 0:2])
            last.then_inc(full[b], 1)

        def modulation(l, units, before=lambda n: None):
            for n, u in enumerate(units):
                before(n)
                modulation_products(l, u)
                if n:
                    modulation_columns(l, units[n - 1])
            modulation_columns(l, units[-1])

        def filter_network(j):
            if j == 3:
                return
            b = begin(("hid", j))
            if j == 0:
                pe.wait_ge(sem("filter_network_in"), 112)
                last = mm(ps[b][0:HY_FF, 0:T], fw1, feat, start=True, stop=True)
            else:
                pe.wait_ge(sem("sine"), j)
                last = mm(ps[b][0:HY_FF, 0:T], fw2[:, j - 1, :], hid[:, 0, :], start=True, stop=True)
            last.then_inc(full[b], 1)

        pe.wait_ge(sem("silu_c"), 1)
        modulation(0, UNITS0[0], filter_network)
        pe.wait_ge(sem("tokens_in"), 32)
        for k in range(KD):
            b = begin(("hT", k))
            for t in range(4):
                src = ctxb[:, t, k * P:(k + 1) * P] if t < 2 else xres[:, t - 2, k * P:(k + 1) * P]
                last = nc.tensor.transpose(ps[b][:, t * P:(t + 1) * P], src, ident)
            last.then_inc(full[b], 1)
        pe.wait_ge(sem("dt_in"), 64)
        b = begin("dt_rows")
        for k in range(KD):
            wait_read(pe, ("hT", k))
            last = mm(ps[b][0:2 * HEADS, :], wdt[:, k, :], hT[:, k, :], start=(k == 0), stop=(k == KD - 1))
        last.then_inc(full[b], 1)
        wait_read(pe, "dt_rows")
        b = begin("dt")
        for t in range(4):
            last = nc.tensor.transpose(ps[b][:, t * 64:(t + 1) * 64], dtrow[:, t * P:(t + 1) * P], ident[0:2 * HEADS, 0:2 * HEADS])
        last.then_inc(full[b], 1)
        for q in range(XBC_CT + 2):
            if q < XBC_CT:
                pe.wait_ge(sem("weights_lo"), q + 1)
                if q == 0:
                    pe.wait_ge(sem("mixer_input_split"), 1)
                b = begin(("xbc", q))
                for k in range(KD):
                    for n, (lhs, rhs) in enumerate(((whi, hThi), (whi, hTlo), (wlo, hThi))):
                        last = mm(ps[b][:, :], lhs[q % 2][:, k, :], rhs[:, k, :], start=(k + n == 0), stop=(k == KD - 1 and n == 2))
                last.then_inc(full[b], 1)
            r = q - 2
            if 0 <= r < 4 or r >= 8:
                pe.wait_ge(sem("conv_silu"), r + 1)
                b = begin(("xT", r))
                for t in range(4):
                    last = nc.tensor.transpose(ps[b][:, t * P:(t + 1) * P], xc[r % 2][:, t * P:(t + 1) * P], ident)
                last.then_inc(full[b], 1)
        pe.wait_ge(sem("a_ready"), 1)
        b = begin("decay")
        F, B = slice(0, HEADS), slice(HEADS, 2 * HEADS)
        for n, terms in enumerate([
            [(C_GT, 0, F), (C_ONE, 1, F)], [(C_GT, 1, F)], [(C_GT, 2, F)],
            [(C_LT, 1, B), (C_ONE, 0, B)], [(C_LT, 0, B)], [(C_LT, 3, B)],
            [(C_LE, 2, F)], [(C_LE, 3, F)], [(C_GE, 2, B)], [(C_GE, 3, B)], [(C_ONE, 2, F)], [(C_ONE, 3, B)],
        ]):
            for j, (m, c, h) in enumerate(terms):
                last = mm(ps[b][:, n * HEADS:(n + 1) * HEADS], cst[:, m, :], a_t[:, c, h],
                          start=(j == 0), stop=(j == len(terms) - 1))
        last.then_inc(full[b], 1)
        for d in range(2):
            chunks = (0, 1, 2) if d == 0 else (1, 0, 3)
            for n, c in enumerate(chunks):
                j = 3 * d + n
                pe.wait_ge(sem("x_weighted"), j + 1)
                for g in range(GROUPS):
                    if n == 0:
                        b = begin(("S1", d, g))
                    elif n == 2:
                        b = begin(("S2", d, g))
                    else:
                        b = plan(("S1", d, g))[0]
                    last = mm(ps[b][:, :], btok[:, c, g * P:(g + 1) * P], xw[j % 2][:, g * GW:(g + 1) * GW],
                              start=(n != 1), stop=(n != 0))
                    if n:
                        last.then_inc(full[b], 1)
                    elif g == GROUPS - 1:
                        last.then_inc(sem("x_weighted_first_used"), 1)
        for c in range(2):
            for g in range(GROUPS):
                ct_ = bcT[:, 4 + g, c * P:(c + 1) * P]
                for d in range(2):
                    b = begin(("yoff", c, g, d))
                    which, states = ("S1", S1) if c == d else ("S2", S2)
                    wait_read(pe, (which, d, g))
                    st = states[:, d, g * GW:(g + 1) * GW]
                    mm(ps[b][:, :], ct_, st, start=True, stop=True).then_inc(full[b], 1)
                b = begin(("cb", c, g))
                mm(ps[b][:, 0:P], bcT[:, g, c * P:(c + 1) * P], ct_, start=True, stop=True).then_inc(full[b], 1)
                for d in range(2):
                    pe.wait_ge(sem("a_masked"), 2 * (4 * c + g) + d + 1)
                    for h in range(HPG):
                        if h % 4 == 0:
                            b = begin(("seg", c, g, d, h // 4))
                        last = mm(ps[b][:, (h % 4) * P:(h % 4 + 1) * P], aM[d][:, h, :], cst[:, (C_LE, C_GE)[d], :],
                                  start=True, stop=True)
                        if h % 4 == 3:
                            last.then_inc(full[b], 1)
                modulation_products(0, UNITS0[1][4 * c + g])
                pe.wait_ge(sem("x_dt"), 2 * (c + 1))
                pe.wait_ge(sem("mixing_ready"), 2 * (4 * c + g) + 2)
                b = begin(("ydiag", c, g))
                for h in range(HPG):
                    for d in range(2):
                        hh = g * HPG + h
                        last = mm(ps[b][:, h * HD:(h + 1) * HD], EM[d][:, h, :], xw[d][:, hh * HD:(hh + 1) * HD],
                                  start=(d == 0), stop=(d == 1))
                last.then_inc(full[b], 1)
                modulation_columns(0, UNITS0[1][4 * c + g])
        for j in range(8):
            w = block_in(first["z"] + j)
            b = begin(("z", j))
            for t in range(TT):
                for k in range(KD):
                    last = mm(ps[b][:, t * BLK:(t + 1) * BLK], hT[:, k, T + t * P:T + (t + 1) * P], w[:, k * BLK:(k + 1) * BLK],
                              start=(k == 0), stop=(k == KD - 1))
            last.then_inc(full[b], 1)
        for j in range(8):
            pe.wait_ge(sem("y_normed"), j // 2 + 1)
            b = begin(("uT", j))
            for c in range(2):
                for t in range(TT):
                    last = nc.tensor.transpose(ps[b][:, (2 * c + t) * P:(2 * c + t + 1) * P],
                                               yv[:, t, (2 * j + c) * P:(2 * j + c + 1) * P], ident)
            last.then_inc(full[b], 1)

        def project(name, keys, lhs, kts, ready):
            for k in range(kts):
                ready(k)
                w = block_in(first[name] + k // 2)
                for t in range(TT):
                    for h in range(2):
                        b = begin(keys[2 * t + h]) if k == 0 else plan(keys[2 * t + h])[0]
                        last = mm(ps[b][:, :], lhs(k, t), w[:, (k % 2) * D + h * 512:(k % 2) * D + (h + 1) * 512],
                                  start=(k == 0), stop=(k == kts - 1))
                        if k == kts - 1:
                            last.then_inc(full[b], 1)
                if k % 2 and k < kts - 1:
                    last.then_inc(w_used, 1)

        for k in range(INNER // P):
            wait_read(pe, ("uT", k // 2))
            pe.wait_ge(sem("weights_lo"), SPLIT["mout"] + k + 1)
            for t in range(TT):
                for h in range(2):
                    b = begin(("mout", 2 * t + h)) if k == 0 else plan(("mout", 2 * t + h))[0]
                    for n, (lhs, rhs) in enumerate(((uThi, whi), (uThi, wlo), (uTlo, whi))):
                        last = mm(ps[b][:, :], lhs[:, k, t * P:(t + 1) * P],
                                  rhs[k % 2][:, :, :].rearrange("p k c -> p (k c)")[:, h * 512:(h + 1) * 512],
                                  start=(k + n == 0), stop=(k == INNER // P - 1 and n == 2))
                    if k == INNER // P - 1:
                        last.then_inc(full[b], 1)
            if k < INNER // P - 1:
                last.then_inc(sem("out_weights_used"), 1)
        modulation(1, UNITS1[0])
        phase_end(pe, 1)

        def peer(l):
            pe.wait_ge(sem("layer_norms_done"), 2 * l + 1)
            for j in range(4):
                b = begin(("tT", l, j))
                for c in range(2):
                    for t in range(TT):
                        last = nc.tensor.transpose(ps[b][:, (2 * c + t) * P:(2 * c + t + 1) * P],
                                                   xres[:, t, (2 * j + c) * P:(2 * j + c + 1) * P], ident)
                last.then_inc(full[b], 1)
            pe.wait_ge(sem("keys_in"), 32 * (l + 1))
            for j in range(4):
                b = begin(("kT", l, j))
                for r in range(4):
                    last = nc.tensor.transpose(ps[b][:, r * P:(r + 1) * P], kraw[:, 4 * j + r, :], ident)
                last.then_inc(full[b], 1)

            def queries(r):
                w = block_in(first[("wq", l)] + r)
                b = begin(("q", l, r))
                for c in range(2):
                    for k in range(KD):
                        if r + c == 0 and k % 2 == 0:
                            wait_read(pe, ("tT", l, k // 2))
                        last = mm(ps[b][:, c * T:(c + 1) * T], w[:, k * BLK + c * P:k * BLK + (c + 1) * P], tT[:, k, :],
                                  start=(k == 0), stop=(k == KD - 1))
                last.then_inc(full[b], 1)

            def scores(r):
                wait_read(pe, ("q", l, r))
                b = begin(("sc", l, r))
                for t in range(TT):
                    for a in range(2):
                        last = mm(ps[b][:, (2 * t + a) * P:(2 * t + a + 1) * P], qT[r % 2][:, a, t * P:(t + 1) * P], kT[:, PH * a + r, :],
                                  start=True, stop=True)
                last.then_inc(full[b], 1)

            for do, r in HEAD_STEPS:
                if do == "queries":
                    queries(r)
                else:
                    if r == 0:
                        for j in range(4):
                            wait_read(pe, ("kT", l, j))
                    scores(r)
            if l == 0:
                modulation(1, UNITS1[1])
            pe.wait_ge(sem("selected"), l + 1)
            for t in range(TT):
                b = begin(("selT", l, t))
                for j in range(3):
                    last = nc.tensor.transpose(ps[b][:, j * P:(j + 1) * P], seltok[:, t, j, :], ident)
                last.then_inc(full[b], 1)
            phase_end(pe, 2 + 5 * l)
            groups = 2 * TC // OH
            with pe.Fori(0, NTC // 2) as i:
                for n in range(groups):
                    pe.wait_ge(sem("one_hot_first"), i * groups + (l * T // OH + n + 1))
                    pe.wait_ge(sem("one_hot_gated"), i * groups + (l * T // OH + n + 1))
                    for t in range(OH):
                        if t % 4 == 0:
                            b = begin(("g", l, 2 * n + t // 4), i)
                        last = mm(ps[b][:, (t % 4) * P:(t % 4 + 1) * P], oneb[n % OHR][:, t, :], onea[n % OHR][:, t, :],
                                  start=True, stop=True)
                        if t % 4 == 3:
                            last.then_inc(full[b], 1)
            base = stream_base[l]
            def transpose_u(m, off, h):
                slot = off % UV
                pe.wait_ge(read[4 + h], m + base[4 + h])
                if h == 0:
                    pe.wait_ge(uv_loaded[slot], (m - slot) * 8 + 32 * (l * (NK // UV) + 1))
                for k in range(4):
                    last = nc.tensor.transpose(ps[4 + h][:, k * P:(k + 1) * P], uvring[slot][:, 0, (4 * h + k) * P:(4 * h + k + 1) * P], ident)
                last.then_inc(full[4 + h], 1)

            def combine(m, off):
                j = off % 2
                pe.wait_ge(sem("w_split"), m + (l * NK + 1))
                pe.wait_ge(sem("v_split"), m + (l * NK + 1))
                final = off == NK - 1
                for t in range(TT):
                    c = slice(t * P, (t + 1) * P)
                    for lhs, rhs in ((Whi, Vhi), (Whi, Vlo), (Wlo, Vhi)):
                        for h in range(2):
                            if off == 0 and lhs is Whi and rhs is Vhi:
                                begin(("peer_out", l, 2 * t + h))
                            last = mm(ps[2 * t + h][:, :], lhs[j][:, c], rhs[j][:, h * 512:(h + 1) * 512],
                                      start=(off == 0 and lhs is Whi and rhs is Vhi),
                                      stop=final and lhs is Wlo, skip_group_check=True)
                            if final and lhs is Wlo:
                                last.then_inc(full[2 * t + h], 1)
                if not final:
                    last.then_inc(sem("combined"), 1)

            def step(m, off, i=None):
                if off != NK - 1:
                    transpose_u(m + 1, off + 1, 0)
                j = off % 2
                half_m = (off // 2) if i is None else i * (ROUND // 2) + off // 2
                pe.wait_ge(read[6 + j], half_m + base[6 + j])
                for h in range(2):
                    pe.wait_ge(read[4 + h], m + (base[4 + h] + 1))
                if off == 0:
                    pe.wait_ge(sem("t_split"), l + 1)
                n = 0
                for k in range(KD):
                    for lhs, rhs in ((UThi, tThi), (UThi, tTlo), (UTlo, tThi)):
                        last = mm(ps[6 + j][:, 0:T], lhs[j][:, k, :], rhs[:, k, :], start=(n == 0), stop=(n == 3 * KD - 1))
                        n += 1
                last.then_inc(full[6 + j], 1)
                if off != NK - 1:
                    transpose_u(m + 1, off + 1, 1)
                if off != 0:
                    combine(m - 1, off - 1)

            for h in range(2):
                transpose_u(0, 0, h)
            phase_end(pe, 3 + 5 * l)
            tiles(pe, step)
            combine(NK - 1, NK - 1)

        peer(0)
        phase_end(pe, 4)
        modulation(1, UNITS1[2])
        pe.wait_ge(sem("hyena_in"), 80)
        n = 0
        for t in range(TT):
            for o in range(ORDER):
                for h in range(2):
                    for side in range(2):
                        b = begin(("hflt", n, side))
                        c = o * 2 * D + side * D + h * 512
                        mm(ps[b][:, :], hidden[:, t * P:(t + 1) * P], w3[:, c:c + 512], start=True, stop=True).then_inc(full[b], 1)
                    n += 1
        pe.wait_ge(sem("filter_sides"), 2 * TT * ORDER)
        n = 0
        for o in range(ORDER):
            for h in range(2):
                for tile, (col, step_, side) in enumerate(((H_FR, 256, 0), (H_FR + P, 256, 0), (H_BZ, P, 1), (H_FI + P, 256, 1), (H_C0, P, 0))):
                    b = begin(("hspec", n))
                    for t in range(TT):
                        last = mm(ps[b][:, :], hc[:, col + t * step_:col + t * step_ + P], sd[:, side, t, o, h * 512:(h + 1) * 512],
                                  start=(t == 0), stop=(t == 1))
                    last.then_inc(full[b], 1)
                    n += 1
                m = 2 * o + h
                pe.wait_ge(sem("filter_squares"), m + 1)
                b = begin(("hnorm", m))
                for j, w in enumerate((H_WS, H_W1, H_WD, H_W1)):
                    last = mm(ps[b][:, :], hc[:, w:w + P], sqr[m % 2][:, j, :], start=(j == 0), stop=(j == 3))
                last.then_inc(full[b], 1)
        pe.wait_ge(sem("layer_norms_done"), 2)
        for j in range(4):
            b = begin(("hhT", j))
            for c in range(2):
                for t in range(TT):
                    last = nc.tensor.transpose(ps[b][:, (2 * c + t) * P:(2 * c + t + 1) * P],
                                               xres[:, t, (2 * j + c) * P:(2 * j + c + 1) * P], ident)
            last.then_inc(full[b], 1)
        phase_end(pe, 5)
        for j in range(4):
            wait_read(pe, ("hhT", j))
        for n in range(12):
            b = begin(("hu", n))
            for c in range(2):
                pe.wait_ge(sem("weights_lo"), SPLIT["hin"] + 2 * n + c + 1)
                if n + c == 0:
                    pe.wait_ge(sem("hyena_input_split"), 1)
                for k in range(KD):
                    for m, (lhs, rhs) in enumerate(((hwhi, hhThi), (hwhi, hhTlo), (hwlo, hhThi))):
                        last = mm(ps[b][:, c * T:(c + 1) * T], lhs[c][:, k, :], rhs[:, k, :],
                                  start=(k + m == 0), stop=(k == KD - 1 and m == 2))
                if c == 0:
                    last.then_inc(sem("hyena_weights_used"), 1)
            last.then_inc(full[b], 1)
        for o in range(ORDER):
            for j in range(4):
                if o == 0:
                    pe.wait_ge(sem("hyena_conv"), 9 + j)
                else:
                    pe.wait_ge(sem("order_done"), 2 * (j + 1))
                b = begin(("vtok", o, j))
                for t in range(TT):
                    for c in range(2):
                        last = nc.tensor.transpose(ps[b][:, (2 * t + c) * P:(2 * t + c + 1) * P],
                                                   huT[:, 16 + 2 * j + c, t * P:(t + 1) * P], ident)
                last.then_inc(full[b], 1)
            for j in range(4):
                wait_read(pe, ("vtok", o, j))
            for n in range(4):
                h, f = n // 2, n % 2
                for part, col in enumerate((H_FR, H_FI)):
                    b = begin(("vs", o, n, part))
                    for t in range(TT):
                        last = mm(ps[b][:, :], hc[:, col + t * 256 + f * P:col + t * 256 + (f + 1) * P], vtok[:, t, h * 512:(h + 1) * 512],
                                  start=(t == 0), stop=(t == 1))
                    last.then_inc(full[b], 1)
            pe.wait_ge(sem("spectrum_done"), 8 * (o + 1))
            for c2 in range(4):
                b = begin(("inv", o, c2))
                for c in range(2):
                    for k in range(4):
                        last = mm(ps[b][:, c * T:(c + 1) * T], Yf[:, k, (2 * c2 + c) * P:(2 * c2 + c + 1) * P],
                                  hc[:, H_INV + k * T:H_INV + (k + 1) * T], start=(k == 0), stop=(k == 3))
                last.then_inc(full[b], 1)
        project("hout", [("hout", j) for j in range(4)], lambda k, t: huT[:, 16 + k, t * P:(t + 1) * P], 8,
                lambda k: pe.wait_ge(sem("order_done"), 8 + k + 1))
        phase_end(pe, 6)
        peer(1)

    @block.gpsimd
    def _(pool):
        tt = nc.gpsimd.tensor_tensor
        for q in range(XBC_CT):
            weights_lo(pool, tt, "xbc", whi, wlo, q)
        wait_full(pool, ("xbc", XBC_CT - 1))
        pool.wait_ge(sem("a_ready"), 1)
        for c in range(2):
            for g in range(GROUPS):
                for d in range(2):
                    if c + g:
                        wait_full(pool, ("seg", c - (g == 0), (g - 1) % GROUPS, d, 1))
                    a = a_t[:, 2 + c, d * HEADS + g * HPG:d * HEADS + (g + 1) * HPG]
                    tt(aM[d][:, :, :], a.unsqueeze(2).to_broadcast([P, HPG, P]),
                       cst[:, (C_GT, C_LT)[d], :].unsqueeze(1).to_broadcast([P, HPG, P]), ALU.mult).then_inc(sem("a_masked"), 1)
            pool.wait_ge(sem("x_dt"), 2 * (c + 1))
            x3 = xtok[:, 2 + c, :].rearrange("p (h d) -> p h d", h=HEADS)
            tt(x3, x3, dskip[:].unsqueeze(2).to_broadcast([P, HEADS, HD]), ALU.mult).then_inc(sem("x_skip"), 1)
        phase_end(pool, 1)

        def peer(l):
            def sums(r):
                pool.wait_ge(sem("keys_selected"), PH * l + r + 1)
                if r >= 2:
                    pool.wait_ge(sem("pairs_selected"), PH * l + r - 1)
                v = topv[r % 2][:, :, :].rearrange("p (t a) k -> p t a k", a=2)
                shape = [P, TOPK, TOPK]
                for t in range(TT):
                    last = tt(cand[r % 2][:, t, :].rearrange("p (a b) -> p a b", a=TOPK), v[:, t, 0, :].unsqueeze(2).to_broadcast(shape),
                              v[:, t, 1, :].unsqueeze(1).to_broadcast(shape), ALU.add)
                last.then_inc(sem("pair_sums"), 1)

            def weigh(r):
                pool.wait_ge(sem("pairs_selected"), PH * l + r + 1)
                for n in range(2 * TT):
                    p = pick[r % 2][:, n, :, :]
                    last = tt(p, p, topf[r % 3][:, n, :].unsqueeze(1).to_broadcast([P, TOPK, TOPK]), ALU.mult)
                last.then_inc(sem("positions_weighed"), 1)

            for r in range(PH + 1):
                if r < PH:
                    sums(r)
                if r >= 1:
                    weigh(r - 1)
            phase_end(pool, 2 + 5 * l)
            groups = 2 * TC // OH
            with pool.Fori(0, NTC // 2) as i:
                for n in range(groups):
                    pool.wait_ge(sem("one_hot_second"), i * groups + (l * T // OH + n + 1))
                    tt(oneb[n % OHR][:, :, :], oneb[n % OHR][:, :, :],
                       selT[:, 2, bass.ds(i * (2 * TC) + n * OH, OH)].unsqueeze(2).to_broadcast([P, OH, NK]),
                       ALU.mult).then_inc(sem("one_hot_gated"), 1)
            phase_end(pool, 3 + 5 * l)

        peer(0)
        phase_end(pool, 4)
        phase_end(pool, 5)
        for q in range(24):
            weights_lo(pool, tt, "hin", hwhi, hwlo, q)
        phase_end(pool, 6)
        peer(1)

    @block.scalar
    def _(act):
        f = nc.scalar.activation

        def copy_out(key, out_, in_=None, func=ACT.Copy, **kw):
            b = wait_full(act, key)
            f(out_, ps[b][:, :] if in_ is None else in_(ps[b]), func, **kw).then_inc(read[b], 1)

        wait_read(act, "vecs")
        f(s_col[:, :, :], vec[:, V_C:V_C + 2 * KD].rearrange("p (j k) -> p k j", j=2), ACT.Silu).then_inc(sem("silu_c"), 1)

        def copy_modulation(l, u):
            part = u // 2
            if part in GATES:
                g = 0 if part == GATES[0] else 1 + l
                copy_out(("ada", l, u), gate[g][:, (u % 2) * 512:(u % 2 + 1) * 512])
            else:
                copy_out(("ada", l, u), mrow[u % 2][:, :], lambda b: b[0:2, :], bias=1.0 if part in (1, 4) else 0.0)

        def copy_modulation_columns(l, u):
            part, k = u // 2, 4 * (u % 2)
            if part not in GATES:
                copy_out(("adaT", l, u), ada[l][:, (0, 1, None, 2, 3)[part], k:k + 4, :], lambda b: b[:, 0:8].rearrange("p (k j) -> p k j", j=2))

        def modulation(l, units, before=lambda n: None):
            for n, u in enumerate(units):
                before(n)
                copy_modulation(l, u)
                if n:
                    copy_modulation_columns(l, units[n - 1])
            copy_modulation_columns(l, units[-1])

        def sine(j):
            if j < 3:
                act.wait_ge(sem("sine_argument"), j + 1)
                f(hid[:, 0, :], hid[:, 3, :], ACT.Sin).then_inc(sem("sine"), 1)

        modulation(0, UNITS0[0], sine)
        for k in range(KD):
            wait_read(act, ("hT", k))
            f(hThi[:, k, :], hT[:, k, :], ACT.Copy).then_inc(sem("mixer_input_hi"), 1)

        def weights_hi(name, hi, q, used):
            n = first[name] + q // 2
            act.wait_ge(w_loaded[n % RING], 16 * (n // RING + 1))
            if q >= 2:
                used(q - 2)
            f(hi[q % 2][:, :, :], half_block(name, q), ACT.Copy).then_inc(sem("weights_hi"), 1)

        def xbc_used(q):
            wait_full(act, ("xbc", q))

        for q in range(2):
            weights_hi("xbc", whi, q, xbc_used)
        act.wait_ge(sem("dt_in"), 64)
        copy_out("dt_rows", dtrow, lambda b: b[0:2 * HEADS, :], ACT.Identity, bias=dtb[:, 0:1])
        f(aneg[:], aneg[:], ACT.Exp)
        wait_read(act, "dt")
        f(dtw[:, 1, :], dtw[:, 0, :], ACT.Abs).then_inc(sem("dt_abs"), 1)
        act.wait_ge(sem("dt_abs"), 1)
        f(dtw[:, 1, :], dtw[:, 1, :], ACT.Exp, scale=-1.0).then_inc(sem("dt_exp"), 1)
        act.wait_ge(sem("dt_plus_one"), 1)
        f(dtw[:, 3, :], dtw[:, 2, :], ACT.Ln).then_inc(sem("dt_log"), 1)
        for q in range(XBC_CT + 2):
            if q < XBC_CT:
                if q >= 2:
                    act.wait_ge(sem("conv_done"), q - 1)
                copy_out(("xbc", q), ubuf[q % 2])
                if q + 2 < XBC_CT:
                    weights_hi("xbc", whi, q + 2, xbc_used)
            r = q - 1
            if 0 <= r < XBC_CT:
                act.wait_ge(sem("conv_done"), r + 1)
                if r >= 2 and (r - 2 < 4 or r - 2 >= 8):
                    wait_full(act, ("xT", r - 2))
                if r < 4:
                    f(bcT[:, r, :], cacc[r % 2][:, T:2 * T], ACT.Silu)
                if r < 4 or r >= 8:
                    f(xc[r % 2], cacc[r % 2], ACT.Silu).then_inc(sem("conv_silu"), 1)
                else:
                    f(bcT[:, r, :], cacc[r % 2][:, T:2 * T], ACT.Silu).then_inc(sem("conv_silu"), 1)
            r = q - 2
            if r == 8:
                act.wait_ge(sem("hidden_stored"), 16)
            if 0 <= r < 4:
                copy_out(("xT", r), btok[:, :, r * P:(r + 1) * P], lambda b: b[:, :].rearrange("p (t c) -> p t c", t=4))
            elif r >= 8:
                copy_out(("xT", r), xtok[:, :, (r - 8) * P:(r - 7) * P], lambda b: b[:, :].rearrange("p (t c) -> p t c", t=4))
        copy_out("decay", dec[:, :, :].rearrange("p a b -> p (a b)"), lambda b: b[:, 0:12 * HEADS], ACT.Exp)
        for d in range(2):
            for g in range(GROUPS):
                copy_out(("S1", d, g), S1[:, d, g * GW:(g + 1) * GW])
        for c in range(2):
            for g in range(GROUPS):
                for d in range(2):
                    if c + g:
                        wait_full(act, ("ydiag", c - (g == 0), (g - 1) % GROUPS))
                    for h in range(2):
                        copy_out(("seg", c, g, d, h), EM[d][:, 4 * h:4 * h + 4, :].rearrange("p a b -> p (a b)"), None, ACT.Exp)
                modulation(0, (UNITS0[1][4 * c + g],))
        for j in range(8):
            if j >= 2:
                act.wait_ge(sem("y_gated"), j - 1)
            copy_out(("z", j), zs[j % 2], None, ACT.Silu)
            if j % 2:
                act.wait_ge(sem("y_gated"), j + 1)
                for t in range(TT):
                    n = (j // 2) * TT + t
                    if n >= TT:
                        act.wait_ge(sem("squares_summed"), n - 1)
                    f(lnt[:, t, :], yv[:, t, (j // 2) * GW:(j // 2 + 1) * GW], ACT.Square,
                      accum_out=ss[:, n:n + 1]).then_inc(sem("squares_summed"), 1)
        for q in range(2):
            weights_hi("mout", whi, q, None)
        act.wait_ge(sem("rms_mean"), 1)
        f(ss[:, 16:24], ss[:, 8:16], ACT.Sqrt).then_inc(sem("rms_root"), 1)
        for j in range(8):
            b = wait_full(act, ("uT", j))
            for c in range(2):
                last = f(uThi[:, 2 * j + c, :], ps[b][:, c * T:(c + 1) * T], ACT.Identity, scale=vec[:, V_NW + 2 * j + c:V_NW + 2 * j + c + 1])
            last.then_inc(sem("output_input_hi"), 1)
        for q in range(2, INNER // P):
            weights_hi("mout", whi, q, lambda k: act.wait_ge(sem("out_weights_used"), k + 1))

        def layer_norm(l, j):
            act.wait_ge(sem("ln_variance"), 2 * l + j + 1)
            f(small[:, :, 15], small[:, :, 14], ACT.Sqrt).then_inc(sem("ln_root"), 1)

        modulation(1, UNITS1[0], lambda n: layer_norm(0, 0) if n == 1 else None)
        phase_end(act, 1)

        def peer(l):
            for j in range(4):
                wait_read(act, ("tT", l, j))
                f(tThi[:, 2 * j:2 * j + 2, :], tT[:, 2 * j:2 * j + 2, :], ACT.Copy).then_inc(sem("t_hi"), 1)
            for j in range(4):
                copy_out(("kT", l, j), kT[:, 4 * j:4 * j + 4, :].rearrange("p a b -> p (a b)"))

            def copy_queries(r):
                if r >= 2:
                    wait_full(act, ("sc", l, r - 2))
                copy_out(("q", l, r), qT[r % 2][:, :, :].rearrange("p a t -> p (a t)"))

            def copy_scores(r):
                if r >= 2:
                    act.wait_ge(sem("keys_selected"), PH * l + r - 1)
                copy_out(("sc", l, r), sc[r % 2][:, :, :].rearrange("p a b -> p (a b)"))

            for do, r in HEAD_STEPS:
                (copy_queries if do == "queries" else copy_scores)(r)
            if l == 0:
                modulation(1, UNITS1[1])
            act.wait_ge(sem("gate_shifted"), l + 1)
            f(selv[:], selv[:], ACT.Exp).then_inc(sem("gate_exp"), 1)
            if l == 0:
                for c in range(2):
                    act.drain().then_inc(g_stored[c], 16)
            phase_end(act, 2 + 5 * l)
            with act.Fori(0, NTC // 2) as i:
                for c in range(2):
                    act.wait_ge(g_stored[c], i * 16 + (16 + 16 * l * (NTC // 2)))
                    for n in range(TC // 4):
                        key = ("g", l, c * (TC // 4) + n)
                        b, u = plan(key, i)
                        act.wait_ge(full[b], u + 1)
                        f(gch[:, c, :, 4 * n:4 * n + 4].rearrange("p i t -> p t i"), ps[b][:, :].rearrange("p (t i) -> p t i", t=4),
                          ACT.Copy).then_inc(read[b], 1)
                    for n in range(TC // 4):
                        wait_read(act, ("g", l, c * (TC // 4) + n), i)
                    act.dma_start(gdram[:, bass.ds(i * 2 + c, 1), :].rearrange("p o c -> p (o c)"),
                                  gch[:, c, :, :].rearrange("p i t -> p (i t)")).then_inc(g_stored[c], 16)
            act.wait_ge(g_stored[0], 16 + 16 * (l + 1) * (NTC // 2))
            phase_end(act, 3 + 5 * l)
            base = stream_base[l]

            def split_u(m, off, h, i=None):
                j = off % 2
                act.wait_ge(full[4 + h], m + (base[4 + h] + 1))
                if off >= 2 and h == 0:
                    act.wait_ge(full[6 + j], half(off, i) + base[6 + j])
                f(UThi[j][:, 4 * h:4 * h + 4, :].rearrange("p a b -> p (a b)"), ps[4 + h][:, :], ACT.Copy).then_inc(sem("u_hi"), 1)

            def half(off, i):
                return off // 2 if i is None else i * (ROUND // 2) + off // 2

            def tile_step(m, off, i=None):
                j = off % 2
                slot = off % UV
                last_tile = off == NK - 1
                if not last_tile:
                    split_u(m + 1, off + 1, 0, i)
                act.wait_ge(uv_loaded[slot], (m - slot) * 8 + 32 * (l * (NK // UV) + 1))
                if off >= 2:
                    act.wait_ge(sem("combined"), m + (l * (NK - 1) - 1))
                f(Vhi[j][:], uvring[slot][:, 1, :], ACT.Copy).then_inc(sem("v_hi"), 1)
                if not last_tile:
                    split_u(m + 1, off + 1, 1, i)
                act.wait_ge(full[6 + j], half(off, i) + (base[6 + j] + 1))
                if off >= 2:
                    act.wait_ge(sem("gated"), m + (l * NK - 1))
                f(gel[j][:], ps[6 + j][:, 0:T], ACT.Gelu).then_inc(read[6 + j], 1)

            for h in range(2):
                split_u(0, 0, h)
            tiles(act, tile_step)

        peer(0)
        phase_end(act, 4)
        act.wait_ge(sem("hyena_in"), 80)
        for t in range(TT):
            f(dcy[:, t, :], delta[:], ACT.Exp, scale=tcol[:, t:t + 1]).then_inc(sem("lag_decay"), 1)
        modulation(1, UNITS1[2])
        act.wait_ge(sem("filter_sides"), 2 * TT * ORDER)
        n = 0
        for o in range(ORDER):
            for h in range(2):
                m = 2 * o + h
                if m >= 2:
                    wait_full(act, ("hnorm", m - 2))
                for side in range(2):
                    for t in range(TT):
                        last = f(sqr[m % 2][:, 2 * side + t, :], sd[:, side, t, o, h * 512:(h + 1) * 512], ACT.Square)
                last.then_inc(sem("filter_squares"), 1)
                for tile in range(5):
                    copy_out(("hspec", n), Hs[:, o, tile, h * 512:(h + 1) * 512])
                    n += 1
                if m == 1:
                    layer_norm(0, 1)
        for m in range(2 * ORDER):
            wait_read(act, ("hnorm", m))
            f(rsn[:, m, :], rsn[:, m, :], ACT.Sqrt).then_inc(sem("norm_root"), 1)
        phase_end(act, 5)
        def hin_used(q):
            if q % 2:
                wait_full(act, ("hu", q // 2))
            else:
                act.wait_ge(sem("hyena_weights_used"), q // 2 + 1)

        for q in range(2):
            weights_hi("hin", hwhi, q, hin_used)
        for j in range(4):
            wait_read(act, ("hhT", j))
            f(hhThi[:, 2 * j:2 * j + 2, :], hhT[:, 2 * j:2 * j + 2, :], ACT.Copy).then_inc(sem("hyena_input_hi"), 1)
        for n in range(12):
            if n < 11:
                for c in range(2):
                    weights_hi("hin", hwhi, 2 * n + 2 + c, hin_used)
            if n >= 2:
                act.wait_ge(sem("hyena_conv"), n - 1)
            copy_out(("hu", n), hub[n % 2][:, :, :].rearrange("p a b -> p (a b)"))
        for o in range(ORDER):
            for j in range(4):
                copy_out(("vtok", o, j), vtok[:, :, j * 2 * P:(j + 1) * 2 * P], lambda b: b[:, :].rearrange("p (t c) -> p t c", t=TT))
        layer_norm(1, 0)
        phase_end(act, 6)
        peer(1)
        layer_norm(1, 1)

    @block.vector
    def _(dve):
        step = Chain(sem("vector_steps"))
        V = nc.vector
        tt, ts, stt = V.tensor_tensor, V.tensor_scalar, V.scalar_tensor_tensor

        def after(n):
            dve.wait_ge(step.sem, n)

        def bc(ap, n, width):
            return ap.unsqueeze(2).to_broadcast([P, n, width])

        dve.wait_ge(full[0], 1)
        V.tensor_copy(vec[:, 0:3 * P], ps[0][:, 0:3 * P]).then_inc(read[0], 1)
        dve.wait_ge(sem("silu_c"), 1)
        V.tensor_copy(s_rep[:, :, :], s_col[:, :, 0:1].to_broadcast([P, KD, P])).then_inc(sem("silu_c_rows"), 1)

        def modulate(key, dsts, l, pair):
            for u in range(4):
                wait_read(dve, ("adaT", l, 6 * pair + u))
            for j in range(4):
                b = wait_full(dve, key + (j,))
                for c in range(2):
                    k = 2 * j + c
                    last = ts(dsts[:, k, :], ps[b][:, c * T:(c + 1) * T], ada[l][:, 2 * pair + 1, k, 0:1], ada[l][:, 2 * pair, k, 0:1], ALU.mult, ALU.add)
                last.then_inc(read[b], 1)

        two_pi = 2 * math.pi
        c1 = 6.28125
        c2 = two_pi - c1
        magic = 1.5 * 2.0 ** 23
        for j in range(3):
            b = wait_full(dve, ("hid", j))
            ts(hid[:, 1, :], ps[b][0:HY_FF, 0:T], fv[:, j:j + 1], fv[:, 3:4], ALU.add, ALU.mult).then_inc(read[b], 1)
            wait_read(dve, ("hid", j))
            n = step(ts(hid[:, 2, :], hid[:, 1, :], 1.0 / two_pi, magic, ALU.mult, ALU.add))
            after(n)
            n = step(ts(hid[:, 2, :], hid[:, 2, :], -magic, None, ALU.add))
            after(n)
            n = step(stt(hid[:, 1, :], hid[:, 2, :], -c1, hid[:, 1, :], ALU.mult, ALU.add))
            after(n)
            n = step(stt(hid[:, 1, :], hid[:, 2, :], -c2, hid[:, 1, :], ALU.mult, ALU.add))
            after(n)
            ts(hid[:, 3, :], hid[:, 1, :], 3.1415925, -3.1415925, ALU.min, ALU.max).then_inc(sem("sine_argument"), 1)
        for u in range(4):
            wait_read(dve, ("adaT", 0, u))
        for k in range(KD):
            b = wait_full(dve, ("hT", k))
            for half_, j in ((0, 1), (1, 0)):
                last = ts(hT[:, k, half_ * T:(half_ + 1) * T], ps[b][:, half_ * T:(half_ + 1) * T],
                          ada[0][:, 1, k, j:j + 1], ada[0][:, 0, k, j:j + 1], ALU.mult, ALU.add)
            last.then_inc(read[b], 1)
        for k in range(KD):
            dve.wait_ge(sem("mixer_input_hi"), k + 1)
            last = tt(hTlo[:, k, :], hT[:, k, :], hThi[:, k, :].bitcast(F32), ALU.subtract)
        last.then_inc(sem("mixer_input_split"), 1)
        b = wait_full(dve, "dt")
        V.tensor_copy(dtw[:, 0, :], ps[b][:, 0:256]).then_inc(read[b], 1)
        dve.wait_ge(sem("dt_exp"), 1)
        ts(dtw[:, 2, :], dtw[:, 1, :], 1.0, None, ALU.add).then_inc(sem("dt_plus_one"), 1)
        dve.wait_ge(sem("dt_plus_one"), 1)
        n = step(ts(dtw[:, 4, :], dtw[:, 2, :], -1.0, None, ALU.add))
        after(n)
        n = step(ts(dtw[:, 5, :], dtw[:, 4, :], 0.0, None, ALU.is_equal))
        after(n)
        n = step(tt(dtw[:, 4, :], dtw[:, 4, :], dtw[:, 5, :], ALU.add))
        dve.wait_ge(sem("dt_log"), 1)
        n = step(tt(dtw[:, 3, :], dtw[:, 3, :], dtw[:, 5, :], ALU.add))
        after(n)
        n = step(tt(dtw[:, 3, :], dtw[:, 3, :], dtw[:, 1, :], ALU.mult))
        n = step(V.reciprocal(dtw[:, 4, :], dtw[:, 4, :]))
        after(n)
        n = step(tt(dtw[:, 3, :], dtw[:, 3, :], dtw[:, 4, :], ALU.mult))
        after(n)
        dtf = dt_t[:, :, :].rearrange("p a b -> p (a b)")
        n = step(stt(dtf, dtw[:, 0, :], 0.0, dtw[:, 3, :], ALU.max, ALU.add))
        after(n)
        stt(a_t[:, :, :], dt_t[:, :, :], -1.0, aneg[:].unsqueeze(1).to_broadcast([P, 4, 2 * HEADS]), ALU.mult, ALU.mult).then_inc(sem("a_ready"), 1)
        for q in range(XBC_CT):
            ct = 16 + q if q < 8 else q - 8
            u, acc = ubuf[q % 2], cacc[q % 2]
            wait_read(dve, ("xbc", q))
            if q >= 2:
                dve.wait_ge(sem("conv_silu"), q - 1)

            def tap(i, j):
                return vec[:, V_CW + (3 * i + j) * 24 + ct:V_CW + (3 * i + j) * 24 + ct + 1]

            bias = vec[:, V_CB + ct:V_CB + ct + 1]
            ug = u[:, T:2 * T].rearrange("p (r c) -> p r c", r=ROWS)
            ag = acc[:, T:2 * T].rearrange("p (r c) -> p r c", r=ROWS)
            nl = nx = step(ts(acc, u, tap(1, 1), bias, ALU.mult, ALU.add))
            ctx_taps = [(1, 0), (1, 2)] if q < 4 or q >= 8 else []
            for i, j in [(1, 0), (1, 2), (0, 1), (2, 1), (0, 0), (0, 2), (2, 0), (2, 2)]:
                if ctx_taps:
                    _, jj = ctx_taps.pop(0)
                    o, s_ = (acc[:, 1:T], u[:, 0:T - 1]) if jj == 0 else (acc[:, 0:T - 1], u[:, 1:T])
                    after(nx)
                    nx = step(stt(o, s_, tap(1, jj), o, ALU.mult, ALU.add))
                di, dj = i - 1, j - 1
                r0, r1, c0, c1 = max(0, -di), ROWS - max(0, di), max(0, -dj), GRID_W - max(0, dj)
                o, s_ = ag[:, r0:r1, c0:c1], ug[:, r0 + di:r1 + di, c0 + dj:c1 + dj]
                after(nl)
                last = stt(o, s_, tap(i, j), o, ALU.mult, ALU.add)
                if (i, j) == (2, 2):
                    last.then_inc(sem("conv_done"), 1)
                else:
                    nl = step(last)
        wait_read(dve, "decay")
        cols = ((DC_F0, 0, 0), (DC_F1, 1, 0), (DC_F2, 2, 0), (DC_B1, 1, 1), (DC_B0, 0, 1), (DC_B3, 3, 1))
        for j, (dc, c, d) in enumerate(cols):
            n = step(tt(wst[:, j, :], dec[:, dc, :], dt_t[:, c, d * HEADS:(d + 1) * HEADS], ALU.mult))
        after(n)
        for r in range(8, XBC_CT):
            if r >= XBC_CT - 2:
                wait_read(dve, ("xT", r))

        def weigh(dst, c, w):
            return tt(dst.rearrange("p (h d) -> p h d", h=HEADS), xtok[:, c, :].rearrange("p (h d) -> p h d", h=HEADS),
                      bc(w, HEADS, HD), ALU.mult)

        def later_state(d):
            for g in range(GROUPS):
                wait_read(dve, ("S1", d, g))
                s2 = S2[:, d, g * GW:(g + 1) * GW]
                t_ = dec[:, (DC_TF2, DC_TB3)[d], g * HPG:(g + 1) * HPG]
                n = step(tt(s2.rearrange("p (h d) -> p h d", h=HPG), S1[:, d, g * GW:(g + 1) * GW].rearrange("p (h d) -> p h d", h=HPG),
                            bc(t_, HPG, HD), ALU.mult))
                b = wait_full(dve, ("S2", d, g))
                after(n)
                tt(s2, s2, ps[b][:, :], ALU.add).then_inc(read[b], 1)

        for j, (dc, c, d) in enumerate(cols):
            if j in (2, 5):
                dve.wait_ge(sem("x_weighted_first_used"), d + 1)
            elif j == 3:
                wait_full(dve, ("S1", 0, GROUPS - 1))
            elif j == 4:
                wait_full(dve, ("S2", 0, GROUPS - 1))
            weigh(xw[j % 2][:, :], c, wst[:, j, :]).then_inc(sem("x_weighted"), 1)
            if j == 2:
                later_state(0)
        later_state(1)
        for c in range(2):
            if c == 0:
                wait_full(dve, ("S1", 1, GROUPS - 1))
                wait_full(dve, ("S2", 1, GROUPS - 1))
            else:
                wait_full(dve, ("ydiag", 0, GROUPS - 1))
            for d in range(2):
                weigh(xw[d][:, :], 2 + c, dt_t[:, 2 + c, d * HEADS:(d + 1) * HEADS]).then_inc(sem("x_dt"), 1)
            for g in range(GROUPS):
                y = yv[:, c, g * GW:(g + 1) * GW]
                b = wait_full(dve, ("cb", c, g))
                n = step(tt(cbm[:, 0, :], ps[b][:, 0:P], cst[:, C_LE, :], ALU.mult))
                tt(cbm[:, 1, :], ps[b][:, 0:P], cst[:, C_GE, :], ALU.mult).then_inc(read[b], 1)
                after(n)
                wait_read(dve, ("cb", c, g))
                for d in range(2):
                    for h in range(2):
                        wait_read(dve, ("seg", c, g, d, h))
                    tt(EM[d][:, :, :], EM[d][:, :, :], cbm[:, d, :].unsqueeze(1).to_broadcast([P, HPG, P]), ALU.mult).then_inc(sem("mixing_ready"), 1)
                for d in range(2):
                    b = wait_full(dve, ("yoff", c, g, d))
                    e = dec[:, (DC_IF2, DC_IB2)[d] + c, g * HPG:(g + 1) * HPG]
                    o = y if d == 0 else lnt[:, 0, :]
                    tt(o.rearrange("p (h d) -> p h d", h=HPG), ps[b][:, :].rearrange("p (h d) -> p h d", h=HPG), bc(e, HPG, HD), ALU.mult).then_inc(read[b], 1)
                for d in range(2):
                    wait_read(dve, ("yoff", c, g, d))
                n = step(tt(y, y, lnt[:, 0, :], ALU.add))
                after(n)
                b = wait_full(dve, ("ydiag", c, g))
                tt(y, y, ps[b][:, :], ALU.add).then_inc(read[b], 1)
            dve.wait_ge(sem("x_skip"), c + 1)
            wait_read(dve, ("ydiag", c, GROUPS - 1))
            n = step(tt(yv[:, c, :], yv[:, c, :], xtok[:, 2 + c, :], ALU.add))
            after(n)
        for j in range(8):
            wait_read(dve, ("z", j))
            y = yv[:, :, j * BLK:(j + 1) * BLK]
            tt(y, y, zs[j % 2].rearrange("p (t c) -> p t c", t=TT), ALU.mult).then_inc(sem("y_gated"), 1)
        dve.wait_ge(sem("squares_summed"), GROUPS * TT)
        ts(ss[:, 8:16], ss[:, 0:8], 1.0 / GW, EPS, ALU.mult, ALU.add).then_inc(sem("rms_mean"), 1)
        for k in range(2):
            weights_lo(dve, tt, "mout", whi, wlo, k)
        dve.wait_ge(sem("rms_root"), 1)
        n = step(V.reciprocal(ss[:, 0:8], ss[:, 16:24]))
        after(n)
        for g in range(GROUPS):
            for t in range(TT):
                y = yv[:, t, g * GW:(g + 1) * GW]
                last = ts(y, y, ss[:, 2 * g + t:2 * g + t + 1], None, ALU.mult)
            last.then_inc(sem("y_normed"), 1)

        def layer_norm(l, j, keys):
            dve.wait_ge(sem("ln_rows_in"), 32 * (2 * l + j + 1))
            for u in range(2):
                wait_read(dve, ("ada", l, 2 * GATES[j] + u))
            gates = gate[j + l * j]
            for t in range(TT):
                for h in range(2):
                    b = wait_full(dve, keys[2 * t + h])
                    tt(lnt[:, h, :], ps[b][:, :], gates[:, h * 512:(h + 1) * 512], ALU.mult).then_inc(read[b], 1)
                for h in range(2):
                    wait_read(dve, keys[2 * t + h])
                    x = xres[:, t, h * 512:(h + 1) * 512]
                    n = step(stt(x, x, ALPHA, lnt[:, h, :], ALU.mult, ALU.add))
                    after(n)
                    n = step(V.bn_stats(small[:, t, 6 * h:6 * h + 6], x))
                after(n)
                n = step(V.bn_aggr(small[:, t, 12:14], small[:, t, 0:12]))
            after(n)
            ts(small[:, :, 14], small[:, :, 13], EPS, None, ALU.add).then_inc(sem("ln_variance"), 1)
            dve.wait_ge(sem("ln_root"), 2 * l + j + 1)
            n = step(V.reciprocal(small[:, :, 16], small[:, :, 15]))
            after(n)
            for t in range(TT):
                n = step(ts(xres[:, t, :], xres[:, t, :], small[:, t, 12:13], small[:, t, 16:17], ALU.subtract, ALU.mult))
            for t in range(TT):
                after(n - 1 + t)
                m = step(tt(xres[:, t, :], xres[:, t, :], lnb[:, 0, :], ALU.mult))
            for t in range(TT):
                after(m - 1 + t)
                last = tt(xres[:, t, :], xres[:, t, :], lnb[:, 1, :], ALU.add)
            last.then_inc(sem("layer_norms_done"), 1)

        for j in range(8):
            dve.wait_ge(sem("output_input_hi"), j + 1)
            b = plan(("uT", j))[0]
            for c in range(2):
                ct = 2 * j + c
                last = stt(uTlo[:, ct, :], ps[b][:, c * T:(c + 1) * T], vec[:, V_NW + ct:V_NW + ct + 1], uThi[:, ct, :].bitcast(F32), ALU.mult, ALU.subtract)
            last.then_inc(read[b], 1)
        for k in range(2, INNER // P):
            weights_lo(dve, tt, "mout", whi, wlo, k)
        layer_norm(0, 0, [("mout", j) for j in range(4)])
        phase_end(dve, 1)

        def best(count, src, rest, val, idx):
            for r in range(count):
                n = step(V.max(val(r)[:, 0:8], src(r)))
            after(n)
            for r in range(count):
                step(V.max_index(idx(r)[:, 0:8], val(r)[:, 0:8], src(r)))
                n = step(V.match_replace(rest(r), val(r)[:, 0:8], src(r), LOWEST))
            after(n)
            for r in range(count):
                n = step(V.max(val(r)[:, 8:16], rest(r)))
            after(n)
            for r in range(count):
                n = step(V.max_index(idx(r)[:, 8:16], val(r)[:, 8:16], rest(r)))
            after(n)

        def select_keys(l, r):
            wait_read(dve, ("sc", l, r))
            if r >= 2:
                dve.wait_ge(sem("pair_sums"), PH * l + r - 1)
            if r >= 3:
                dve.wait_ge(sem("positions_weighed"), PH * l + r - 2)
            j = r % 2
            best(4, lambda n: sc[j][:, n, :], lambda n: left[:, n, :], lambda n: topv[j][:, n, :], lambda n: topi[j][:, n, :])
            V.tensor_copy(topf[r % 3][:, :, :], topi[j][:, :, :]).then_inc(sem("keys_selected"), 1)

        def select_pairs(l, r):
            dve.wait_ge(sem("pair_sums"), PH * l + r + 1)
            j = r % 2
            best(TT, lambda t: cand[j][:, t, :], lambda t: cand_left[:, t, :], lambda t: selv[:, t, r, :], lambda t: seli[:, t, :])
            step(ts(posr[:, :, 0, :], seli[:, :, :], 4, None, ALU.logical_shift_right))
            n = step(ts(posr[:, :, 1, :], seli[:, :, :], 15, None, ALU.bitwise_and))
            after(n)
            n = step(V.tensor_copy(posf[:, :, :, :], posr[:, :, :, :]))
            after(n)
            tt(pick[j][:, :, :, :].rearrange("p n k a -> p (n k) a"), cst[:, C_IOTA, 0:TOPK].unsqueeze(1).to_broadcast([P, 4 * TOPK, TOPK]),
               bc(posf[:, :, :, :].rearrange("p t a k -> p (t a k)"), 4 * TOPK, TOPK), ALU.is_equal).then_inc(sem("pairs_selected"), 1)

        def selected_keys(l, r):
            dve.wait_ge(sem("positions_weighed"), PH * l + r + 1)
            for t in range(TT):
                n = step(V.tensor_reduce(seltok[:, t, 0:2, r * TOPK:(r + 1) * TOPK], pick[r % 2][:, 2 * t:2 * t + 2, :, :], AX.X, ALU.add))
            after(n)

        def peer(l):
            modulate(("tT", l), tT, l, 1)
            for j in range(4):
                dve.wait_ge(sem("t_hi"), 4 * l + j + 1)
                s_ = slice(2 * j, 2 * j + 2)
                last = tt(tTlo[:, s_, :], tT[:, s_, :], tThi[:, s_, :].bitcast(F32), ALU.subtract)
            last.then_inc(sem("t_split"), 1)
            for r in range(PH + 2):
                if r < PH:
                    select_keys(l, r)
                if r >= 2:
                    selected_keys(l, r - 2)
                if 1 <= r <= PH:
                    select_pairs(l, r - 1)
            n = step(V.tensor_copy(ksum[:, 0, :, :], selv[:, :, :, 0]))
            after(n)
            flat = selv[:, :, :, :].rearrange("p t h k -> p (t h) k")
            sums = ksum[:, :, :, :].rearrange("p j t h -> p j (t h)")
            tt(flat, flat, bc(sums[:, 0, :], TT * PH, TOPK), ALU.subtract).then_inc(sem("gate_shifted"), 1)
            dve.wait_ge(sem("gate_exp"), l + 1)
            n = step(V.tensor_reduce(sums[:, 0, :], flat, AX.X, ALU.add))
            after(n)
            n = step(V.reciprocal(sums[:, 1, :], sums[:, 0, :]))
            after(n)
            for t in range(TT):
                last = tt(seltok[:, t, 2, :].rearrange("p (h k) -> p h k", h=PH), selv[:, t, :, :], bc(ksum[:, 1, t, :], PH, TOPK), ALU.mult)
            last.then_inc(sem("selected"), 1)
            for u in range(TT):
                b = wait_full(dve, ("selT", l, u))
                V.tensor_copy(selT[:, :, u * P:(u + 1) * P], ps[b][:, 0:3 * P].rearrange("p (j c) -> p j c", j=3)).then_inc(read[b], 1)
            for u in range(TT):
                wait_read(dve, ("selT", l, u))
            phase_end(dve, 2 + 5 * l)
            groups = 2 * TC // OH
            with dve.Fori(0, NTC // 2) as i:
                for n in range(groups):
                    place_free(dve, l, n, i)
                    for half, one in ((1, oneb), (0, onea)):
                        tt(one[n % OHR][:, :, :], cst[:, C_IOTA, :].unsqueeze(1).to_broadcast([P, OH, NK]),
                           bc(selT[:, half, bass.ds(i * (2 * TC) + n * OH, OH)], OH, NK),
                           ALU.is_equal).then_inc(sem(("one_hot_first", "one_hot_second")[half]), 1)
            phase_end(dve, 3 + 5 * l)
            base = stream_base[l]

            def split_u(m, off, h):
                j = off % 2
                dve.wait_ge(sem("u_hi"), m * 2 + (2 * l * NK + h + 1))
                c = slice(4 * h, 4 * h + 4)
                tt(UTlo[j][:, c, :].rearrange("p a b -> p (a b)"), ps[4 + h][:, :], UThi[j][:, c, :].rearrange("p a b -> p (a b)").bitcast(F32),
                   ALU.subtract).then_inc(read[4 + h], 1)

            def tile_step(m, off, i=None):
                j = off % 2
                slot = off % UV
                half = off // 2 if i is None else i * (ROUND // 2) + off // 2
                if off != NK - 1:
                    split_u(m + 1, off + 1, 0)
                dve.wait_ge(sem("v_hi"), m + (l * NK + 1))
                tt(Vlo[j][:], uvring[slot][:, 1, :], Vhi[j][:].bitcast(F32), ALU.subtract).then_inc(sem("v_split"), 1)
                if off != NK - 1:
                    split_u(m + 1, off + 1, 1)
                dve.wait_ge(read[6 + j], half + (base[6 + j] + 1))
                gj = (off // GI) % 2
                rounds_ = off // (2 * GI) if i is None else i + off // (2 * GI)
                dve.wait_ge(g_loaded[gj], rounds_ * 16 + 16 * (l * (NK // GI // 2) + 1))
                tt(gw[j][:].rearrange("p (c t) -> p c t", c=NTC), gel[j][:].rearrange("p (c t) -> p c t", c=NTC),
                   gt[gj][:, :, (off % GI) * TC:(off % GI + 1) * TC], ALU.mult).then_inc(sem("gated"), 1)
                dve.wait_ge(sem("gated"), m + (l * NK + 1))
                V.tensor_copy(Whi[j][:], gw[j][:]).then_inc(sem("w_hi"), 1)
                dve.wait_ge(sem("w_hi"), m + (l * NK + 1))
                tt(Wlo[j][:], gw[j][:], Whi[j][:].bitcast(F32), ALU.subtract).then_inc(sem("w_split"), 1)

            for h in range(2):
                split_u(0, 0, h)
            tiles(dve, tile_step)

        peer(0)
        phase_end(dve, 4)
        n = 0
        for t in range(TT):
            dve.wait_ge(sem("lag_decay"), t + 1)
            for o in range(ORDER):
                for h in range(2):
                    if n:
                        dve.wait_ge(sem("filter_sides"), n)
                    for side in range(2):
                        b = wait_full(dve, ("hflt", n, side))
                        tt(lnt[:, side, :], ps[b][:, :], dcy[:, t, h * 512:(h + 1) * 512], ALU.mult).then_inc(read[b], 1)
                    for side in range(2):
                        wait_read(dve, ("hflt", n, side))
                    tt(sd[:, 0, t, o, h * 512:(h + 1) * 512], lnt[:, 0, :], lnt[:, 1, :], ALU.add)
                    tt(sd[:, 1, t, o, h * 512:(h + 1) * 512], lnt[:, 0, :], lnt[:, 1, :], ALU.subtract).then_inc(sem("filter_sides"), 1)
                    n += 1
        dve.wait_ge(sem("filter_sides"), n)
        layer_norm(0, 1, [("peer_out", 0, j) for j in range(4)])
        for m in range(2 * ORDER):
            b = wait_full(dve, ("hnorm", m))
            ts(rsn[:, m, :], ps[b][:, :], HY_EPS, None, ALU.add).then_inc(read[b], 1)
        phase_end(dve, 5)
        modulate(("hhT",), hhT, 1, 0)
        for j in range(4):
            dve.wait_ge(sem("hyena_input_hi"), j + 1)
            c = slice(2 * j, 2 * j + 2)
            last = tt(hhTlo[:, c, :], hhT[:, c, :], hhThi[:, c, :].bitcast(F32), ALU.subtract)
        last.then_inc(sem("hyena_input_split"), 1)
        for m in range(2 * ORDER):
            dve.wait_ge(sem("norm_root"), m + 1)
            V.reciprocal(rsn[:, m, :], rsn[:, m, :]).then_inc(sem("filter_norm"), 1)
        for m in range(12):
            wait_read(dve, ("hu", m))
            for c in range(2):
                ct = 2 * m + c
                u, o = hub[m % 2][:, c, :], huT[:, ct, :]

                def tap(j):
                    return vec[:, V_HCW + 24 * j + ct:V_HCW + 24 * j + ct + 1]

                n = step(ts(o, u, tap(1), vec[:, V_HCB + ct:V_HCB + ct + 1], ALU.mult, ALU.add))
                after(n)
                n = step(stt(o[:, 1:T], u[:, 0:T - 1], tap(0), o[:, 1:T], ALU.mult, ALU.add))
                after(n)
                last = stt(o[:, 0:T - 1], u[:, 1:T], tap(2), o[:, 0:T - 1], ALU.mult, ALU.add)
            last.then_inc(sem("hyena_conv"), 1)
            for n in range(2 * m, min(2 * m + 2, 5 * 2 * ORDER)):
                if n % 5 == 0:
                    dve.wait_ge(sem("filter_norm"), n // 5 + 1)
                wait_read(dve, ("hspec", n))
                s_ = Hs[:, n // 10, n % 5, (n // 5 % 2) * 512:(n // 5 % 2 + 1) * 512]
                tt(s_, s_, rsn[:, n // 5, :], ALU.mult).then_inc(sem("spectra_normed"), 1)
        for o in range(ORDER):
            for n in range(4):
                h, fr = n // 2, n % 2
                c = slice(h * 512, (h + 1) * 512)
                if o + n:
                    dve.wait_ge(sem("spectrum_done"), 8 * o + 2 * n)
                dve.wait_ge(sem("spectra_normed"), 5 * (2 * o + h + 1))
                b0 = wait_full(dve, ("vs", o, n, 0))
                b1 = wait_full(dve, ("vs", o, n, 1))
                fa, fb, fc = Hs[:, o, fr, c], Hs[:, o, 2 + fr, c], Hs[:, o, 4 if fr == 0 else 1, c]
                step(tt(ytm[:, 0, :], ps[b0][:, :], fa, ALU.mult))
                tt(ytm[:, 2, :], ps[b0][:, :], fb, ALU.mult).then_inc(read[b0], 1)
                k = step(tt(ytm[:, 1, :], ps[b1][:, :], fb, ALU.mult))
                tt(ytm[:, 3, :], ps[b1][:, :], fc, ALU.mult).then_inc(read[b1], 1)
                after(k)
                tt(Yf[:, fr, c], ytm[:, 0, :], ytm[:, 1, :], ALU.subtract).then_inc(sem("spectrum_done"), 1)
                wait_read(dve, ("vs", o, n, 0))
                wait_read(dve, ("vs", o, n, 1))
                tt(Yf[:, 2 + fr, c], ytm[:, 2, :], ytm[:, 3, :], ALU.add).then_inc(sem("spectrum_done"), 1)
            for c2 in range(4):
                if o + c2:
                    dve.wait_ge(sem("order_done"), 8 * o + 2 * c2)
                b = wait_full(dve, ("inv", o, c2))
                for c in range(2):
                    ct = 2 * c2 + c
                    v = huT[:, 16 + ct, :]
                    last = stt(hyt[:, c, :], v, vec[:, V_HB + 8 * o + ct:V_HB + 8 * o + ct + 1], ps[b][:, c * T:(c + 1) * T], ALU.mult, ALU.add)
                    if c == 0:
                        k = step(last)
                last.then_inc(read[b], 1)
                after(k)
                wait_read(dve, ("inv", o, c2))
                for c in range(2):
                    ct = 2 * c2 + c
                    tt(huT[:, 16 + ct, :], hyt[:, c, :], huT[:, 8 * o + ct, :], ALU.mult).then_inc(sem("order_done"), 1)
        dve.wait_ge(sem("order_done"), 8 * ORDER)
        layer_norm(1, 0, [("hout", j) for j in range(4)])
        phase_end(dve, 6)
        peer(1)
        layer_norm(1, 1, [("peer_out", 1, j) for j in range(4)])


def dft_tables(np):
    n = 2 * T
    tok = np.arange(T)
    frq = np.arange(T)
    ang = 2 * np.pi * np.outer(tok, frq) / n
    alt = (-1.0) ** tok
    re, im = np.cos(ang), -np.sin(ang)
    fi = im.copy()
    fi[:, 0] = alt
    c0 = re[:, :P].copy()
    c0[:, 0] = alt
    inv_r = 2 * re.T / n
    inv_r[0] = 1.0 / n
    inv_i = 2 * im.T / n
    inv_i[0] = alt / n

    def parts(m):
        return m.reshape(-1, P, m.shape[1]).transpose(1, 0, 2).reshape(P, -1)

    ws = np.full((P, P), 0.5)
    ws[0] = 1.0
    wd = np.full((P, P), 0.5)
    wd[0] = 0.0
    half = np.full((P, P), 0.5)
    return np.ascontiguousarray(np.concatenate(
        [parts(re), parts(fi), parts(im[:, :P]), parts(c0), parts(np.concatenate([inv_r, inv_i])), ws, wd, half], axis=1).astype(np.float32))


def shape_constants(np):
    f32 = np.float32
    i = np.arange(P)
    u, t = i[:, None], i[None, :]
    mats = [u == t, u <= t, u >= t, u < t, u > t, np.ones((P, P)), np.broadcast_to(t, (P, P))]
    tl = np.linspace(0.0, 1.0, T, dtype=f32)
    bands = (HY_EMB - 1) // 2
    ang = (f32(2.0 * math.pi) * np.arange(T, dtype=f32) / f32(T)).astype(f32)
    fb = np.linspace(1e-4, bands - 1, bands, dtype=f32)
    arg = (fb[:, None] * ang[None, :]).astype(f32).astype(np.float64)
    feats = np.concatenate([tl[None, :], np.cos(arg), -np.sin(arg)], axis=0).astype(f32)
    rates = np.abs(np.linspace(math.log(1e-2) / 1.5, math.log(1e-2) / 0.3, D, dtype=f32))
    return {
        "constants": np.ascontiguousarray(np.concatenate([np.asarray(m, f32) for m in mats], axis=1)),
        "hyena_constants": dft_tables(np),
        "filter_features": np.ascontiguousarray(feats),
        "lag_times": np.ascontiguousarray(-tl.reshape(TT, P).T),
        "decay_rates": rates.astype(f32),
    }


INPUTS = ["x", "c", "ctx", "c_ctx", "ada_w", "ada_b", "ln_g", "ln_b", "m_w_in", "m_conv_w", "m_conv_b", "m_a_log",
          "m_dt_bias", "m_d", "m_norm_w", "m_w_out", "h_w_in", "h_conv_w", "h_conv_b", "h_f_w1", "h_f_b1", "h_f_w2",
          "h_f_b2", "h_f_w3", "h_freq", "h_bias", "h_w_out", "p_wq", "p_k1", "p_k2", "p_u", "p_v"]


def kernel(**inputs):
    import numpy as np
    import concourse.bacc as bacc
    from concourse.bass_utils import run_bass_kernel_spmd as run

    nc = bacc.Bacc("TRN2", target_bir_lowering=False, num_devices=1)
    arrays, aps = {}, {}
    given = {n: np.ascontiguousarray(inputs[n]) for n in INPUTS} | shape_constants(np)
    for name, a in given.items():
        arrays[f"in_{name}"] = a
        aps[name] = nc.dram_tensor(f"in_{name}", a.shape, mybir.dt.from_np(a.dtype), kind="ExternalInput").ap()
    out = nc.dram_tensor("out_x", (1, T, D), F32, kind="ExternalOutput").ap()
    build_program(nc, aps, out)
    r = run(nc, [arrays], core_ids=[0])
    return r.results[0]["out_x"]
```
